# Optimizing a Trainium2 kernel written in Bass

```python
import jax, jax.numpy as jnp
from jax import lax
import numpy as np
import math

D_MODEL = 1024
BATCH = 1
SEQ = 256
DEPTH = 2

HEAD_DIM = 64
DIL_PATTERNS = ((128, 1), (512, 4), (2048, 16))
DIL_HEADS = 4
N_DIL_SUB = DIL_HEADS * len(DIL_PATTERNS)
DIL_QKV = N_DIL_SUB * HEAD_DIM
DIL_OUT = DIL_HEADS * HEAD_DIM
DIL_BLOCK = 64
WIN_HALF = 128
WIN_BLOCK = 128
WIN_Q = D_MODEL
WIN_Q_HEADS = WIN_Q // HEAD_DIM
WIN_KV_HEADS = 4
WIN_KV = WIN_KV_HEADS * HEAD_DIM
N_BRANCH = 2
SPLITS = (DIL_QKV, 2 * DIL_QKV, 3 * DIL_QKV,
          3 * DIL_QKV + WIN_Q, 3 * DIL_QKV + WIN_Q + WIN_KV, 3 * DIL_QKV + WIN_Q + 2 * WIN_KV)
IN_COLS = 3 * DIL_QKV + WIN_Q + 2 * WIN_KV + N_BRANCH * D_MODEL
N_EXPERTS = 16
CAPACITY_FACTOR = 2
D_EXPERT = 1024
RMS_EPS = 1e-6
NEG_INF = -1e30


def rmsnorm(x, g):
    xf = x.astype(jnp.float32)
    y = xf * lax.rsqrt(jnp.mean(xf * xf, axis=-1, keepdims=True) + RMS_EPS)
    return (y * g.astype(jnp.float32)).astype(x.dtype)

def alibi_slopes(n):
    return 2.0 ** (-8.0 * jnp.arange(1, n + 1, dtype=jnp.float32) / n)

def banded_attention(q, k, v, half, blk, slopes, pos_scale, sink=None):
    N, L, H, dh = q.shape
    Hk = k.shape[2]
    G = H // Hk
    nb = -(-L // blk)
    Lp = nb * blk
    pad = Lp - L
    qb = jnp.pad(q, ((0, 0), (0, pad), (0, 0), (0, 0))).reshape(N, nb, blk, Hk, G, dh)

    def key_blocks(t):
        tp = jnp.pad(t, ((0, 0), (blk, pad + blk), (0, 0), (0, 0)))
        return jnp.concatenate([
            tp[:, :Lp].reshape(N, nb, blk, Hk, dh),
            tp[:, blk:blk + Lp].reshape(N, nb, blk, Hk, dh),
            tp[:, 2 * blk:].reshape(N, nb, blk, Hk, dh)], axis=2)

    kb = key_blocks(k)
    vb = key_blocks(v)
    a = jnp.arange(blk)[:, None]
    b = jnp.arange(3 * blk)[None, :]
    rel = b - blk - a
    kpos = (jnp.arange(nb)[:, None, None] - 1) * blk + b[None]
    mask = (jnp.abs(rel) <= half)[None] & (kpos >= 0) & (kpos < L)
    bias = -slopes.astype(jnp.float32).reshape(Hk, G)[:, :, None, None] * \
        (pos_scale * jnp.abs(rel)).astype(jnp.float32)[None, None]
    s = jnp.einsum('nibkgd,nijkd->nikgbj', qb, kb).astype(jnp.float32) * (dh ** -0.5) + bias
    s = jnp.where(mask[None, :, None, None], s, NEG_INF)
    m = jnp.max(s, axis=-1)
    if sink is not None:
        sk = sink.astype(jnp.float32).reshape(Hk, G)[:, :, None]
        m = jnp.maximum(m, sk)
    p = jnp.exp(s - m[..., None])
    denom = jnp.sum(p, axis=-1)
    if sink is not None:
        denom = denom + jnp.exp(sk - m)
    p = p / denom[..., None]
    o = jnp.einsum('nikgbj,nijkd->nibkgd', p.astype(v.dtype), vb)
    o = o.reshape(N, Lp, H, dh)[:, :L]
    lse = jnp.moveaxis(m + jnp.log(denom), -1, 2).reshape(N, Lp, H)[:, :L]
    return o, lse

def dilated_mixture(q, k, v):
    B, S = q.shape[:2]
    slopes = alibi_slopes(N_DIL_SUB)
    outs, lses = [], []
    for g, (w, r) in enumerate(DIL_PATTERNS):
        sl = slice(g * DIL_HEADS, (g + 1) * DIL_HEADS)

        def strided(t):
            return t[:, :, sl].reshape(B, S // r, r, DIL_HEADS, HEAD_DIM).transpose(0, 2, 1, 3, 4) \
                .reshape(B * r, S // r, DIL_HEADS, HEAD_DIM)

        o, lse = banded_attention(strided(q), strided(k), strided(v), w // (2 * r), DIL_BLOCK,
                                  slopes[sl], r)
        outs.append(o.reshape(B, r, S // r, DIL_HEADS, HEAD_DIM).transpose(0, 2, 1, 3, 4)
                    .reshape(B, S, DIL_HEADS, HEAD_DIM))
        lses.append(lse.reshape(B, r, S // r, DIL_HEADS).transpose(0, 2, 1, 3).reshape(B, S, DIL_HEADS))
    wts = jax.nn.softmax(jnp.stack(lses, axis=0), axis=0)
    return jnp.sum(wts[..., None].astype(q.dtype) * jnp.stack(outs, axis=0), axis=0)

def hybrid_mixer(h, w_in, w_branch_a, w_branch_b, b_gate, sink_logit, w_out):
    B, S, D = h.shape
    proj = jnp.einsum('bsd,dc->bsc', h, w_in)
    qa, ka, va, qw, kw, vw, gates = jnp.split(proj, SPLITS, axis=-1)
    oa = dilated_mixture(qa.reshape(B, S, N_DIL_SUB, HEAD_DIM),
                         ka.reshape(B, S, N_DIL_SUB, HEAD_DIM),
                         va.reshape(B, S, N_DIL_SUB, HEAD_DIM))
    ya = jnp.einsum('bsc,cd->bsd', oa.reshape(B, S, DIL_OUT), w_branch_a)
    ob, _ = banded_attention(qw.reshape(B, S, WIN_Q_HEADS, HEAD_DIM),
                             kw.reshape(B, S, WIN_KV_HEADS, HEAD_DIM),
                             vw.reshape(B, S, WIN_KV_HEADS, HEAD_DIM),
                             WIN_HALF, WIN_BLOCK, alibi_slopes(WIN_Q_HEADS), 1, sink_logit)
    yb = jnp.einsum('bsc,cd->bsd', ob.reshape(B, S, WIN_Q), w_branch_b)
    g = jax.nn.sigmoid((gates + b_gate).astype(jnp.float32)).astype(h.dtype).reshape(B, S, N_BRANCH, D)
    merged = g[:, :, 0] * ya + g[:, :, 1] * yb
    return jnp.einsum('bsd,de->bse', merged, w_out)

def expert_choice_ffn(h, w_router, w_gate, w_up, w_down):
    B, S, D = h.shape
    cap = CAPACITY_FACTOR * S // N_EXPERTS
    aff = jax.nn.softmax(jnp.einsum('bsd,de->bse', h, w_router).astype(jnp.float32), axis=-1)
    gate, idx = lax.top_k(jnp.swapaxes(aff, 1, 2), cap)
    bidx = jnp.arange(B)[:, None, None]
    xe = h[bidx, idx]
    a = jnp.einsum('becd,edf->becf', xe, w_gate)
    u = jnp.einsum('becd,edf->becf', xe, w_up)
    ye = jnp.einsum('becf,efd->becd', jax.nn.silu(a) * u, w_down)
    return jnp.zeros_like(h).at[bidx, idx].add(gate[..., None].astype(h.dtype) * ye)

def first_inputs(seed: int = 0) -> dict:
    key = jax.random.key(seed)
    ks = jax.random.split(key, 14)
    f = jnp.float32
    return {
        "x": jax.random.normal(ks[0], (BATCH, SEQ, D_MODEL), f),
        "norm_mix": 1.0 + 0.02 * jax.random.normal(ks[1], (DEPTH, D_MODEL), f),
        "w_in": jax.random.normal(ks[2], (DEPTH, D_MODEL, IN_COLS), f) * D_MODEL ** -0.5,
        "w_branch_a": jax.random.normal(ks[3], (DEPTH, DIL_OUT, D_MODEL), f) * DIL_OUT ** -0.5,
        "w_branch_b": jax.random.normal(ks[4], (DEPTH, WIN_Q, D_MODEL), f) * WIN_Q ** -0.5,
        "b_gate": 0.1 * jax.random.normal(ks[5], (DEPTH, N_BRANCH * D_MODEL), f),
        "sink_logit": 0.5 * jax.random.normal(ks[6], (DEPTH, WIN_Q_HEADS), f),
        "w_out": jax.random.normal(ks[7], (DEPTH, D_MODEL, D_MODEL), f) * D_MODEL ** -0.5,
        "norm_ffn": 1.0 + 0.02 * jax.random.normal(ks[8], (DEPTH, D_MODEL), f),
        "w_router": jax.random.normal(ks[9], (DEPTH, D_MODEL, N_EXPERTS), f) * D_MODEL ** -0.5,
        "w_expert_gate": jax.random.normal(ks[10], (DEPTH, N_EXPERTS, D_MODEL, D_EXPERT), f) * D_MODEL ** -0.5,
        "w_expert_up": jax.random.normal(ks[11], (DEPTH, N_EXPERTS, D_MODEL, D_EXPERT), f) * D_MODEL ** -0.5,
        "w_expert_down": jax.random.normal(ks[12], (DEPTH, N_EXPERTS, D_EXPERT, D_MODEL), f) * D_EXPERT ** -0.5,
        "norm_final": 1.0 + 0.02 * jax.random.normal(ks[13], (D_MODEL,), f),
    }

def first_block(x, norm_mix, w_in, w_branch_a, w_branch_b, b_gate, sink_logit, w_out,
              norm_ffn, w_router, w_expert_gate, w_expert_up, w_expert_down, norm_final):
    h = x
    for l in range(DEPTH):
        h = h + hybrid_mixer(rmsnorm(h, norm_mix[l]), w_in[l], w_branch_a[l], w_branch_b[l],
                             b_gate[l], sink_logit[l], w_out[l])
        h = h + expert_choice_ffn(rmsnorm(h, norm_ffn[l]), w_router[l], w_expert_gate[l],
                                  w_expert_up[l], w_expert_down[l])
    return rmsnorm(h, norm_final)


DEPTH_2 = 1

CTX_LEN = 256
GRID_W = 64
EPS = 1e-6

HG_HEADS = 4
HG_DK = 128
HG_DV = 128
HG_KDIM = HG_HEADS * HG_DK
HG_WIDTH = HG_HEADS * HG_DV
CHUNK = 32

HY_WIDTH = 512
HY_SHORT = 3
HY_EMB = 33
HY_FILTER_HIDDEN = 64
HY_FILTER_SCALE = 0.05
HY_DECAY_TARGET = 1e-2
HY_FAST_PCT = 0.3
HY_SLOW_PCT = 1.5

SPLIT_POINTS = (HG_KDIM, 2 * HG_KDIM, 3 * HG_KDIM, 3 * HG_KDIM + HG_WIDTH,
                3 * HG_KDIM + 2 * HG_WIDTH, 3 * HG_KDIM + 2 * HG_WIDTH + 3 * HY_WIDTH)
IN_WIDTH = 3 * HG_KDIM + 2 * HG_WIDTH + 3 * HY_WIDTH + 2 * D_MODEL

N_GROUPS = 4
EXPERTS_PER_GROUP = 8
TOP_K = 2
D_EXPERT_2 = 512


F32 = jnp.float32

def rms_norm(x, g):
    xf = x.astype(F32)
    y = xf * lax.rsqrt(jnp.mean(xf * xf, axis=-1, keepdims=True) + EPS)
    return (y * g.astype(F32)).astype(x.dtype)

def adaln(cvec, w, b):
    m = jax.nn.silu(cvec) @ w + b
    return [t[..., None, :] for t in jnp.split(m, 6, axis=-1)]

def modulate(h, shift, scale):
    return h * (1.0 + scale) + shift

def sincos_2d(n_tokens):
    rows = n_tokens // GRID_W
    r = jnp.repeat(jnp.arange(rows, dtype=F32), GRID_W)
    col = jnp.tile(jnp.arange(GRID_W, dtype=F32), rows)
    quarter = D_MODEL // 4
    omega = 1.0 / (10000.0 ** (jnp.arange(quarter, dtype=F32) / quarter))

    def axis_emb(pos):
        a = pos[:, None] * omega[None, :]
        return jnp.concatenate([jnp.sin(a), jnp.cos(a)], axis=-1)

    return jnp.concatenate([axis_emb(r), axis_emb(col)], axis=-1)

def lower_bounds(lb_param):
    p = jax.nn.softmax(lb_param.astype(F32), axis=0)
    return jnp.cumsum(p, axis=0)[:DEPTH_2]

def heads(t, d):
    B, L, _ = t.shape
    return t.reshape(B, L, HG_HEADS, d).transpose(0, 2, 1, 3)

def flip(t):
    return jnp.flip(t, axis=2)

def hgrn2_keys(z, lb):
    z = z.astype(F32)
    log_f = jnp.log(lb + (1.0 - lb) * jax.nn.sigmoid(z))
    k = (1.0 - lb) * jax.nn.sigmoid(-z)
    return heads(k, HG_DK), heads(log_f, HG_DK)

def gla_chunk_scan(q, k, v, log_f, s0):
    B, H, L, DK = q.shape
    DV = v.shape[-1]
    n = L // CHUNK

    def to_chunks(t):
        return t.reshape(B, H, n, CHUNK, t.shape[-1]).transpose(2, 0, 1, 3, 4)

    b = to_chunks(lax.cumsum(log_f.reshape(B, H, n, CHUNK, DK), axis=3).reshape(B, H, L, DK))
    mask = jnp.tril(jnp.ones((CHUNK, CHUNK), dtype=bool))
    mid = CHUNK // 2

    def step(S, xs):
        qc, kc, vc, bc = xs
        total = bc[:, :, -1:, :]
        ref = bc[:, :, mid:mid + 1, :]
        scores = jnp.einsum('bhtk,bhsk->bhts', qc * jnp.exp(bc - ref), kc * jnp.exp(ref - bc))
        scores = jnp.where(mask, scores, 0.0)
        o = (jnp.einsum('bhtk,bhkv->bhtv', qc * jnp.exp(bc), S)
             + jnp.einsum('bhts,bhsv->bhtv', scores, vc))
        S_new = (jnp.exp(total[:, :, 0, :])[..., None] * S
                 + jnp.einsum('bhsk,bhsv->bhkv', kc * jnp.exp(total - bc), vc))
        return S_new, o

    s_fin, o = lax.scan(step, s0, (to_chunks(q), to_chunks(k), to_chunks(v), b))
    return o.transpose(1, 2, 0, 3, 4).reshape(B, H, L, DV), s_fin

def gla_final_state(k, v, log_f):
    decay = jnp.exp(lax.cumsum(log_f, axis=2, reverse=True) - log_f)
    return jnp.einsum('bhlk,bhlv->bhkv', k * decay, v)

def hgrn2_bidir(q, v, fwd, bwd, s0_f, s0_b):
    o_f, s_f = gla_chunk_scan(q, fwd[0], v, fwd[1], s0_f)
    o_b, s_b = gla_chunk_scan(flip(q), flip(bwd[0]), flip(v), flip(bwd[1]), s0_b)
    return o_f + flip(o_b), s_f, s_b

def hgrn2_readout(o, g, norm_g, dtype):
    o = o * lax.rsqrt(jnp.mean(o * o, axis=-1, keepdims=True) + EPS) * norm_g.astype(F32)
    B, H, L, DV = o.shape
    o = o.transpose(0, 2, 1, 3).reshape(B, L, H * DV)
    return (o * jax.nn.silu(g.astype(F32))).astype(dtype)

def short_conv3(u, w, b):
    up = jnp.pad(u, ((0, 0), (1, 1), (0, 0)))
    return up[:, :-2] * w[0] + up[:, 1:-1] * w[1] + up[:, 2:] * w[2] + b

def hyena_filters(L, w1, b1, fr1, w2, b2, fr2, w3):
    t = jnp.linspace(0.0, 1.0, L, dtype=F32)[:, None]
    bands = (HY_EMB - 1) // 2
    ang = (2.0 * math.pi * jnp.arange(L, dtype=F32) / L)[:, None] * \
        jnp.linspace(1e-4, bands - 1, bands, dtype=F32)[None, :]
    z = jnp.concatenate([t, jnp.cos(ang), -jnp.sin(ang)], axis=-1)
    h = jnp.sin(fr1.astype(F32) * (z @ w1.astype(F32) + b1.astype(F32)))
    h = jnp.sin(fr2.astype(F32) * (h @ w2.astype(F32) + b2.astype(F32)))
    h = h @ w3.astype(F32)
    deltas = jnp.abs(jnp.linspace(math.log(HY_DECAY_TARGET) / HY_SLOW_PCT,
                                  math.log(HY_DECAY_TARGET) / HY_FAST_PCT, HY_WIDTH, dtype=F32))
    h = h.reshape(L, 2, HY_WIDTH) * jnp.exp(-t * deltas)[:, None, :]
    return h[:, 0], h[:, 1]

def long_conv_bidir(u, h_fwd, h_bwd, d_skip):
    B, L, C = u.shape
    kern = jnp.concatenate([h_fwd, jnp.zeros((1, C), F32), jnp.flip(h_bwd[1:], axis=0)], axis=0)
    y = jnp.fft.irfft(jnp.fft.rfft(u, n=2 * L, axis=1) * jnp.fft.rfft(kern, axis=0)[None],
                      n=2 * L, axis=1)[:, :L]
    return y + u * d_skip

def hyena_branch(p_hy, conv_w, conv_b, filt, d_skip):
    L = p_hy.shape[1]
    u = short_conv3(p_hy, conv_w, conv_b).astype(F32)
    v, x1, x0 = jnp.split(u, 3, axis=-1)
    h_fwd, h_bwd = hyena_filters(L, *filt)
    y = x0 * long_conv_bidir(v * x1, h_fwd, h_bwd, d_skip.astype(F32))
    return y.astype(p_hy.dtype)

def merge_branches(y_a, y_b, g_logits, w_pa, w_pb, w_o):
    g_a, g_b = jnp.split(g_logits, 2, axis=-1)
    mixed = jax.nn.sigmoid(g_a) * (y_a @ w_pa) + jax.nn.sigmoid(g_b) * (y_b @ w_pb)
    return mixed @ w_o

def token_mixer(p, lb, s0_f, s0_b, hg_norm_g, conv_w, conv_b, filt, d_skip, w_pa, w_pb, w_o):
    q, z_f, z_b, vi, g, p_hy, g_logits = jnp.split(p, SPLIT_POINTS, axis=-1)
    fwd = hgrn2_keys(z_f, lb[0])
    bwd = hgrn2_keys(z_b, lb[1])
    o, s_f, s_b = hgrn2_bidir(heads(q.astype(F32), HG_DK), heads(vi.astype(F32), HG_DV),
                              fwd, bwd, s0_f, s0_b)
    y_a = hgrn2_readout(o, g, hg_norm_g, p.dtype)
    y_b = hyena_branch(p_hy, conv_w, conv_b, filt, d_skip)
    return merge_branches(y_a, y_b, g_logits, w_pa, w_pb, w_o), s_f, s_b

def context_states(p_c, lb):
    z_f, z_b, vi = jnp.split(p_c, (HG_KDIM, 2 * HG_KDIM), axis=-1)
    kf, lf = hgrn2_keys(z_f, lb[0])
    kb, lb_ = hgrn2_keys(z_b, lb[1])
    v = heads(vi.astype(F32), HG_DV)
    return gla_final_state(kf, v, lf), gla_final_state(flip(kb), flip(v), flip(lb_))

def hier_moe(h, wg, bg, we, be, w_gate, w_up, w_down):
    B, L, D = h.shape
    t = h.reshape(B * L, D)
    p_group = jax.nn.softmax((t @ wg + bg).astype(F32), axis=-1)
    p_top_g, g_idx = lax.top_k(p_group, 1)
    e_logits = (jnp.einsum('td,gde->tge', t, we) + be).astype(F32)
    e_logits = jnp.take_along_axis(e_logits, g_idx[:, :, None], axis=1)[:, 0]
    p_top_e, e_idx = lax.top_k(jax.nn.softmax(e_logits, axis=-1), TOP_K)
    w_sel = p_top_g * p_top_e / jnp.sum(p_top_e, axis=-1, keepdims=True)
    combine = (jnp.einsum('tk,tke->te', w_sel, jax.nn.one_hot(e_idx, EXPERTS_PER_GROUP, dtype=F32))[:, None, :]
               * jax.nn.one_hot(g_idx[:, 0], N_GROUPS, dtype=F32)[:, :, None])
    out = jnp.zeros((B * L, D), F32)
    for gi in range(N_GROUPS):
        hid = (jax.nn.silu(jnp.einsum('td,edf->tef', t, w_gate[gi]))
               * jnp.einsum('td,edf->tef', t, w_up[gi])
               * combine[:, gi, :, None].astype(t.dtype))
        out = out + jnp.einsum('tef,efd->td', hid, w_down[gi])
    return out.reshape(B, L, D).astype(h.dtype)

def second_inputs(seed: int = 0) -> dict:
    key = jax.random.key(seed)
    ks = jax.random.split(key, 32)

    def nrm(k, shape, scale):
        return scale * jax.random.normal(k, shape, F32)

    G, E, F = N_GROUPS, EXPERTS_PER_GROUP, D_EXPERT_2
    return {
        "x": nrm(ks[0], (BATCH, SEQ, D_MODEL), 1.0),
        "c": nrm(ks[1], (BATCH, D_MODEL), 1.0),
        "ctx": nrm(ks[2], (BATCH, CTX_LEN, D_MODEL), 1.0),
        "c_ctx": nrm(ks[3], (D_MODEL,), 1.0),
        "ada_w": nrm(ks[4], (DEPTH_2, D_MODEL, 6 * D_MODEL), 0.5 * D_MODEL ** -0.5),
        "ada_b": nrm(ks[5], (DEPTH_2, 6 * D_MODEL), 0.02),
        "norm1_g": 1.0 + nrm(ks[6], (DEPTH_2, D_MODEL), 0.05),
        "norm2_g": 1.0 + nrm(ks[7], (DEPTH_2, D_MODEL), 0.05),
        "w_in": nrm(ks[8], (DEPTH_2, D_MODEL, IN_WIDTH), D_MODEL ** -0.5),
        "hgrn_lb": nrm(ks[9], (DEPTH_2 + 1, 2, HG_KDIM), 0.1),
        "hgrn_norm_g": 1.0 + nrm(ks[10], (DEPTH_2, HG_DV), 0.05),
        "hy_conv_w": nrm(ks[11], (DEPTH_2, HY_SHORT, 3 * HY_WIDTH), HY_SHORT ** -0.5),
        "hy_conv_b": nrm(ks[12], (DEPTH_2, 3 * HY_WIDTH), 0.02),
        "hy_filt_w1": nrm(ks[13], (DEPTH_2, HY_EMB, HY_FILTER_HIDDEN), HY_EMB ** -0.5),
        "hy_filt_b1": nrm(ks[14], (DEPTH_2, HY_FILTER_HIDDEN), 0.1),
        "hy_filt_freq1": 1.0 + nrm(ks[15], (DEPTH_2, HY_FILTER_HIDDEN), 0.1),
        "hy_filt_w2": nrm(ks[16], (DEPTH_2, HY_FILTER_HIDDEN, HY_FILTER_HIDDEN), HY_FILTER_HIDDEN ** -0.5),
        "hy_filt_b2": nrm(ks[17], (DEPTH_2, HY_FILTER_HIDDEN), 0.1),
        "hy_filt_freq2": 1.0 + nrm(ks[18], (DEPTH_2, HY_FILTER_HIDDEN), 0.1),
        "hy_filt_w3": nrm(ks[19], (DEPTH_2, HY_FILTER_HIDDEN, 2 * HY_WIDTH), HY_FILTER_SCALE * HY_FILTER_HIDDEN ** -0.5),
        "hy_d": nrm(ks[20], (DEPTH_2, HY_WIDTH), 0.1),
        "w_proj_a": nrm(ks[21], (DEPTH_2, HG_WIDTH, D_MODEL), HG_WIDTH ** -0.5),
        "w_proj_b": nrm(ks[22], (DEPTH_2, HY_WIDTH, D_MODEL), HY_WIDTH ** -0.5),
        "w_out": nrm(ks[23], (DEPTH_2, D_MODEL, D_MODEL), D_MODEL ** -0.5),
        "moe_router_g_w": nrm(ks[24], (DEPTH_2, D_MODEL, G), D_MODEL ** -0.5),
        "moe_router_g_b": nrm(ks[25], (DEPTH_2, G), 0.01),
        "moe_router_e_w": nrm(ks[26], (DEPTH_2, G, D_MODEL, E), D_MODEL ** -0.5),
        "moe_router_e_b": nrm(ks[27], (DEPTH_2, G, E), 0.01),
        "moe_w_gate": nrm(ks[28], (DEPTH_2, G, E, D_MODEL, F), D_MODEL ** -0.5),
        "moe_w_up": nrm(ks[29], (DEPTH_2, G, E, D_MODEL, F), D_MODEL ** -0.5),
        "moe_w_down": nrm(ks[30], (DEPTH_2, G, E, F, D_MODEL), F ** -0.5),
        "final_norm_g": 1.0 + nrm(ks[31], (D_MODEL,), 0.05),
    }

def second_block(x, c, ctx, c_ctx, ada_w, ada_b, norm1_g, norm2_g, w_in, hgrn_lb, hgrn_norm_g,
              hy_conv_w, hy_conv_b, hy_filt_w1, hy_filt_b1, hy_filt_freq1, hy_filt_w2, hy_filt_b2,
              hy_filt_freq2, hy_filt_w3, hy_d, w_proj_a, w_proj_b, w_out, moe_router_g_w,
              moe_router_g_b, moe_router_e_w, moe_router_e_b, moe_w_gate, moe_w_up, moe_w_down,
              final_norm_g):
    B = x.shape[0]
    x = x + sincos_2d(x.shape[1]).astype(x.dtype)
    lbs = lower_bounds(hgrn_lb)
    zero_state = jnp.zeros((B, HG_HEADS, HG_DK, HG_DV), F32)
    for l in range(DEPTH_2):
        last = l == DEPTH_2 - 1
        sh1, sc1, gt1, sh2, sc2, gt2 = adaln(c, ada_w[l], ada_b[l])
        csh1, csc1, cgt1, csh2, csc2, cgt2 = adaln(c_ctx, ada_w[l], ada_b[l])
        filt = (hy_filt_w1[l], hy_filt_b1[l], hy_filt_freq1[l], hy_filt_w2[l], hy_filt_b2[l],
                hy_filt_freq2[l], hy_filt_w3[l])
        mix_args = (hgrn_norm_g[l], hy_conv_w[l], hy_conv_b[l], filt, hy_d[l],
                    w_proj_a[l], w_proj_b[l], w_out[l])
        hc = modulate(rms_norm(ctx, norm1_g[l]), csh1, csc1)
        if last:
            s_f, s_b = context_states(hc @ w_in[l][:, HG_KDIM:3 * HG_KDIM + HG_WIDTH], lbs[l])
        else:
            ctx_mix, s_f, s_b = token_mixer(hc @ w_in[l], lbs[l], zero_state, zero_state, *mix_args)
        hx = modulate(rms_norm(x, norm1_g[l]), sh1, sc1)
        x_mix, _, _ = token_mixer(hx @ w_in[l], lbs[l], s_f, s_b, *mix_args)
        x = x + gt1 * x_mix
        moe_args = (moe_router_g_w[l], moe_router_g_b[l], moe_router_e_w[l], moe_router_e_b[l],
                    moe_w_gate[l], moe_w_up[l], moe_w_down[l])
        x = x + gt2 * hier_moe(modulate(rms_norm(x, norm2_g[l]), sh2, sc2), *moe_args)
        if not last:
            ctx = ctx + cgt1 * ctx_mix
            ctx = ctx + cgt2 * hier_moe(modulate(rms_norm(ctx, norm2_g[l]), csh2, csc2), *moe_args)
    return rms_norm(x, final_norm_g)


def setup_inputs(seed=0):
    out = dict(first_inputs(seed))
    for name, value in second_inputs(seed + 1).items():
        if name != "x":
            out[name + "_2"] = value
    return out


def reference(
    x, norm_mix, w_in, w_branch_a, w_branch_b, b_gate, sink_logit, w_out, norm_ffn, w_router,
    w_expert_gate, w_expert_up, w_expert_down, norm_final, c_2, ctx_2, c_ctx_2, ada_w_2,
    ada_b_2, norm1_g_2, norm2_g_2, w_in_2, hgrn_lb_2, hgrn_norm_g_2, hy_conv_w_2, hy_conv_b_2,
    hy_filt_w1_2, hy_filt_b1_2, hy_filt_freq1_2, hy_filt_w2_2, hy_filt_b2_2, hy_filt_freq2_2,
    hy_filt_w3_2, hy_d_2, w_proj_a_2, w_proj_b_2, w_out_2, moe_router_g_w_2, moe_router_g_b_2,
    moe_router_e_w_2, moe_router_e_b_2, moe_w_gate_2, moe_w_up_2, moe_w_down_2, final_norm_g_2,
):
    x = first_block(
        x, norm_mix, w_in, w_branch_a, w_branch_b, b_gate, sink_logit, w_out, norm_ffn,
        w_router, w_expert_gate, w_expert_up, w_expert_down, norm_final,
    )
    return second_block(
        x, c_2, ctx_2, c_ctx_2, ada_w_2, ada_b_2, norm1_g_2, norm2_g_2, w_in_2, hgrn_lb_2,
        hgrn_norm_g_2, hy_conv_w_2, hy_conv_b_2, hy_filt_w1_2, hy_filt_b1_2, hy_filt_freq1_2,
        hy_filt_w2_2, hy_filt_b2_2, hy_filt_freq2_2, hy_filt_w3_2, hy_d_2, w_proj_a_2,
        w_proj_b_2, w_out_2, moe_router_g_w_2, moe_router_g_b_2, moe_router_e_w_2,
        moe_router_e_b_2, moe_w_gate_2, moe_w_up_2, moe_w_down_2, final_norm_g_2,
    )


_drawn_inputs = setup_inputs


def setup_inputs(seed=0):
    import zlib

    import numpy as np

    out = dict(_drawn_inputs(seed))
    spreads = {}
    factors = {'norm_mix': 3.988,
     'b_gate': 3.061,
     'sink_logit': 21.448,
     'norm_final': 3.023,
     'ctx_2': 7.644,
     'c_ctx_2': 8.0,
     'ada_b_2': 3.36,
     'norm1_g_2': 4.618,
     'norm2_g_2': 3.179,
     'hgrn_lb_2': 7.467,
     'hgrn_norm_g_2': 8.0,
     'hy_conv_b_2': 8.0,
     'hy_filt_b1_2': 6.34,
     'hy_filt_freq1_2': 8.0,
     'hy_filt_b2_2': 5.881,
     'hy_filt_freq2_2': 8.0,
     'hy_d_2': 2.736,
     'moe_router_g_b_2': 21.634,
     'moe_router_e_b_2': 38.272}
    for name, (base, spread) in spreads.items():
        noise = np.random.default_rng([zlib.crc32(name.encode()), seed]).standard_normal(out[name].shape)
        drawn = base * np.exp(spread * noise) if base else spread * noise
        out[name] = __import__('jax').numpy.asarray(drawn.astype(out[name].dtype))
    for name, factor in factors.items():
        out[name] = (out[name] * factor).astype(out[name].dtype)
    return out
```

```python
from contextlib import ExitStack

import concourse.bass as bass
import numpy as np
from concourse import mybir

F32 = mybir.dt.float32
U32 = mybir.dt.uint32
I32 = mybir.dt.int32
ALU = mybir.AluOpType
ACT = mybir.ActivationFunctionType
AX_X = mybir.AxisListType.X

P = 128
D = 1024
DC = D // P
S = 256
TH = S // P
LAYERS = 2
HD = 64
DIL_SLOTS = 4
DIL_GROUPS = 3
DIL_QKV = DIL_SLOTS * DIL_GROUPS * HD
DIL_STEP = (1, 4, 16)
DIL_REACH = (64, 256, 1024)
WIN_HEADS = 16
WIN_KV = 4
WIN_REACH = 128
IN1 = 3 * DIL_QKV + WIN_HEADS * HD + 2 * WIN_KV * HD + 2 * D
EXPERTS = 16
CAP = 2 * S // EXPERTS
FE = 1024
EPS = 1e-6
MASKED = -1e30

TILE_E = 4
SLOTS = P // TILE_E
TILES1 = EXPERTS // TILE_E

RING = 6
UNIT = 4096
UNITS1_HEAD = 18
UNITS1_TILE = 24
UNITS1 = UNITS1_HEAD + TILES1 * UNITS1_TILE

HY = 512
HY_EMB, HY_HID = 33, 64
KD = 512
HEADS2 = KD // P
CHUNK = 32
CHUNKS = S // CHUNK
GRID = 64
GROUPS, TOP8 = 4, 8
EXPERTS2 = GROUPS * TOP8
ROUTES = GROUPS + EXPERTS2
FE2 = 512
TILES2 = EXPERTS2 // TILE_E
UNITS_L = LAYERS * UNITS1
UNITS2_HEAD = 30
UNITS2_TILE = 12
TURN = 2 * np.pi
TURN_PIECES = (6.28125, 0.0019350051879882812, 3.019916050561733e-07)
ROUNDER = 1.5 * 2.0 ** 23
HALF_TURN = 3.1415925
ARENA = 24832
ROOM = 13355

def slopes(n):
    return [2.0 ** (-8.0 * (i + 1) / n) for i in range(n)]


class Progress:

    def __init__(self, table):
        self.table, self.new = table, {}
        self.n, self.open = 0, []

    def mark(self, *steps):
        self.n += 1
        for step in steps:
            self.new[step] = (self.n, tuple(s for s, _ in self.open))
        return 1

    def enter(self, scope):
        self.open.append((scope, self.n))

    def leave(self, rounds):
        scope, start = self.open.pop()
        self.new[("per", scope)] = (self.n - start, rounds)
        self.n = start + (self.n - start) * rounds

    def leave_counted(self):
        scope, start = self.open[-1]
        self.new[("per", scope)] = (self.n - start, 1)

    @property
    def credit(self):
        return self.table.get(("per", "layer"), (1, 1))[0]

    def at(self, step, loops=None, **back):
        loops = loops or {}
        n, scopes = self.table.get(step, (1, ()))
        value = n + self.credit
        moving = []
        for scope in scopes:
            per, rounds = self.table.get(("per", scope), (1, 1))
            value -= back.get(scope, 0) * per
            round_ = loops.get(scope, rounds - 1)
            if isinstance(round_, int):
                value += round_ * per
            else:
                moving.append(round_ * per)
        for term in moving:
            value = term + value
        return value


C_IDENT, C_ONES = 0, P
C_DIST = 2 * P
C_IOTA = C_DIST + 4 * TH * S
C_TOK = C_IOTA + S
C_EPS = C_TOK + TH
C_COLS = C_EPS + 1
WIN_TABLE = 3


def constants():
    c = np.zeros((P, C_COLS), np.float32)
    c[:, C_IDENT:C_IDENT + P] = np.eye(P)
    c[:, C_ONES:C_ONES + P] = 1.0
    i = np.arange(S)
    dist = np.abs(i[:, None] - i[None, :])
    reach = [(r, m) for r, m in zip(DIL_STEP, DIL_REACH)] + [(1, WIN_REACH)]
    for n, (step, far) in enumerate(reach):
        table = np.where((dist <= far) & (dist % step == 0), -dist.astype(np.float32), np.float32(MASKED))
        c[:, C_DIST + n * TH * S:C_DIST + (n + 1) * TH * S] = (
            table.reshape(TH, P, S).transpose(1, 0, 2).reshape(P, TH * S))
    c[:, C_IOTA:C_IOTA + S] = i
    c[:, C_TOK:C_TOK + TH] = i.reshape(TH, P).T
    c[:, C_EPS] = EPS
    return c


Q_NORM1, Q_NORM2 = 0, DC
Q_BGATE = 2 * DC
Q_SINK = Q_BGATE + 2 * DC
Q_ROUTER = Q_SINK + WIN_HEADS
Q_COLS = Q_ROUTER + DC * EXPERTS


B_CTX = 0
B_SCAN = B_CTX + 2 * P
B_DFT = B_SCAN + 2 * 4 * P
B_IDFT = B_DFT + TH * 2 * S
B_DECAY = B_IDFT + 4 * S
B_POS = B_DECAY + TH * HY
B_COLS = B_POS + S


def constants_2():
    f4 = np.float32
    c = np.zeros((P, B_COLS), np.float32)
    i = np.arange(P)
    of, to = i[:, None], i[None, :]
    c[:, B_CTX:B_CTX + P] = of > to
    c[:, B_CTX + P:B_CTX + 2 * P] = of < to
    together = of // CHUNK == to // CHUNK
    start = to // CHUNK * CHUNK
    for d in range(2):
        before = of <= to if d == 0 else of >= to
        middle = start + CHUNK // 2 - d
        reach = of <= middle if d == 0 else of >= middle
        left = of > to if d == 0 else of < to
        tables = (together & before, together * (before.astype(f4) - reach.astype(f4)), together & left,
                  together & before)
        for n, table in enumerate(tables):
            at = B_SCAN + (d * 4 + n) * P
            c[:, at:at + P] = table
    t, f = np.arange(S, dtype=np.float64), np.arange(S, dtype=np.float64)
    angle = 2 * np.pi * np.outer(t, f) / (2 * S)
    cos, sin = np.cos(angle), np.sin(angle)
    sin[:, 0] = (-1.0) ** t
    for half in range(TH):
        at = B_DFT + half * 2 * S
        rows = slice(half * P, (half + 1) * P)
        c[:, at:at + S], c[:, at + S:at + 2 * S] = cos[rows], sin[rows]
    scale = np.where(f == 0, 1.0, 2.0)[:, None] / (2 * S)
    for n, wave in enumerate((cos.T, sin.T)):
        for chunk in range(2):
            at = B_IDFT + (n * 2 + chunk) * S
            c[:, at:at + S] = (wave * scale)[chunk * P:(chunk + 1) * P]
    along = np.linspace(0, 1, S, dtype=f4)[:, None]
    deltas = np.abs(np.linspace(np.log(1e-2) / 1.5, np.log(1e-2) / 0.3, HY, dtype=f4))
    decay = np.exp(-along * deltas)
    for half in range(TH):
        c[:, B_DECAY + half * HY:B_DECAY + (half + 1) * HY] = decay[half * P:(half + 1) * P]
    bands = (HY_EMB - 1) // 2
    turns = (f4(2 * np.pi) * np.arange(S, dtype=f4) / f4(S))[:, None] * np.linspace(1e-4, bands - 1, bands, dtype=f4)
    c[0:HY_EMB, B_POS:B_POS + S] = np.concatenate([along, np.cos(turns), -np.sin(turns)], axis=1).T
    return c


def positions():
    quarter = D // 4
    omega = (1.0 / 10000.0 ** (np.arange(quarter, dtype=np.float32) / np.float32(quarter))).astype(np.float32)
    token = np.arange(S)
    parts = []
    for pos in (token // GRID, token % GRID):
        a = pos.astype(np.float32)[:, None] * omega
        parts += [np.sin(a), np.cos(a)]
    return np.ascontiguousarray(np.concatenate(parts, axis=1).T.astype(np.float32))


R_FINAL1, R_FINAL2, R_NORM1, R_NORM2 = 0, DC, 2 * DC, 3 * DC
R_ADA = 4 * DC
R_C = R_ADA + 6 * DC
R_HGN = R_C + 2 * DC
R_CONV = R_HGN + 1
R_CONVB = R_CONV + 3 * 3 * HY // P
R_SKIP = R_CONVB + 3 * HY // P
R_ROUTER = R_SKIP + HY // P
R_RBIAS = R_ROUTER + DC * ROUTES
R_W1 = R_RBIAS + ROUTES
R_W2 = R_W1 + HY_HID
R_W3 = R_W2 + HY_HID
R_B1 = R_W3 + 2 * HY
R_FR1, R_B2, R_FR2 = R_B1 + 1, R_B1 + 2, R_B1 + 3
R_COLS = R_B1 + 4


def build(nc, io, tables):
    pe_p, act_p, dve_p = (Progress(tables.get(n, {})) for n in ("pe", "act", "dve"))
    pe_at, act_at, dve_at = pe_p.at, act_p.at, dve_p.at
    with ExitStack() as ctx:
        def sb(name, cols, dt=F32, rows=P):
            return ctx.enter_context(nc.sbuf_tensor(name, [rows, cols], dt))

        def sem(name):
            return ctx.enter_context(nc.semaphore(name))

        ring = sb("ring", RING * UNIT)
        hT = sb("hT", DC * S)
        hnT = sb("hnT", DC * S)
        cst = sb("cst", C_COLS)
        par = sb("par", Q_COLS)
        rms = sb("rms", 2 * S)
        small = sb("small", 208)
        picks = sb("picks", CAP, U32, rows=EXPERTS)
        arena = sb("arena", ARENA)
        n_passes = sb("n_passes", 1, I32)
        banks = [ctx.enter_context(nc.psum_tensor(f"bank{i}", [P, 512], F32)) for i in range(8)]

        h3 = hT[:].rearrange("p (c t) -> p c t", c=DC)
        hn3 = hnT[:].rearrange("p (c t) -> p c t", c=DC)
        ident = cst[:, C_IDENT:C_IDENT + P]
        ones = cst[:, C_ONES:C_ONES + P]
        eps = cst[:, C_EPS:C_EPS + 1]
        rms_root, rms_inv = rms[:, 0:S], rms[:, S:2 * S]

        def dist(table, half):
            at = C_DIST + (table * TH + half) * S
            return cst[:, at:at + S]

        used = [0]

        def piece(cols, start=None):
            if start is not None:
                used[0] = start
            at = used[0]
            used[0] += cols
            assert used[0] <= ARENA
            return arena[:, at:at + cols]

        q_dil = piece(6 * S, 0).rearrange("p (c t) -> p c t", c=6)
        k_dil = piece(12 * S).rearrange("p (c t) -> p c t", c=12)
        v_dil = piece(TH * DIL_QKV).rearrange("p (h c) -> p h c", h=TH)
        q_win_flat = piece(8 * S)
        q_win = q_win_flat.rearrange("p (c t) -> p c t", c=8)
        k_win = piece(8 * S).rearrange("p (c t) -> p c t", c=8)
        v_win = piece(TH * WIN_KV * HD).rearrange("p (h c) -> p h c", h=TH)
        gates_flat = piece(16 * S)
        gates = gates_flat.rearrange("p (c t) -> p c t", c=16)
        prob = piece(2 * TH * DIL_GROUPS * S)
        prob_t = piece(2 * DIL_GROUPS * 512)
        prob_dil = prob.rearrange("p (q h k) -> p q h k", q=TH, h=2)
        WCOLS = S + 1
        prob_win = prob[:, 0:4 * 2 * WCOLS].rearrange("p (b q h k) -> p b q h k", b=2, q=TH, h=2)
        probT_dil = prob_t.rearrange("p (h g x) -> p h g x", h=2, g=DIL_GROUPS)
        probT_win = prob_t[:, 0:2048].rearrange("p (b h x) -> p b h x", b=2, h=2)
        squares = prob[:, 0:2048].rearrange("p (c t) -> p c t", c=DC)
        o_dil = q_dil
        o_win = k_dil
        merged = q_win
        part = prob[:, 0:512]
        hn_tok = piece(TH * D, 0).rearrange("p (h c) -> p h c", h=TH)
        pick = piece(TH * EXPERTS * SLOTS).rearrange("p (h s) -> p h s", h=TH)
        spread1 = piece(TILES1 * S).rearrange("p (g t) -> p g t", g=TILES1)
        x_slots = piece(DC * P).rearrange("p (c s) -> p c s", c=DC)
        silu_sb = piece(FE)
        hid = piece(FE)
        hidT = piece(FE).rearrange("p (f s) -> p f s", f=FE // P)
        y_sb = piece(D)
        idx_diag = piece(EXPERTS * CAP)
        gate_diag = piece(EXPERTS * CAP)
        aff_rows = piece(2 * S)
        topv = piece(CAP)
        idxf = piece(CAP)

        neg_max = small[:, 0:40]
        row_sum = small[:, 40:80]
        row_inv = small[:, 80:120]
        r_max = small[:, 120:122]
        r_sum = small[:, 122:124]
        r_inv = small[:, 124:126]
        r_exp = small[:, 128:160].rearrange("p (h e) -> p h e", h=TH)
        aff = small[:, 160:192].rearrange("p (h e) -> p h e", h=TH)
        slot_cols = small[:, 192:200]

        cst2 = piece(B_COLS, ROOM)
        par2 = piece(R_COLS)
        bounds = piece(4 * KD)
        lower = bounds[:, 0:2 * KD].rearrange("p (d c) -> p d c", d=2)
        upper = bounds[:, 2 * KD:4 * KD].rearrange("p (d c) -> p d c", d=2)
        ada_flat = piece(48 * 2)
        ada = ada_flat.rearrange("p (n r) -> p n r", r=2)
        gain_x, gain_c, gain_2 = (piece(DC) for _ in range(3))
        hc_flat = piece(DC * S)
        hcT = hc_flat.rearrange("p (c t) -> p c t", c=DC)
        y_b = piece(4 * S).rearrange("p (c t) -> p c t", c=4)
        k_cos = piece(2 * HY, 0).rearrange("p (f c) -> p f c", f=2)
        k_sin = piece(2 * HY).rearrange("p (f c) -> p f c", f=2)
        k_nyq = piece(HY)
        hy_work = used[0]
        f_arg, f_turns, f_sin = piece(S), piece(S), piece(S)
        taps_f = piece(2 * HY).rearrange("p (h c) -> p h c", h=TH)
        taps_b = piece(2 * HY).rearrange("p (h c) -> p h c", h=TH)
        taps_sum = piece(2 * HY).rearrange("p (h c) -> p h c", h=TH)
        ada_rows = piece(3 * 512).rearrange("p (r x) -> p r x", r=3)
        c_silu = piece(DC * 32).rearrange("p (k m) -> p k m", k=DC)
        squares2_flat = piece(DC * S)
        squares2 = squares2_flat.rearrange("p (c t) -> p c t", c=DC)
        lb_raw = squares2_flat.rearrange("p (a d c) -> p a d c", a=2, d=2)
        posT = piece(DC * S).rearrange("p (c t) -> p c t", c=DC)
        assert used[0] <= ROOM
        conv = piece(12 * S, hy_work).rearrange("p (c t) -> p c t", c=12)
        u_tok = piece(2 * HY).rearrange("p (h c) -> p h c", h=TH)
        u_cos = piece(2 * HY).rearrange("p (f c) -> p f c", f=2)
        u_sin = piece(2 * HY).rearrange("p (f c) -> p f c", f=2)
        prod_cos = piece(2 * HY).rearrange("p (f c) -> p f c", f=2)
        prod_sin = piece(2 * HY).rearrange("p (f c) -> p f c", f=2)
        prod_part = piece(2 * HY).rearrange("p (f c) -> p f c", f=2)
        assert used[0] <= ROOM
        q_hg = piece(4 * S, 0).rearrange("p (h t) -> p h t", h=HEADS2)
        g_hg = piece(4 * S).rearrange("p (h t) -> p h t", h=HEADS2)
        logf_flat = piece(4 * KD)
        keys_flat = piece(4 * KD)
        vals_flat = piece(2 * KD)
        state0 = piece(2 * KD).rearrange("p (d x) -> p d x", d=2)
        hg_work = used[0]
        logf_c_flat = piece(4 * KD)
        keys_c_flat = piece(4 * KD)
        vals_c_flat = piece(2 * KD)
        assert used[0] <= ROOM
        logf, keys, logf_c, keys_c = (x.rearrange("p (d s c) -> p d s c", d=2, s=TH)
                                      for x in (logf_flat, keys_flat, logf_c_flat, keys_c_flat))
        vals, vals_c = (x.rearrange("p (s c) -> p s c", s=TH) for x in (vals_flat, vals_c_flat))
        keys_decayed = hc_flat.rearrange("p (d s c) -> p d s c", d=2, s=TH)
        e_cum = bounds[:, 0:4 * S].rearrange("p (h t) -> p h t", h=HEADS2)
        q_cum = bounds[:, 4 * S:8 * S].rearrange("p (h t) -> p h t", h=HEADS2)
        k_rest = hc_flat[:, 0:2 * KD].rearrange("p (s c) -> p s c", s=TH)
        inner_flat = hc_flat[:, 2 * KD:4 * KD]
        inner = inner_flat.rearrange("p (s h t) -> p s h t", s=TH, h=HEADS2)
        q_mid = piece(4 * S, hg_work).rearrange("p (h t) -> p h t", h=HEADS2)
        k_mid = piece(4 * S).rearrange("p (h t) -> p h t", h=HEADS2)
        states = piece(4 * KD).rearrange("p (n x) -> p n x", n=4)
        o_tok = piece(2 * KD, hg_work).rearrange("p (s c) -> p s c", s=TH)
        y_a = piece(4 * S).rearrange("p (h t) -> p h t", h=HEADS2)
        o_sq = piece(2 * KD).rearrange("p (s c) -> p s c", s=TH)
        part2 = piece(512).rearrange("p (c t) -> p c t", c=2)
        gates2 = arena[:, 8 * S:24 * S].rearrange("p (c t) -> p c t", c=16)
        merged2 = arena[:, 24 * S:32 * S].rearrange("p (c t) -> p c t", c=DC)
        pick2 = piece(TH * TILES2 * P, 9216).rearrange("p (h s) -> p h s", h=TH)
        weighed = piece(TH * TILES2 * P).rearrange("p (h s) -> p h s", h=TH)
        spread2 = piece(TILES2 * S).rearrange("p (g t) -> p g t", g=TILES2)
        sq_moe = arena[:, 9216:9216 + DC * S].rearrange("p (c t) -> p c t", c=DC)
        routes = piece(1024)
        assert used[0] <= ROOM + B_COLS

        def direction(d):
            at = B_SCAN + d * 4 * P
            return cst2[:, at:at + 2 * P], cst2[:, at + 2 * P:at + 3 * P], cst2[:, at + 3 * P:at + 4 * P]
        routed = [0]

        def field(cols, pattern=None, **sizes):
            at = routed[0]
            routed[0] += cols
            assert routed[0] <= 1024
            out = routes[:, at:at + cols]
            return out.rearrange(pattern, **sizes) if pattern else out

        chosen, weights, rank = (field(TH * EXPERTS2, "p (h e) -> p h e", h=TH) for _ in range(3))
        logits2 = field(TH * ROUTES, "p (h r) -> p h r", h=TH)
        g_padded = field(TH * TOP8, "p (h e) -> p h e", h=TH)
        g_top = field(TH * TOP8, "p (h e) -> p h e", h=TH)
        g_at = field(TH * TOP8).bitcast(U32).rearrange("p (h e) -> p h e", h=TH)
        g_max, g_sum, g_index = (field(TH) for _ in range(3))
        g_exp = field(TH * GROUPS, "p (h g) -> p h g", h=TH)
        in_group = field(TH * GROUPS, "p (h g) -> p h g", h=TH)
        e_masked = field(TH * EXPERTS2, "p (h g e) -> p h g e", h=TH, g=GROUPS)
        e_logits = field(TH * TOP8, "p (h e) -> p h e", h=TH)
        e_top = field(TH * TOP8, "p (h e) -> p h e", h=TH)
        e_at = field(TH * TOP8).bitcast(U32).rearrange("p (h e) -> p h e", h=TH)
        e_index, e_weight = (field(TH * 2, "p (h n) -> p h n", h=TH) for _ in range(2))
        e_diff, e_second = (field(TH) for _ in range(2))
        e_hot, e_part = (field(2 * TH * TOP8, "p (n h e) -> p n h e", n=2, h=TH) for _ in range(2))
        fullest, lots_sum = field(1), field(1)
        lots = field(TOP8)
        o_sum, o_root, o_inv = small[:, 0:8], small[:, 8:16], small[:, 16:24]

        pe_done = sem("tensor_steps_done")
        act_done = sem("scalar_steps_done")
        dve_done = sem("vector_steps_done")
        unit_loaded = [sem(f"unit_loaded_{i}") for i in range(RING)]
        consts_loaded = sem("consts_loaded")
        params_loaded = sem("params_loaded")
        consts2_loaded = sem("second_consts_loaded")
        inputs2_loaded = sem("second_inputs_loaded")
        stored = sem("output_stored")
        waited = sem("waited")

        block = ctx.enter_context(nc.Block())

        def slot(i):
            return ring[:, (i % RING) * UNIT:(i % RING + 1) * UNIT]

        @block.tensor
        def _(pe):
            loops = {}
            taken = {}

            def take(bank, engine, reader):
                if bank in taken:
                    done, at, step = taken[bank]
                    pe.wait_ge(done, at(step, loops))
                taken[bank] = (act_done, act_at, reader) if engine == "act" else (dve_done, dve_at, reader)
                return banks[bank]

            ring_a, ring_v = [0], [0]

            def to_act(reader):
                ring_a[0] += 1
                return take(ring_a[0] % 2, "act", reader)

            def to_dve(reader):
                ring_v[0] += 1
                return take(2 + ring_v[0] % 2, "dve", reader)

            def unit_ready(base, i, rounds=0):
                pe.wait_ge(unit_loaded[i % RING], (rounds + (base + i) // RING + 1) * 16)

            def chunks(out, w, src, n0, n1, cols=P):
                for n in range(n0, n1):
                    for k in range(DC):
                        last = pe.matmul(out[:, (n - n0) * S:(n - n0 + 1) * S], w[:, k, n * P:(n + 1) * P],
                                         src[:, k, :], start=k == 0, stop=k == DC - 1)
                return last

            def by_token(out, w, src, half, c0, cols):
                for k in range(DC):
                    last = pe.matmul(out, src[:, k, half * P:(half + 1) * P], w[:, k, c0:c0 + cols],
                                     start=k == 0, stop=k == DC - 1)
                return last

            def sum_squares(step, sq, cols=S):
                out = to_act(step + " root")
                for k in range(DC):
                    last = pe.matmul(out[:, 0:cols], ones, sq[:, k, :], start=k == 0, stop=k == DC - 1)
                last.then_inc(pe_done, pe_p.mark(step + " sum"))

            def expert_tile(name, base, rounds, hn, pick_of, spread_of, f_width):
                fc = f_width // P
                halves = f_width // 512
                per_unit = 2 // halves
                n_in = DC // per_unit
                for j in range(2):
                    out = to_act(f"{name} x{j}")
                    for c in range(4 * j, 4 * j + 4):
                        for half in range(TH):
                            last = pe.matmul(out[:, (c % 4) * P:(c % 4 + 1) * P], hn[:, half, c * P:(c + 1) * P],
                                             pick_of(half), start=half == 0, stop=half == TH - 1)
                    last.then_inc(pe_done, pe_p.mark(f"{name} x{j}"))
                pe.wait_ge(act_done, act_at(f"{name} x1", loops))
                pe.wait_ge(act_done, act_at(f"{name} y1", loops, **{name: 1}))
                pe.wait_ge(dve_done, dve_at(f"{name} hid", loops, **{name: 1}))
                for which, bank0 in (("gate", 4), ("up", 6)):
                    for n in range(n_in):
                        u = n + (n_in if which == "up" else 0)
                        unit_ready(base, u, rounds)
                        w = slot(u).rearrange("p (e k f) -> p k e f", k=per_unit, e=TILE_E)
                        for k in range(per_unit):
                            c = n * per_unit + k
                            for f in range(halves):
                                for e in range(TILE_E):
                                    last = pe.matmul(banks[bank0 + f][32 * e:32 * e + 32, :],
                                                     x_slots[:, c, 32 * e:32 * e + 32],
                                                     w[:, k, e, f * 512:(f + 1) * 512],
                                                     start=c == 0, stop=c == DC - 1)
                        steps = [f"{name} unit {u}"] + ([f"{name} {which}"] if n == n_in - 1 else [])
                        last.then_inc(pe_done, pe_p.mark(*steps))
                pe.wait_ge(dve_done, dve_at(f"{name} hid", loops))
                for j in range(fc // 4):
                    out = to_act(f"{name} hidT{j}")
                    for f in range(4):
                        last = pe.transpose(out[:, f * P:(f + 1) * P], hid[:, (4 * j + f) * P:(4 * j + f + 1) * P],
                                            ident)
                    last.then_inc(pe_done, pe_p.mark(f"{name} hidT{j}"))
                pe.wait_ge(act_done, act_at(f"{name} hidT{fc // 4 - 1}", loops))
                for f in range(fc):
                    u = 2 * n_in + f
                    unit_ready(base, u, rounds)
                    w = slot(u).rearrange("p (e d) -> p e d", e=TILE_E)
                    for d in range(2):
                        for e in range(TILE_E):
                            last = pe.matmul(banks[4 + d][32 * e:32 * e + 32, :], hidT[:, f, 32 * e:32 * e + 32],
                                             w[:, e, d * 512:(d + 1) * 512], start=f == 0, stop=f == fc - 1)
                    steps = [f"{name} unit {u}"] + ([f"{name} down"] if f == fc - 1 else [])
                    last.then_inc(pe_done, pe_p.mark(*steps))
                pe.wait_ge(act_done, act_at(f"{name} y1", loops))
                for j in range(4):
                    out = to_dve(f"{name} add{j}")
                    for c in range(2):
                        last = pe.matmul(out[:, c * S:(c + 1) * S], y_sb[:, (2 * j + c) * P:(2 * j + c + 1) * P],
                                         spread_of(), start=True, stop=True)
                    last.then_inc(pe_done, pe_p.mark(f"{name} back{j}"))

            pe.sem_inc(pe_done, pe_p.credit)
            pe.wait_ge(consts_loaded, 32)
            pe_p.enter("layer")
            with pe.Fori(0, LAYERS) as layer:
                loops["layer"] = layer
                ring_rounds = layer * (UNITS1 // RING)

                def unit_done(i):
                    return f"unit {i}"

                pe.wait_ge(act_done, act_at("squares", loops))
                sum_squares("norm1", squares)
                pe.wait_ge(dve_done, dve_at("hn1", loops))
                for u in range(8):
                    unit_ready(0, u, ring_rounds)
                    w = slot(u).rearrange("p (k n) -> p k n", k=DC)
                    if u in (0, 1, 2):
                        for j in range(2):
                            pair = 2 * u + j
                            step = f"qk_dil {pair}"
                            out = to_act(step) if pair < 3 else to_dve(step)
                            last = chunks(out, w, hn3, 2 * j, 2 * j + 2)
                            steps = [step] + ([unit_done(u)] if j else [])
                            last.then_inc(pe_done, pe_p.mark(*steps))
                    elif u == 3:
                        for half in range(TH):
                            out = to_act(f"v_dil {half}")
                            last = by_token(out[:], w, hn3, half, 0, 512)
                            last.then_inc(pe_done, pe_p.mark(f"v_dil {half}", unit_done(u)))
                    elif u == 4:
                        w = slot(u)[:, 0:DC * 256].rearrange("p (k n) -> p k n", k=DC)
                        out = to_act("v_dil 2")
                        for half in range(TH):
                            last = by_token(out[:, half * 256:(half + 1) * 256], w, hn3, half, 0, 256)
                        last.then_inc(pe_done, pe_p.mark("v_dil 2", unit_done(u)))
                    elif u in (5, 6):
                        for j in range(2):
                            step = f"q_win {2 * (u - 5) + j}"
                            out = to_act(step)
                            last = chunks(out, w, hn3, 2 * j, 2 * j + 2)
                            last.then_inc(pe_done, pe_p.mark(step, unit_done(u)))
                    else:
                        out = to_dve("k_win")
                        chunks(out, w, hn3, 0, 2).then_inc(pe_done, pe_p.mark("k_win"))
                        out = to_act("v_win")
                        for half in range(TH):
                            last = by_token(out[:, half * 256:(half + 1) * 256], w, hn3, half, 256, 256)
                        last.then_inc(pe_done, pe_p.mark("v_win", unit_done(u)))

                def gate_job(n):
                    u = 8 + n // 2
                    if n % 2 == 0:
                        unit_ready(0, u, ring_rounds)
                    w = slot(u).rearrange("p (k n) -> p k n", k=DC)
                    out = to_dve(f"gate {n}")
                    last = chunks(out, w, hn3, 2 * (n % 2), 2 * (n % 2) + 2)
                    last.then_inc(pe_done, pe_p.mark(f"gate {n}", unit_done(u)))

                flip = {"s": 0, "p": 0}

                def scores(step, q, k):
                    flip["s"] ^= 1
                    out = take(4 + flip["s"], "dve", step)
                    pe.matmul(out[:], q, k, start=True, stop=True).then_inc(pe_done, pe_p.mark(step))

                def turn(step, of):
                    flip["p"] ^= 1
                    out = take(6 + flip["p"], "act", step)
                    for kh in range(TH):
                        for qh in range(TH):
                            last = pe.transpose(out[:, kh * S + qh * P:kh * S + (qh + 1) * P], of(qh, kh), ident)
                    last.then_inc(pe_done, pe_p.mark(step))

                pe.wait_ge(dve_done, dve_at("qk_dil 5", loops))
                pe.wait_ge(act_done, act_at("qk_dil 2", loops))
                for sp in range(DIL_SLOTS // 2):
                    for qh in range(TH):
                        for g in range(DIL_GROUPS):
                            c = 2 * g + sp
                            scores(f"s dil {sp} {qh} {g}", q_dil[:, c, qh * P:(qh + 1) * P],
                                   k_dil[:, 2 * c:2 * c + 2, :])
                    gate_job(2 * sp)
                    gate_job(2 * sp + 1)
                    pe.wait_ge(dve_done, dve_at(f"p dil {sp} {TH - 1}", loops))
                    for g in range(DIL_GROUPS):
                        for h in range(2):
                            turn(f"t dil {sp} {h} {g}",
                                 lambda qh, kh: prob_dil[:, qh, h, g * S + kh * P:g * S + (kh + 1) * P])
                    pe.wait_ge(act_done, act_at(f"t dil {sp} 1 {DIL_GROUPS - 1}", loops))
                    pe.wait_ge(act_done, act_at("v_dil 2", loops))
                    out = to_act(f"o dil {sp}")
                    for g in range(DIL_GROUPS):
                        for kh in range(TH):
                            for h in range(2):
                                head = g * DIL_SLOTS + 2 * sp + h
                                last = pe.matmul(out[h * HD:(h + 1) * HD, 0:S],
                                                 v_dil[:, kh, head * HD:(head + 1) * HD],
                                                 probT_dil[:, h, g, kh * S:(kh + 1) * S],
                                                 start=g == 0 and kh == 0,
                                                 stop=g == DIL_GROUPS - 1 and kh == TH - 1)
                    last.then_inc(pe_done, pe_p.mark(f"o dil {sp}"))

                def win_scores(w):
                    kv = w // 2
                    for qh in range(TH):
                        scores(f"s win {w} {qh}", q_win[:, w, qh * P:(qh + 1) * P], k_win[:, 2 * kv:2 * kv + 2, :])

                pe.wait_ge(dve_done, dve_at("k_win", loops))
                pe.wait_ge(act_done, act_at("v_win", loops))
                pairs = WIN_HEADS // 2
                win_scores(0)
                for w in range(pairs):
                    if w + 1 < pairs:
                        win_scores(w + 1)
                    if w < 4:
                        gate_job(4 + w)
                    pe.wait_ge(dve_done, dve_at(f"p win {w} {TH - 1}", loops))
                    for h in range(2):
                        turn(f"t win {w} {h}",
                             lambda qh, kh: prob_win[:, w % 2, qh, h, kh * P:(kh + 1) * P])
                    pe.wait_ge(act_done, act_at(f"t win {w} 1", loops))
                    out = to_act(f"o win {w}")
                    kv = w // 2
                    for kh in range(TH):
                        for h in range(2):
                            last = pe.matmul(out[h * HD:(h + 1) * HD, 0:S], v_win[:, kh, kv * HD:(kv + 1) * HD],
                                             probT_win[:, w % 2, h, kh * S:(kh + 1) * S],
                                             start=kh == 0, stop=kh == TH - 1)
                    last.then_inc(pe_done, pe_p.mark(f"o win {w}"))

                pe.wait_ge(act_done, act_at(f"o win {pairs - 1}", loops))
                unit_ready(0, 12, ring_rounds)
                unit_ready(0, 13, ring_rounds)
                for j in range(4):
                    out = to_dve(f"ya {j}")
                    for n in range(2):
                        for c in range(2):
                            last = pe.matmul(out[:, n * S:(n + 1) * S],
                                             slot(12 + c)[:, (2 * j + n) * P:(2 * j + n + 1) * P], o_dil[:, c, :],
                                             start=c == 0, stop=c == 1)
                    last.then_inc(pe_done, pe_p.mark(f"ya {j}", unit_done(12), unit_done(13)))
                for j in range(4):
                    u = 14 + j // 2
                    unit_ready(0, u, ring_rounds)
                    w = slot(u).rearrange("p (k n) -> p k n", k=DC)
                    out = to_dve(f"yb {j}")
                    last = chunks(out, w, o_win, 2 * (j % 2), 2 * (j % 2) + 2)
                    last.then_inc(pe_done, pe_p.mark(f"yb {j}", unit_done(u)))
                pe.wait_ge(dve_done, dve_at("yb 3", loops))
                for j in range(4):
                    u = 16 + j // 2
                    unit_ready(0, u, ring_rounds)
                    w = slot(u).rearrange("p (k n) -> p k n", k=DC)
                    out = to_dve(f"mix {j}")
                    last = chunks(out, w, merged, 2 * (j % 2), 2 * (j % 2) + 2)
                    last.then_inc(pe_done, pe_p.mark(f"mix {j}", unit_done(u)))

                pe.wait_ge(act_done, act_at("squares2", loops))
                sum_squares("norm2", squares)
                pe.wait_ge(dve_done, dve_at("hn2", loops))
                out = take(0, "act", "router exp")
                for half in range(TH):
                    for k in range(DC):
                        last = pe.matmul(out[:, half * EXPERTS:(half + 1) * EXPERTS],
                                         hn3[:, k, half * P:(half + 1) * P],
                                         par[:, Q_ROUTER + k * EXPERTS:Q_ROUTER + (k + 1) * EXPERTS],
                                         start=k == 0, stop=k == DC - 1)
                last.then_inc(pe_done, pe_p.mark("router"))
                for j in range(4):
                    half, c0 = j // 2, 4 * (j % 2)
                    out = take((1, 4, 5, 6)[j], "act", f"hn_tok {j}")
                    for c in range(4):
                        last = pe.transpose(out[:, c * P:(c + 1) * P], hn3[:, c0 + c, half * P:(half + 1) * P], ident)
                    last.then_inc(pe_done, pe_p.mark(f"hn_tok {j}"))
                pe.wait_ge(dve_done, dve_at("aff", loops))
                out = take(2, "dve", "aff rows")
                for half in range(TH):
                    last = pe.transpose(out[0:EXPERTS, half * P:(half + 1) * P], aff[:, half, :], ident)
                last.then_inc(pe_done, pe_p.mark("aff rows"))
                pe.wait_ge(dve_done, dve_at("diag", loops))
                out = take(3, "dve", "picked")
                pe.matmul(out[:], ones[0:EXPERTS, :], idx_diag[0:EXPERTS, :], start=True, stop=True)\
                  .then_inc(pe_done, pe_p.mark("slot tokens"))
                out = take(2, "dve", "slot cols")
                for g in range(TILES1):
                    for n, diag in enumerate((idx_diag, gate_diag)):
                        last = pe.matmul(out[:, n * TILES1 + g:n * TILES1 + g + 1],
                                         diag[0:EXPERTS, g * P:(g + 1) * P], ones[0:EXPERTS, 0:1],
                                         start=True, stop=True)
                last.then_inc(pe_done, pe_p.mark("slot cols"))

                pe.wait_ge(dve_done, dve_at("spread", loops))
                pe.wait_ge(act_done, act_at("hn_tok 3", loops))
                pe.sem_inc(waited, 1)
                taken.clear()
                ring_a[0] = ring_v[0] = 0
                taken[1] = (act_done, lambda step, l: act_at(step, l, tile=1), f"tile hidT0")
                taken[0] = (act_done, lambda step, l: act_at(step, l, tile=1), f"tile hidT1")
                taken[3] = (dve_done, lambda step, l: dve_at(step, l, tile=1), f"tile add2")
                taken[2] = (dve_done, lambda step, l: dve_at(step, l, tile=1), f"tile add3")
                pe_p.enter("tile")
                with pe.Fori(0, TILES1) as t:
                    loops["tile"] = t
                    expert_tile("tile", UNITS1_HEAD, ring_rounds + t * (UNITS1_TILE // RING), hn_tok,
                                lambda half: pick[:, half, bass.ds(t * P, P)],
                                lambda: spread1[:, t, :], FE)
                pe_p.leave(TILES1)
                del loops["tile"]
                taken.clear()
                ring_a[0] = ring_v[0] = 0
            pe_p.leave(LAYERS)
            del loops["layer"]
            def row_of(half):
                return slice(half * P, (half + 1) * P)

            pe.wait_ge(consts2_loaded, 48)
            pe.wait_ge(dve_done, dve_at("tile add3"))
            out = to_act("f_sin 1")
            pe.matmul(out[0:HY_HID, 0:S], par2[0:HY_EMB, R_W1:R_W1 + HY_HID], cst2[0:HY_EMB, B_POS:B_POS + S], start=True,
                      stop=True).then_inc(pe_done, pe_p.mark("filter 1"))
            pe.wait_ge(act_done, act_at("f_sin 1"))
            out = to_act("f_sin 2")
            pe.matmul(out[0:HY_HID, 0:S], par2[0:HY_HID, R_W2:R_W2 + HY_HID], f_sin[0:HY_HID, :], start=True,
                      stop=True).then_inc(pe_done, pe_p.mark("filter 2"))
            pe.wait_ge(act_done, act_at("f_sin 2"))
            for n in range(2):
                for half in range(TH):
                    out = to_dve(f"taps {n} {half}")
                    pe.matmul(out[:], f_sin[0:HY_HID, row_of(half)], par2[0:HY_HID, R_W3 + n * HY:R_W3 + (n + 1) * HY],
                              start=True, stop=True).then_inc(pe_done, pe_p.mark(f"taps {n} {half}"))

            def spectrum(step, taps, sine, f):
                out = to_dve(step)
                for half in range(TH):
                    at = B_DFT + half * 2 * S + sine * S + f * P
                    last = pe.matmul(out[:], cst2[:, at:at + P], taps[:, half, :], start=half == 0, stop=half == TH - 1)
                last.then_inc(pe_done, pe_p.mark(step))

            pe.wait_ge(dve_done, dve_at("taps"))
            for f in range(2):
                spectrum(f"k_cos {f}", taps_sum, 0, f)
            for f in range(2):
                spectrum(f"k_sin {f}", taps_f, 1, f)
            out = to_dve("k_nyq")
            for half in range(TH):
                at = B_DFT + half * 2 * S + S
                last = pe.matmul(out[0:1, :], cst2[:, at:at + 1], taps_sum[:, half, :], start=half == 0, stop=half == 1)
            last.then_inc(pe_done, pe_p.mark("k_nyq"))

            pe.wait_ge(act_done, act_at("c_silu"))
            pe.wait_ge(dve_done, dve_at("c_pad"))
            for u in range(12):
                if u % 4 == 0:
                    out = to_act(f"ada {u // 4}")
                unit_ready(UNITS_L, u)
                w = slot(u).rearrange("p (k n) -> p k n", k=DC)
                for k in range(DC):
                    for b in range(4):
                        last = pe.matmul(out[32 * b:32 * b + 32, (u % 4) * P:(u % 4 + 1) * P], c_silu[:, k, :],
                                         w[:, k, b * P:(b + 1) * P], start=k == 0, stop=k == DC - 1)
                steps = [f"unit2 {u}"] + ([f"ada {u // 4}"] if u % 4 == 3 else [])
                last.then_inc(pe_done, pe_p.mark(*steps))
            for r in range(3):
                pe.wait_ge(act_done, act_at(f"ada {r}"))
                out = to_dve(f"ada cols {r}")
                for b in range(4):
                    last = pe.transpose(out[:, b * P:(b + 1) * P], ada_rows[:, r, b * P:(b + 1) * P], ident)
                last.then_inc(pe_done, pe_p.mark(f"ada cols {r}"))

            pe.wait_ge(act_done, act_at("c squares"))
            sum_squares("c norm", squares2)
            pe.wait_ge(act_done, act_at("f squares"))
            sum_squares("f norm", squares2)
            pe.wait_ge(act_done, act_at("x squares"))
            sum_squares("x norm", squares2)

            pe.wait_ge(dve_done, dve_at("hx"))
            for u in range(12, 15):
                unit_ready(UNITS_L, u)
                w = slot(u).rearrange("p (k n) -> p k n", k=DC)
                for j in range(2):
                    step = f"hy {2 * (u - 12) + j}"
                    out = to_dve(step)
                    last = chunks(out, w, hn3, 2 * j, 2 * j + 2)
                    last.then_inc(pe_done, pe_p.mark(step, f"unit2 {u}"))
            pe.wait_ge(dve_done, dve_at("hy u"))
            for half in range(TH):
                out = to_act(f"u_tok {half}")
                for c in range(4):
                    last = pe.transpose(out[:, c * P:(c + 1) * P], conv[:, c, row_of(half)], ident)
                last.then_inc(pe_done, pe_p.mark(f"u_tok {half}"))
            pe.wait_ge(act_done, act_at("u_tok 1"))
            for f in range(2):
                for sine in range(2):
                    step = f"u {'sin' if sine else 'cos'} {f}"
                    out = to_act(step)
                    for half in range(TH):
                        at = B_DFT + half * 2 * S + sine * S + f * P
                        last = pe.matmul(out[:], cst2[:, at:at + P], u_tok[:, half, :], start=half == 0,
                                         stop=half == TH - 1)
                    last.then_inc(pe_done, pe_p.mark(step))
            pe.wait_ge(dve_done, dve_at("products"))
            for j in range(2):
                out = to_dve(f"hy y {j}")
                for c in range(2):
                    ch = slice((2 * j + c) * P, (2 * j + c + 1) * P)
                    for n, prod in enumerate((prod_cos, prod_sin)):
                        for f in range(2):
                            at = B_IDFT + (n * 2 + f) * S
                            last = pe.matmul(out[:, c * S:(c + 1) * S], prod[:, f, ch], cst2[:, at:at + S],
                                             start=n == 0 and f == 0, stop=n == 1 and f == 1)
                last.then_inc(pe_done, pe_p.mark(f"hy y {j}"))

            pe.wait_ge(dve_done, dve_at("y_b"))
            for u in range(15, 18):
                unit_ready(UNITS_L, u)
                w = slot(u).rearrange("p (k n) -> p k n", k=DC)
                for n in range(4):
                    src, half = (hcT, hn3)[n // 2], n % 2
                    out = to_act(f"z {u - 15} {n}")
                    last = by_token(out[:], w, src, half, 0, 512)
                    last.then_inc(pe_done, pe_p.mark(f"z {u - 15} {n}", f"unit2 {u}"))
            for u in range(18, 20):
                unit_ready(UNITS_L, u)
                w = slot(u).rearrange("p (k n) -> p k n", k=DC)
                for j in range(2):
                    step = f"qg {2 * (u - 18) + j}"
                    out = to_act(step)
                    last = chunks(out, w, hn3, 2 * j, 2 * j + 2)
                    last.then_inc(pe_done, pe_p.mark(step, f"unit2 {u}"))

            pe.wait_ge(act_done, act_at("log c"))
            for d in range(2):
                near = cst2[:, B_CTX + d * P:B_CTX + (d + 1) * P]
                for half in range(TH):
                    out = to_act(f"decay {d} {half}")
                    whole = half == d
                    last = pe.matmul(out[:], near, logf_c[:, d, half, :], start=True, stop=not whole)
                    if whole:
                        last = pe.matmul(out[:], ones, logf_c[:, d, 1 - half, :], start=False, stop=True)
                    last.then_inc(pe_done, pe_p.mark(f"decay {d} {half}"))
            for d in range(2):
                pe.wait_ge(dve_done, dve_at(f"decayed {d}"))
                out = to_dve(f"state0 {d}")
                for h in range(HEADS2):
                    for half in range(TH):
                        last = pe.matmul(out[:, h * P:(h + 1) * P], keys_decayed[:, d, half, h * P:(h + 1) * P],
                                         vals_c[:, half, h * P:(h + 1) * P], start=half == 0, stop=half == TH - 1)
                last.then_inc(pe_done, pe_p.mark(f"state0 {d}"))

            pe.wait_ge(act_done, act_at("log x"))
            pe.wait_ge(act_done, act_at("qg 3"))
            o_banks = (4, 5)
            for d in range(2):
                sums, rest, _ = direction(d)
                for half in range(TH):
                    for pair in range(2):
                        out = to_act(f"cum {d} {half} {pair}")
                        for h in range(2):
                            last = pe.matmul(out[:, h * S:(h + 1) * S],
                                             logf[:, d, half, (2 * pair + h) * P:(2 * pair + h + 1) * P], sums,
                                             start=True, stop=True)
                        last.then_inc(pe_done, pe_p.mark(f"cum {d} {half} {pair}"))
                    out = to_act(f"rest {d} {half}")
                    pe.matmul(out[:], rest, logf[:, d, half, :], start=True, stop=True)\
                      .then_inc(pe_done, pe_p.mark(f"rest {d} {half}"))
                    out = to_dve(f"keyT {d} {half}")
                    for h in range(HEADS2):
                        last = pe.transpose(out[:, h * P:(h + 1) * P], keys[:, d, half, h * P:(h + 1) * P], ident)
                    last.then_inc(pe_done, pe_p.mark(f"keyT {d} {half}"))
                for half in range(TH):
                    pe.wait_ge(dve_done, dve_at(f"qk {d} {half}"))
                    out = to_dve(f"inner {d} {half}")
                    for h in range(HEADS2):
                        last = pe.matmul(out[:, h * P:(h + 1) * P], k_mid[:, h, row_of(half)], q_mid[:, h, row_of(half)],
                                         start=True, stop=True)
                    last.then_inc(pe_done, pe_p.mark(f"inner {d} {half}"))
                for half in range(TH):
                    pe.wait_ge(dve_done, dve_at(f"inner {d} {half}"))
                    for h in range(HEADS2):
                        last = pe.matmul(banks[o_banks[half]][:, h * P:(h + 1) * P], inner[:, half, h, :],
                                         vals[:, half, h * P:(h + 1) * P], start=d == 0 and h == 0, stop=False,
                                         skip_group_check=True)
                    last.then_inc(pe_done, pe_p.mark(f"o inner {d} {half}"))
                pe.wait_ge(dve_done, dve_at(f"k_rest {d}"))
                for n in range(CHUNKS):
                    c = n if d == 0 else CHUNKS - 1 - n
                    half, at = c // 4, 32 * (c % 4)
                    rows = slice(at, at + CHUNK)
                    if n < CHUNKS - 1:
                        out = to_dve(f"grown {d} {n}")
                        for h in range(HEADS2):
                            last = pe.matmul(out[:, h * P:(h + 1) * P], k_rest[rows, half, h * P:(h + 1) * P],
                                             vals[rows, half, h * P:(h + 1) * P], start=True, stop=True)
                        last.then_inc(pe_done, pe_p.mark(f"grown {d} {n}"))
                    pe.wait_ge(dve_done, dve_at(f"state {d} {n}"))
                    state = state0[:, d, :] if n == 0 else states[:, n % 4, :]
                    for h in range(HEADS2):
                        last = pe.matmul(banks[o_banks[half]][rows, h * P:(h + 1) * P],
                                         q_cum[:, h, half * P + at:half * P + at + CHUNK],
                                         state[:, h * P:(h + 1) * P], start=False,
                                         stop=d == 1, skip_group_check=True)
                    last.then_inc(pe_done, pe_p.mark(f"o {d} {n}"))
            taken[4] = taken[5] = (act_done, act_at, "o_sq 1")
            for half in range(TH):
                pe.wait_ge(dve_done, dve_at(f"o_tok {half}"))
                out = to_dve(f"y_a {half}")
                for h in range(HEADS2):
                    last = pe.transpose(out[:, h * P:(h + 1) * P], o_tok[:, half, h * P:(h + 1) * P], ident)
                last.then_inc(pe_done, pe_p.mark(f"y_a {half}"))

            for u in range(20, 24):
                unit_ready(UNITS_L, u)
                w = slot(u).rearrange("p (k n) -> p k n", k=DC)
                for j in range(2):
                    step = f"gates2 {2 * (u - 20) + j}"
                    out = to_act(step)
                    last = chunks(out, w, hn3, 2 * j, 2 * j + 2)
                    last.then_inc(pe_done, pe_p.mark(step, f"unit2 {u}"))
            for name, u0, src in (("pa", 24, y_a), ("pb", 26, y_b)):
                pe.wait_ge(dve_done, dve_at("y_a 1"))
                unit_ready(UNITS_L, u0)
                unit_ready(UNITS_L, u0 + 1)
                for j in range(4):
                    out = to_dve(f"{name} {j}")
                    for n in range(2):
                        for k in range(4):
                            w = slot(u0 + k // 2)[:, 0:2 * D].rearrange("p (k n) -> p k n", k=2)
                            last = pe.matmul(out[:, n * S:(n + 1) * S], w[:, k % 2, (2 * j + n) * P:(2 * j + n + 1) * P],
                                             src[:, k, :], start=k == 0, stop=k == 3)
                    last.then_inc(pe_done, pe_p.mark(f"{name} {j}", f"unit2 {u0}", f"unit2 {u0 + 1}"))
            pe.wait_ge(dve_done, dve_at("pb 3"))
            for j in range(4):
                u = 28 + j // 2
                unit_ready(UNITS_L, u)
                w = slot(u).rearrange("p (k n) -> p k n", k=DC)
                out = to_dve(f"mix2 {j}")
                last = chunks(out, w, merged2, 2 * (j % 2), 2 * (j % 2) + 2)
                last.then_inc(pe_done, pe_p.mark(f"mix2 {j}", f"unit2 {u}"))

            pe.wait_ge(act_done, act_at("m squares"))
            sum_squares("m norm", sq_moe)
            pe.wait_ge(dve_done, dve_at("h2"))
            out = to_dve("logits2")
            for half in range(TH):
                for k in range(DC):
                    at = R_ROUTER + k * ROUTES
                    last = pe.matmul(out[:, half * ROUTES:(half + 1) * ROUTES], hn3[:, k, row_of(half)],
                                     par2[:, at:at + ROUTES], start=k == 0, stop=k == DC - 1)
            last.then_inc(pe_done, pe_p.mark("logits2"))
            for j in range(4):
                half, c0 = j // 2, 4 * (j % 2)
                out = to_act(f"hn_tok2 {j}")
                for c in range(4):
                    last = pe.transpose(out[:, c * P:(c + 1) * P], hn3[:, c0 + c, row_of(half)], ident)
                last.then_inc(pe_done, pe_p.mark(f"hn_tok2 {j}"))
            pe.wait_ge(dve_done, dve_at("chosen"))
            out = to_dve("rank")
            before = cst2[:, B_CTX + P:B_CTX + 2 * P]
            for half in range(TH):
                cols = slice(half * EXPERTS2, (half + 1) * EXPERTS2)
                last = pe.matmul(out[:, cols], before, chosen[:, half, :], start=True, stop=half == 0)
                if half:
                    last = pe.matmul(out[:, cols], ones, chosen[:, 0, :], start=False, stop=True)
            for half in range(TH):
                last = pe.matmul(out[:, TH * EXPERTS2:(TH + 1) * EXPERTS2], ones, chosen[:, half, :],
                                 start=half == 0, stop=half == TH - 1)
            last.then_inc(pe_done, pe_p.mark("rank"))

            pe.wait_ge(dve_done, dve_at("passes"))
            passes = pe.value_load(n_passes[0:1, 0:1], min_val=1, max_val=S // SLOTS)
            pe_p.enter("pass")
            with pe.Fori(0, passes) as p:
                loops["pass"] = p
                taken.clear()
                ring_a[0] = ring_v[0] = 0
                pe.wait_ge(dve_done, dve_at("weighed", loops))
                pe.wait_ge(act_done, act_at("hn_tok2 3", loops))
                for j in range(TILES2 // 2):
                    out = to_act(f"spread2 {j}")
                    for n in range(2):
                        for half in range(TH):
                            g = 2 * j + n
                            last = pe.transpose(out[:, n * S + half * P:n * S + (half + 1) * P],
                                                weighed[:, half, g * P:(g + 1) * P], ident)
                    last.then_inc(pe_done, pe_p.mark(f"spread2 {j}"))
                pe.wait_ge(act_done, act_at(f"spread2 {TILES2 // 2 - 1}", loops))
                pe.sem_inc(waited, 1)
                taken.clear()
                ring_a[0] = ring_v[0] = 0
                taken[1] = (act_done, lambda step, l: act_at(step, l, tile2=1), "tile2 hidT0")
                taken[0] = (act_done, lambda step, l: act_at(step, l, tile2=1), "tile2 x1")
                taken[3] = (dve_done, lambda step, l: dve_at(step, l, tile2=1), "tile2 add2")
                taken[2] = (dve_done, lambda step, l: dve_at(step, l, tile2=1), "tile2 add3")
                pe_p.enter("tile2")
                with pe.Fori(0, TILES2) as t:
                    loops["tile2"] = t
                    expert_tile("tile2", UNITS_L + UNITS2_HEAD,
                                p * (TILES2 * UNITS2_TILE // RING) + t * (UNITS2_TILE // RING), hn_tok,
                                lambda half: pick2[:, half, bass.ds(t * P, P)], lambda: spread2[:, t, :], FE2)
                pe_p.leave(TILES2)
                del loops["tile2"]
            pe_p.leave_counted()
            loops["pass"] = passes
            pe.wait_ge(act_done, act_at("l squares", loops, **{"pass": 1}))
            for k in range(DC):
                last = pe.matmul(banks[0][:, 0:S], ones, sq_moe[:, k, :], start=k == 0, stop=k == DC - 1)
            last.then_inc(pe_done, pe_p.mark("l norm sum"))

        @block.scalar
        def _(act):
            loops = {}

            def copy(step, out, in_, scale=1.0):
                act.wait_ge(pe_done, pe_at(step, loops))
                act.activation(out, in_, ACT.Copy, scale=scale).then_inc(act_done, act_p.mark(step))

            def two(bank, n=2):
                return bank[:].rearrange("p (c t) -> p c t", c=n)

            ring_a = [0]

            def bank_a():
                ring_a[0] += 1
                return banks[ring_a[0] % 2]

            def root(step, cols=S, out=None):
                bank = bank_a()
                act.wait_ge(pe_done, pe_at(step + " sum", loops))
                act.activation(rms_root if out is None else out, bank[:, 0:cols], ACT.Sqrt, bias=eps,
                               scale=1.0 / D).then_inc(act_done, act_p.mark(step + " root"))

            def expert_tile(name, f_width):
                fc = f_width // P
                for j in range(2):
                    copy(f"{name} x{j}", x_slots[:, 4 * j:4 * j + 4, :], two(bank_a(), 4))
                act.wait_ge(dve_done, dve_at(f"{name} hid", loops, **{name: 1}))
                act.wait_ge(pe_done, pe_at(f"{name} gate", loops))
                for f in range(f_width // 512):
                    act.activation(silu_sb[:, f * 512:(f + 1) * 512], banks[4 + f][:], ACT.Silu)\
                       .then_inc(act_done, act_p.mark(f"{name} silu {f}"))
                for j in range(fc // 4):
                    copy(f"{name} hidT{j}", hidT[:, 4 * j:4 * j + 4, :], two(bank_a(), 4))
                act.wait_ge(pe_done, pe_at(f"{name} back3", loops, **{name: 1}))
                act.wait_ge(pe_done, pe_at(f"{name} down", loops))
                for d in range(2):
                    act.activation(y_sb[:, d * 512:(d + 1) * 512], banks[4 + d][:], ACT.Copy)\
                       .then_inc(act_done, act_p.mark(f"{name} y{d}"))

            act.sem_inc(act_done, act_p.credit)
            act.wait_ge(consts_loaded, 32)
            act_p.enter("layer")
            with act.Fori(0, LAYERS) as layer:
                loops["layer"] = layer
                act.wait_ge(dve_done, dve_at("tile add3", loops, layer=1))
                act.activation(squares, h3, ACT.Square).then_inc(act_done, act_p.mark("squares"))
                root("norm1")
                for j in range(3):
                    copy(f"qk_dil {j}", q_dil[:, 2 * j:2 * j + 2, :], two(bank_a()), HD ** -0.5)
                for half in range(TH):
                    copy(f"v_dil {half}", v_dil[:, half, 0:512], bank_a()[:])
                copy("v_dil 2", v_dil[:, :, 512:768], two(bank_a()))
                for j in range(4):
                    copy(f"q_win {j}", q_win[:, 2 * j:2 * j + 2, :], two(bank_a()), HD ** -0.5)
                copy("v_win", v_win, two(bank_a()))
                flip = [0]

                def bank_p():
                    flip[0] ^= 1
                    return banks[6 + flip[0]]

                def exps(step, col, row):
                    act.wait_ge(dve_done, dve_at("m" + step, loops))
                    for h in range(2):
                        act.activation(row(h), row(h), ACT.Exp, bias=neg_max[:, col + h:col + h + 1],
                                       accum_out=row_sum[:, col + h:col + h + 1])\
                           .then_inc(act_done, act_p.mark(f"e{step} {h}"))

                for sp in range(2):
                    for qh in range(TH):
                        exps(f" dil {sp} {qh}", 4 * sp + 2 * qh, lambda h: prob_dil[:, qh, h, :])
                    if sp:
                        act.wait_ge(pe_done, pe_at(f"o dil {sp - 1}", loops))
                    for g in range(DIL_GROUPS):
                        for h in range(2):
                            copy(f"t dil {sp} {h} {g}", probT_dil[:, h, g, :], bank_p()[:])
                    copy(f"o dil {sp}", o_dil[:, sp, :], bank_a()[:, 0:S])
                pairs = WIN_HEADS // 2

                def win_exps(w):
                    for qh in range(TH):
                        exps(f" win {w} {qh}", 8 + 4 * w + 2 * qh, lambda h: prob_win[:, w % 2, qh, h, :])

                win_exps(0)
                for w in range(pairs):
                    if w + 1 < pairs:
                        win_exps(w + 1)
                    act.wait_ge(pe_done, pe_at(f"o win {w - 2}" if w >= 2 else "o dil 1", loops))
                    for h in range(2):
                        copy(f"t win {w} {h}", probT_win[:, w % 2, h, :], bank_p()[:])
                    copy(f"o win {w}", o_win[:, w, :], bank_a()[:, 0:S])
                act.wait_ge(dve_done, dve_at("gate 7", loops))
                act.activation(gates_flat, gates_flat, ACT.Sigmoid).then_inc(act_done, act_p.mark("gates"))
                act.wait_ge(dve_done, dve_at("mix 3", loops))
                act.activation(squares, h3, ACT.Square).then_inc(act_done, act_p.mark("squares2"))
                root("norm2")
                act.wait_ge(dve_done, dve_at("router max", loops))
                for half in range(TH):
                    act.activation(r_exp[:, half, :], banks[0][:, half * EXPERTS:(half + 1) * EXPERTS], ACT.Exp,
                                   bias=r_max[:, half:half + 1], accum_out=r_sum[:, half:half + 1])\
                       .then_inc(act_done, act_p.mark("router exp"))
                for j in range(4):
                    half, c0 = j // 2, 4 * (j % 2)
                    copy(f"hn_tok {j}", hn_tok[:, half, c0 * P:(c0 + 4) * P], banks[(1, 4, 5, 6)[j]][:])
                ring_a[0] = 0
                act_p.enter("tile")
                with act.Fori(0, TILES1) as t:
                    loops["tile"] = t
                    expert_tile("tile", FE)
                act_p.leave(TILES1)
                del loops["tile"]
                ring_a[0] = 0
            act_p.leave(LAYERS)
            del loops["layer"]
            def row_of(half):
                return slice(half * P, (half + 1) * P)

            act.wait_ge(consts2_loaded, 48)
            act.wait_ge(inputs2_loaded, 32)
            act.wait_ge(dve_done, dve_at("lb shifted"))
            act.activation(lb_raw, lb_raw, ACT.Exp).then_inc(act_done, act_p.mark("lb exp"))
            act.wait_ge(dve_done, dve_at("c_pad"))
            for r in range(2):
                act.activation(c_silu[:, :, r], par2[:, R_C + r * DC:R_C + (r + 1) * DC], ACT.Silu)\
                   .then_inc(act_done, act_p.mark("c_silu"))
            for n in (1, 2):
                bank_a()
                if n == 2:
                    act.wait_ge(pe_done, pe_at("filter 2"))
                act.wait_ge(dve_done, dve_at(f"f_arg {n}"))
                act.activation(f_sin[0:HY_HID, :], f_arg[0:HY_HID, :], ACT.Sin)\
                   .then_inc(act_done, act_p.mark(f"f_sin {n}"))
            for r in range(3):
                copy(f"ada {r}", ada_rows[:, r, :], bank_a()[:])
            act.wait_ge(dve_done, dve_at("bounds"))
            act.activation(squares2, hcT, ACT.Square).then_inc(act_done, act_p.mark("c squares"))
            root("c norm")
            act.activation(squares2, h3, ACT.Square).then_inc(act_done, act_p.mark("f squares"))
            act.wait_ge(dve_done, dve_at("c norm inv"))
            root("f norm")
            act.wait_ge(dve_done, dve_at("x"))
            act.activation(squares2, h3, ACT.Square).then_inc(act_done, act_p.mark("x squares"))
            root("x norm")
            for half in range(TH):
                copy(f"u_tok {half}", u_tok[:, half, :], bank_a()[:])
            for f in range(2):
                copy(f"u cos {f}", u_cos[:, f, :], bank_a()[:])
                copy(f"u sin {f}", u_sin[:, f, :], bank_a()[:])
            for d in range(2):
                for n in range(4):
                    bank = bank_a()
                    lf, ks, half = (logf_c, keys_c, n) if n < 2 else (logf, keys, n - 2)
                    act.wait_ge(pe_done, pe_at(f"z {d} {n}"))
                    act.activation(lf[:, d, half, :], bank[:], ACT.Sigmoid)
                    act.activation(ks[:, d, half, :], bank[:], ACT.Sigmoid, scale=-1.0)\
                       .then_inc(act_done, act_p.mark(f"z {d} {n}"))
            for n in range(4):
                copy(f"z 2 {n}", (vals_c if n < 2 else vals)[:, n % 2, :], bank_a()[:])
            for j in range(2):
                copy(f"qg {j}", q_hg[:, 2 * j:2 * j + 2, :], two(bank_a()))
            for j in range(2):
                act.wait_ge(pe_done, pe_at(f"qg {2 + j}"))
                act.activation(g_hg[:, 2 * j:2 * j + 2, :], two(bank_a()), ACT.Silu)\
                   .then_inc(act_done, act_p.mark(f"qg {2 + j}"))
            for which, flat in (("c", logf_c_flat), ("x", logf_flat)):
                act.wait_ge(dve_done, dve_at(f"keys {which}"))
                act.activation(flat, flat, ACT.Ln).then_inc(act_done, act_p.mark(f"log {which}"))
            for d in range(2):
                for half in range(TH):
                    act.wait_ge(pe_done, pe_at(f"decay {d} {half}"))
                    act.activation(keys_decayed[:, d, half, :], bank_a()[:], ACT.Exp)\
                       .then_inc(act_done, act_p.mark(f"decay {d} {half}"))
            for d in range(2):
                if d:
                    act.wait_ge(pe_done, pe_at(f"o 0 {CHUNKS - 1}"))
                    act.wait_ge(dve_done, dve_at(f"state 0 {CHUNKS - 1}"))
                else:
                    act.wait_ge(dve_done, dve_at("decayed 1"))
                for half in range(TH):
                    for pair in range(2):
                        bank = bank_a()[:].rearrange("p (h x t) -> p h x t", h=2, x=2)
                        heads = slice(2 * pair, 2 * pair + 2)
                        act.wait_ge(pe_done, pe_at(f"cum {d} {half} {pair}"))
                        act.activation(e_cum[:, heads, row_of(half)], bank[:, :, 0, :], ACT.Exp)
                        act.activation(q_mid[:, heads, row_of(half)], bank[:, :, 1, :], ACT.Exp)
                        act.activation(k_mid[:, heads, row_of(half)], bank[:, :, 1, :], ACT.Exp, scale=-1.0)\
                           .then_inc(act_done, act_p.mark(f"cum {d} {half} {pair}"))
                    act.wait_ge(pe_done, pe_at(f"rest {d} {half}"))
                    act.activation(k_rest[:, half, :], bank_a()[:], ACT.Exp)\
                       .then_inc(act_done, act_p.mark(f"rest {d} {half}"))
            act.wait_ge(pe_done, pe_at(f"o 1 {CHUNKS - 1}"))
            for half in range(TH):
                act.activation(o_sq[:, half, :], banks[4 + half][:], ACT.Square)\
                   .then_inc(act_done, act_p.mark(f"o_sq {half}"))
            act.wait_ge(dve_done, dve_at("o sums"))
            act.activation(o_root, o_sum, ACT.Sqrt, bias=eps, scale=1.0 / P).then_inc(act_done, act_p.mark("o root"))
            for j in range(8):
                act.wait_ge(pe_done, pe_at(f"gates2 {j}"))
                act.activation(gates2[:, 2 * j:2 * j + 2, :], two(bank_a()), ACT.Sigmoid)\
                   .then_inc(act_done, act_p.mark(f"gates2 {j}"))
            act.wait_ge(dve_done, dve_at("mix2 3"))
            act.activation(sq_moe, h3, ACT.Square).then_inc(act_done, act_p.mark("m squares"))
            root("m norm")
            for j in range(4):
                half, c0 = j // 2, 4 * (j % 2)
                place = hn_tok[:, half, :].rearrange("t (k c q) -> t c q k", k=DC, c=DC)[:, c0:c0 + 4]
                copy(f"hn_tok2 {j}", place, bank_a()[:].rearrange("t (c q k) -> t c q k", c=4, k=DC))
            act.wait_ge(dve_done, dve_at("group max"))
            for half in range(TH):
                act.activation(g_exp[:, half, :], logits2[:, half, 0:GROUPS], ACT.Exp,
                               bias=g_max[:, half:half + 1], accum_out=g_sum[:, half:half + 1])\
                   .then_inc(act_done, act_p.mark("group exp"))
            act.wait_ge(dve_done, dve_at("second less first"))
            act.activation(e_second, e_diff, ACT.Exp).then_inc(act_done, act_p.mark("second"))

            act.wait_ge(dve_done, dve_at("passes"))
            passes = act.value_load(n_passes[0:1, 0:1], min_val=1, max_val=S // SLOTS)
            act_p.enter("pass")
            with act.Fori(0, passes) as p:
                loops["pass"] = p
                ring_a[0] = 0
                for j in range(TILES2 // 2):
                    copy(f"spread2 {j}", spread2[:, 2 * j:2 * j + 2, :], two(bank_a()))
                ring_a[0] = 0
                act_p.enter("tile2")
                with act.Fori(0, TILES2) as t:
                    loops["tile2"] = t
                    expert_tile("tile2", FE2)
                act_p.leave(TILES2)
                del loops["tile2"]
            act_p.leave_counted()
            loops["pass"] = passes
            one_back = {"pass": 1}
            act.wait_ge(dve_done, dve_at("tile2 add3", loops, **one_back))
            act.activation(sq_moe, h3, ACT.Square).then_inc(act_done, act_p.mark("l squares"))
            act.wait_ge(pe_done, pe_at("l norm sum", loops, **one_back))
            act.activation(rms_root, banks[0][:, 0:S], ACT.Sqrt, bias=eps, scale=1.0 / D)\
               .then_inc(act_done, act_p.mark("l norm root"))

        @block.vector
        def _(dve):
            loops = {}
            ring_v = [0]

            def bank_v():
                ring_v[0] += 1
                return banks[2 + ring_v[0] % 2]

            def then(ins, step):
                ins.then_inc(dve_done, dve_p.mark(step))
                dve.wait_ge(dve_done, dve_at(step, loops))

            def two(bank, n=2):
                return bank[:].rearrange("p (c t) -> p c t", c=n)

            def normed(step, name, gain, src, out):
                dve.wait_ge(act_done, act_at(step + " root", loops))
                then(dve.reciprocal(rms_inv, rms_root), step + " inv")
                for c in range(DC):
                    last = dve.scalar_tensor_tensor(out[:, c, :], src[:, c, :], gain[:, c:c + 1], rms_inv,
                                                    ALU.mult, ALU.mult)
                last.then_inc(dve_done, dve_p.mark(name))

            def expert_tile(name, f_width, add):
                dve.wait_ge(pe_done, pe_at(f"{name} hidT{f_width // 512 - 1}", loops, **{name: 1}))
                dve.wait_ge(pe_done, pe_at(f"{name} up", loops))
                for f in range(f_width // 512):
                    dve.wait_ge(act_done, act_at(f"{name} silu {f}", loops))
                    last = dve.tensor_tensor(hid[:, f * 512:(f + 1) * 512], silu_sb[:, f * 512:(f + 1) * 512],
                                             banks[6 + f][:], ALU.mult)
                last.then_inc(dve_done, dve_p.mark(f"{name} hid"))
                for j in range(4):
                    bank = bank_v()
                    dve.wait_ge(pe_done, pe_at(f"{name} back{j}", loops))
                    add(j, two(bank)).then_inc(dve_done, dve_p.mark(f"{name} add{j}"))

            dve.sem_inc(dve_done, dve_p.credit)
            dve.wait_ge(consts_loaded, 32)
            dve_p.enter("layer")
            with dve.Fori(0, LAYERS) as layer:
                loops["layer"] = layer
                then(dve.memset(k_dil, 0.0), "k_dil zero")
                then(dve.memset(k_win, 0.0), "k_win zero")
                dve.wait_ge(params_loaded, layer * 16 + 16)
                normed("norm1", "hn1", par[:, Q_NORM1:Q_NORM1 + DC], h3, hn3)
                for j in range(3, 6):
                    bank = two(bank_v())
                    c = 2 * (j - 3)
                    dve.wait_ge(pe_done, pe_at(f"qk_dil {j}", loops))
                    for r in range(2):
                        rows = slice(r * HD, (r + 1) * HD)
                        last = dve.tensor_copy(k_dil[rows, 2 * c + r:2 * c + r + 3:2, :], bank[rows, :, :])
                    last.then_inc(dve_done, dve_p.mark(f"qk_dil {j}"))
                bank = two(bank_v())
                dve.wait_ge(pe_done, pe_at("k_win", loops))
                for kv in range(2):
                    for r in range(2):
                        last = dve.tensor_copy(k_win[r * HD:(r + 1) * HD, 2 * kv + r:2 * kv + r + 5:4, :],
                                               bank[kv * HD:(kv + 1) * HD, :, :])
                last.then_inc(dve_done, dve_p.mark("k_win"))
                flip = [0]

                def bank_s():
                    flip[0] ^= 1
                    return banks[4 + flip[0]]

                def biased(step, name, table, qh, slope, row):
                    bank = bank_s()
                    dve.wait_ge(pe_done, pe_at(step, loops))
                    for h in range(2):
                        last = dve.scalar_tensor_tensor(row(h), dist(table, qh), slope(h),
                                                        bank[:, h * S:(h + 1) * S], ALU.mult, ALU.add)
                    last.then_inc(dve_done, dve_p.mark(step, name))

                def maxima(step, name, col, rows):
                    dve.wait_ge(dve_done, dve_at(name, loops))
                    dve.tensor_reduce(neg_max[:, col:col + 2], rows, AX_X, ALU.max, negate=True)\
                       .then_inc(dve_done, dve_p.mark(step))

                def probs(step, col, row):
                    dve.wait_ge(act_done, act_at(f"e{step} 1", loops))
                    then(dve.reciprocal(row_inv[:, col:col + 2], row_sum[:, col:col + 2]), "inv" + step)
                    for h in range(2):
                        last = dve.tensor_scalar(row(h), row(h), row_inv[:, col + h:col + h + 1], None, ALU.mult)
                    last.then_inc(dve_done, dve_p.mark("p" + step))

                def gate_job(n):
                    bank = two(bank_v())
                    dve.wait_ge(pe_done, pe_at(f"gate {n}", loops))
                    for c in range(2):
                        last = dve.tensor_scalar(gates[:, 2 * n + c, :], bank[:, c, :],
                                                 par[:, Q_BGATE + 2 * n + c:Q_BGATE + 2 * n + c + 1], None, ALU.add)
                    last.then_inc(dve_done, dve_p.mark(f"gate {n}"))

                dil_slope = slopes(DIL_SLOTS * DIL_GROUPS)
                for sp in range(2):
                    if sp:
                        dve.wait_ge(pe_done, pe_at(f"t dil {sp - 1} 1 {DIL_GROUPS - 1}", loops))
                    for qh in range(TH):
                        for g in range(DIL_GROUPS):
                            biased(f"s dil {sp} {qh} {g}", f"b dil {sp} {qh} {g}", g, qh,
                                   lambda h: dil_slope[g * DIL_SLOTS + 2 * sp + h],
                                   lambda h: prob_dil[:, qh, h, g * S:(g + 1) * S])
                        maxima(f"m dil {sp} {qh}", f"b dil {sp} {qh} {DIL_GROUPS - 1}", 4 * sp + 2 * qh,
                               prob_dil[:, qh, :, :])
                    for qh in range(TH):
                        probs(f" dil {sp} {qh}", 4 * sp + 2 * qh, lambda h: prob_dil[:, qh, h, :])
                    gate_job(2 * sp)
                    gate_job(2 * sp + 1)

                win_slope = slopes(WIN_HEADS)

                def win_scores(w):
                    before = f"t win {w - 2} 1" if w >= 2 else f"t dil 1 1 {DIL_GROUPS - 1}"
                    dve.wait_ge(pe_done, pe_at(before, loops))
                    for qh in range(TH):
                        dve.tensor_copy(prob_win[:, w % 2, qh, :, S:S + 1],
                                        par[:, Q_SINK + 2 * w:Q_SINK + 2 * w + 2].unsqueeze(2))\
                           .then_inc(dve_done, dve_p.mark(f"sink {w} {qh}"))
                        biased(f"s win {w} {qh}", f"b win {w} {qh}", WIN_TABLE, qh,
                               lambda h: win_slope[2 * w + h], lambda h: prob_win[:, w % 2, qh, h, 0:S])
                        maxima(f"m win {w} {qh}", f"b win {w} {qh}", 8 + 4 * w + 2 * qh, prob_win[:, w % 2, qh, :, :])

                win_scores(0)
                for w in range(WIN_HEADS // 2):
                    if w + 1 < WIN_HEADS // 2:
                        win_scores(w + 1)
                    for qh in range(TH):
                        probs(f" win {w} {qh}", 8 + 4 * w + 2 * qh, lambda h: prob_win[:, w % 2, qh, h, 0:S])
                    if w < 4:
                        gate_job(4 + w)

                dve.wait_ge(act_done, act_at("gates", loops))
                for j in range(4):
                    bank = bank_v()
                    dve.wait_ge(pe_done, pe_at(f"ya {j}", loops))
                    dve.tensor_tensor(merged[:, 2 * j:2 * j + 2, :], two(bank), gates[:, 2 * j:2 * j + 2, :],
                                      ALU.mult).then_inc(dve_done, dve_p.mark(f"ya {j}"))
                for j in range(4):
                    bank = bank_v()
                    dve.wait_ge(pe_done, pe_at(f"yb {j}", loops))
                    then(dve.tensor_tensor(part.rearrange("p (c t) -> p c t", c=2), two(bank),
                                           gates[:, 8 + 2 * j:8 + 2 * j + 2, :], ALU.mult), f"yb {j} gated")
                    then(dve.tensor_tensor(merged[:, 2 * j:2 * j + 2, :], merged[:, 2 * j:2 * j + 2, :],
                                           part.rearrange("p (c t) -> p c t", c=2), ALU.add), f"yb {j}")
                for j in range(4):
                    bank = bank_v()
                    dve.wait_ge(pe_done, pe_at(f"mix {j}", loops))
                    dve.tensor_tensor(h3[:, 2 * j:2 * j + 2, :], h3[:, 2 * j:2 * j + 2, :], two(bank), ALU.add)\
                       .then_inc(dve_done, dve_p.mark(f"mix {j}"))

                normed("norm2", "hn2", par[:, Q_NORM2:Q_NORM2 + DC], h3, hn3)
                dve.wait_ge(pe_done, pe_at("router", loops))
                logits = banks[0][:, 0:TH * EXPERTS].rearrange("p (h e) -> p h e", h=TH)
                dve.tensor_reduce(r_max, logits, AX_X, ALU.max, negate=True)\
                   .then_inc(dve_done, dve_p.mark("router max"))
                dve.wait_ge(act_done, act_at("router exp", loops))
                then(dve.reciprocal(r_inv, r_sum), "router inv")
                dve.tensor_tensor(aff, r_exp, r_inv.unsqueeze(2).broadcast_to([P, TH, EXPERTS]), ALU.mult)\
                   .then_inc(dve_done, dve_p.mark("aff"))
                dve.wait_ge(pe_done, pe_at("aff rows", loops))
                left = [aff_rows[0:EXPERTS, 0:S], aff_rows[0:EXPERTS, S:2 * S]]
                then(dve.tensor_copy(left[0], banks[2][0:EXPERTS, 0:S]), "aff rows")
                dve.sem_inc(waited, 1)
                for r in range(CAP // 8):
                    best = topv[0:EXPERTS, 8 * r:8 * r + 8]
                    then(dve.max(best, left[r % 2]), f"top {r}")
                    dve.sem_inc(waited, 1)
                    dve.max_index(picks[:, 8 * r:8 * r + 8], best, left[r % 2])\
                       .then_inc(dve_done, dve_p.mark(f"index {r}"))
                    if r + 1 < CAP // 8:
                        then(dve.match_replace(left[1 - r % 2], best, left[r % 2], -1.0), f"left {r}")
                        dve.sem_inc(waited, 1)
                dve.wait_ge(dve_done, dve_at(f"index {CAP // 8 - 1}", loops))
                then(dve.tensor_copy(idxf[0:EXPERTS, :], picks[:, :]), "index")
                eye = ident[0:EXPERTS, 0:EXPERTS].unsqueeze(2).broadcast_to([EXPERTS, EXPERTS, CAP])
                for diag, rows in ((idx_diag, idxf), (gate_diag, topv)):
                    last = dve.tensor_tensor(diag[0:EXPERTS, :].rearrange("p (e s) -> p e s", e=EXPERTS), eye,
                                             rows[0:EXPERTS, :].unsqueeze(1).broadcast_to([EXPERTS, EXPERTS, CAP]),
                                             ALU.mult)
                last.then_inc(dve_done, dve_p.mark("diag"))
                dve.wait_ge(pe_done, pe_at("slot tokens", loops))
                for half in range(TH):
                    last = dve.tensor_scalar(pick[:, half, :], banks[3][:], cst[:, C_TOK + half:C_TOK + half + 1],
                                             None, ALU.is_equal)
                last.then_inc(dve_done, dve_p.mark("picked"))
                dve.wait_ge(pe_done, pe_at("slot cols", loops))
                then(dve.tensor_copy(slot_cols, banks[2][:, 0:8]), "slot cols")
                for g in range(TILES1):
                    last = dve.tensor_scalar(spread1[:, g, :], cst[:, C_IOTA:C_IOTA + S], slot_cols[:, g:g + 1],
                                             slot_cols[:, TILES1 + g:TILES1 + g + 1], ALU.is_equal, ALU.mult)
                last.then_inc(dve_done, dve_p.mark("spread"))
                ring_v[0] = 0
                dve_p.enter("tile")
                with dve.Fori(0, TILES1) as t:
                    loops["tile"] = t
                    expert_tile("tile", FE, lambda j, back: dve.tensor_tensor(
                        h3[:, 2 * j:2 * j + 2, :], h3[:, 2 * j:2 * j + 2, :], back, ALU.add))
                dve_p.leave(TILES1)
                del loops["tile"]
                ring_v[0] = 0
            dve_p.leave(LAYERS)
            del loops["layer"]
            def row_of(half):
                return slice(half * P, (half + 1) * P)

            def scaled(step, name, src, out, gain, shift):
                dve.wait_ge(act_done, act_at(step + " root", loops))
                then(dve.reciprocal(rms_inv, rms_root), step + " inv")
                then(dve.tensor_tensor(out, src, rms_inv.unsqueeze(1).broadcast_to([P, DC, S]), ALU.mult),
                     step + " normed")
                for c in range(DC):
                    last = dve.tensor_scalar(out[:, c, :], out[:, c, :], gain[:, c:c + 1], shift(c), ALU.mult, ALU.add)
                last.then_inc(dve_done, dve_p.mark(name))

            dve.wait_ge(consts2_loaded, 48)
            dve.wait_ge(inputs2_loaded, 32)
            then(dve.tensor_tensor(lower, lb_raw[:, 0], lb_raw[:, 1], ALU.max), "lb max")
            for a in range(2):
                last = dve.tensor_tensor(lb_raw[:, a], lb_raw[:, a], lower, ALU.subtract)
            last.then_inc(dve_done, dve_p.mark("lb shifted"))
            then(dve.memset(c_silu, 0.0), "c_pad")
            dve.wait_ge(act_done, act_at("lb exp"))
            then(dve.tensor_tensor(upper, lb_raw[:, 0], lb_raw[:, 1], ALU.add), "lb sum")
            then(dve.reciprocal(upper, upper), "lb inv")
            then(dve.tensor_tensor(lower, lb_raw[:, 0], upper, ALU.mult), "lower")
            then(dve.tensor_scalar(upper, lower, -1.0, 1.0, ALU.mult, ALU.add), "bounds")

            def sine_arg(n, bank, bias, freq):
                a, m = f_arg[0:HY_HID, :], f_turns[0:HY_HID, :]
                dve.wait_ge(pe_done, pe_at(f"filter {n}"))
                then(dve.tensor_scalar(a, bank[0:HY_HID, 0:S], par2[0:HY_HID, bias:bias + 1], par2[0:HY_HID, freq:freq + 1],
                                       ALU.add, ALU.mult), f"arg {n}")
                then(dve.tensor_scalar(m, a, 1.0 / TURN, ROUNDER, ALU.mult, ALU.add), f"turns {n} rounded")
                then(dve.tensor_scalar(m, m, -ROUNDER, None, ALU.add), f"turns {n}")
                for i, piece_ in enumerate(TURN_PIECES):
                    then(dve.scalar_tensor_tensor(a, m, -piece_, a, ALU.mult, ALU.add), f"turn {n} {i}")
                then(dve.tensor_scalar(a, a, HALF_TURN, -HALF_TURN, ALU.min, ALU.max), f"f_arg {n}")

            sine_arg(1, banks[1], R_B1, R_FR1)
            sine_arg(2, banks[0], R_B2, R_FR2)
            for n, taps in enumerate((taps_f, taps_b)):
                for half in range(TH):
                    bank = bank_v()
                    dve.wait_ge(pe_done, pe_at(f"taps {n} {half}"))
                    at = B_DECAY + half * HY
                    dve.tensor_tensor(taps[:, half, :], bank[:], cst2[:, at:at + HY], ALU.mult)\
                       .then_inc(dve_done, dve_p.mark(f"taps {n} {half}"))
            dve.wait_ge(dve_done, dve_at("taps 1 1"))
            then(dve.memset(taps_b[0:1, 0, :], 0.0), "taps_b zero")
            then(dve.tensor_tensor(taps_sum, taps_f, taps_b, ALU.add), "taps sum")
            then(dve.tensor_tensor(taps_f, taps_f, taps_b, ALU.subtract), "taps")
            for name, dst in (("k_cos", k_cos), ("k_sin", k_sin)):
                for f in range(2):
                    bank = bank_v()
                    dve.wait_ge(pe_done, pe_at(f"{name} {f}"))
                    dve.tensor_copy(dst[:, f, :], bank[:]).then_inc(dve_done, dve_p.mark(f"{name} {f}"))
            dve.wait_ge(dve_done, dve_at("k_sin 1"))
            dve.memset(k_sin[0:1, 0, :], 0.0)
            then(dve.tensor_copy(k_nyq, k_cos[:, 0, :]), "k_nyq rest")
            bank = bank_v()
            dve.wait_ge(pe_done, pe_at("k_nyq"))
            dve.tensor_copy(k_nyq[0:1, :], bank[0:1, :]).then_inc(dve_done, dve_p.mark("k_nyq"))

            for r in range(3):
                bank = bank_v()[:].rearrange("p (j b x) -> p j b x", j=4, b=4)
                dve.wait_ge(pe_done, pe_at(f"ada cols {r}"))
                cols = slice(16 * r, 16 * r + 16)
                bias = par2[:, R_ADA + 16 * r:R_ADA + 16 * r + 16].rearrange("p (j b) -> p j b", j=4)
                then(dve.tensor_tensor(ada[:, cols, :].rearrange("p (j b) r -> p j b r", j=4), bank[:, :, :, 0:2],
                                       bias.unsqueeze(3).broadcast_to([P, 4, 4, 2]), ALU.add), f"ada cols {r}")
            for gain, scale, row, norm in ((gain_x, 1, 0, R_NORM1), (gain_c, 1, 1, R_NORM1), (gain_2, 4, 0, R_NORM2)):
                last = dve.scalar_tensor_tensor(gain, ada[:, scale * DC:(scale + 1) * DC, row], 1.0,
                                                par2[:, norm:norm + DC], ALU.add, ALU.mult)
            then(last, "gains")
            scaled("c norm", "hc", hcT, hcT, gain_c, lambda c: ada[:, c, 1:2])
            normed("f norm", "first block", par2[:, R_FINAL1:R_FINAL1 + DC], h3, h3)
            dve.wait_ge(dve_done, dve_at("first block"))
            then(dve.tensor_tensor(h3, h3, posT, ALU.add), "x")
            scaled("x norm", "hx", h3, hn3, gain_x, lambda c: ada[:, c, 0:1])

            for j in range(6):
                bank = two(bank_v())
                dve.wait_ge(pe_done, pe_at(f"hy {j}"))

                def tap(c, w):
                    at = R_CONV + w * 12 + 2 * j + c
                    return par2[:, at:at + 1]

                for c in range(2):
                    at = R_CONVB + 2 * j + c
                    last = dve.tensor_scalar(conv[:, 2 * j + c, :], bank[:, c, :], tap(c, 1), par2[:, at:at + 1],
                                             ALU.mult, ALU.add)
                then(last, f"conv {j} 1")
                for c in range(2):
                    now = conv[:, 2 * j + c, 1:S]
                    last = dve.scalar_tensor_tensor(now, bank[:, c, 0:S - 1], tap(c, 0), now, ALU.mult, ALU.add)
                then(last, f"conv {j} 0")
                for c in range(2):
                    now = conv[:, 2 * j + c, 0:S - 1]
                    last = dve.scalar_tensor_tensor(now, bank[:, c, 1:S], tap(c, 2), now, ALU.mult, ALU.add)
                then(last, f"hy {j}")
            then(dve.tensor_tensor(conv[:, 0:4, :], conv[:, 0:4, :], conv[:, 4:8, :], ALU.mult), "hy u")
            dve.wait_ge(act_done, act_at("u sin 1"))
            dve.tensor_tensor(prod_cos, u_cos, k_cos, ALU.mult)
            then(dve.tensor_tensor(prod_part, u_sin, k_sin, ALU.mult), "products 1")
            then(dve.tensor_tensor(prod_cos, prod_cos, prod_part, ALU.subtract), "products 2")
            dve.tensor_tensor(prod_sin, u_cos, k_sin, ALU.mult)
            dve.tensor_tensor(prod_part[:, 0, :], u_sin[:, 0, :], k_nyq, ALU.mult)
            then(dve.tensor_tensor(prod_part[:, 1, :], u_sin[:, 1, :], k_cos[:, 1, :], ALU.mult), "products 3")
            then(dve.tensor_tensor(prod_sin, prod_sin, prod_part, ALU.add), "products")
            for j in range(2):
                bank = two(bank_v())
                dve.wait_ge(pe_done, pe_at(f"hy y {j}"))
                for c in range(2):
                    at = R_SKIP + 2 * j + c
                    last = dve.scalar_tensor_tensor(y_b[:, 2 * j + c, :], conv[:, 2 * j + c, :], par2[:, at:at + 1],
                                                    bank[:, c, :], ALU.mult, ALU.add)
                then(last, f"hy y {j}")
            then(dve.tensor_tensor(y_b, y_b, conv[:, 8:12, :], ALU.mult), "y_b")

            for d in range(2):
                for which, lf, ks, n in (("c", logf_c, keys_c, 1), ("x", logf, keys, 3)):
                    wide = [P, TH, KD]
                    up, low = (x[:, d, :].unsqueeze(1).broadcast_to(wide) for x in (upper, lower))
                    dve.wait_ge(act_done, act_at(f"z {d} {n}"))
                    dve.tensor_tensor(ks[:, d], ks[:, d], up, ALU.mult)
                    then(dve.tensor_tensor(lf[:, d], lf[:, d], up, ALU.mult), f"gate {d} {which}")
                    then(dve.tensor_tensor(lf[:, d], lf[:, d], low, ALU.add), f"keys {which}" if d else f"keys 0 {which}")
            for d in range(2):
                dve.wait_ge(act_done, act_at(f"decay {d} 1"))
                dve.tensor_tensor(keys_decayed[:, d], keys_decayed[:, d], keys_c[:, d], ALU.mult)\
                   .then_inc(dve_done, dve_p.mark(f"decayed {d}"))
            for d in range(2):
                bank = bank_v()
                dve.wait_ge(pe_done, pe_at(f"state0 {d}"))
                then(dve.tensor_copy(state0[:, d, :], bank[:]), f"state0 {d}")
            for d in range(2):
                mask = direction(d)[2].bitcast(U32)
                for half in range(TH):
                    bank = bank_v()[:].rearrange("p (h t) -> p h t", h=HEADS2)
                    rows = row_of(half)
                    dve.wait_ge(act_done, act_at(f"cum {d} {half} 1"))
                    dve.tensor_tensor(q_mid[:, :, rows], q_mid[:, :, rows], q_hg[:, :, rows], ALU.mult)
                    dve.tensor_tensor(q_cum[:, :, rows], e_cum[:, :, rows], q_hg[:, :, rows], ALU.mult)
                    dve.wait_ge(pe_done, pe_at(f"keyT {d} {half}"))
                    dve.tensor_tensor(k_mid[:, :, rows], k_mid[:, :, rows], bank, ALU.mult)\
                       .then_inc(dve_done, dve_p.mark(f"keyT {d} {half}", f"qk {d} {half}"))
                dve.wait_ge(pe_done, pe_at("o inner 0 1" if d else "state0 1"))
                then(dve.memset(inner_flat, 0.0), f"inner {d} zero")
                for half in range(TH):
                    bank = bank_v()[:].rearrange("p (h t) -> p h t", h=HEADS2)
                    dve.wait_ge(pe_done, pe_at(f"inner {d} {half}"))
                    dve.copy_predicated(inner[:, half], mask.unsqueeze(1).broadcast_to([P, HEADS2, P]), bank)\
                       .then_inc(dve_done, dve_p.mark(f"inner {d} {half}"))
                dve.wait_ge(act_done, act_at(f"rest {d} 1"))
                dve.tensor_tensor(k_rest, k_rest, keys[:, d], ALU.mult)\
                   .then_inc(dve_done, dve_p.mark(f"k_rest {d}", f"state {d} 0"))
                for n in range(CHUNKS - 1):
                    c = n if d == 0 else CHUNKS - 1 - n
                    end = c * CHUNK + (CHUNK - 1 if d == 0 else 0)
                    bank = bank_v()
                    before = state0[:, d, :] if n == 0 else states[:, n % 4, :]
                    if n >= 3:
                        dve.wait_ge(pe_done, pe_at(f"o {d} {n - 3}"))
                    elif d and n == 0:
                        dve.wait_ge(pe_done, pe_at(f"o 0 {CHUNKS - 1}"))
                    dve.wait_ge(pe_done, pe_at(f"grown {d} {n}"))
                    for h in range(HEADS2):
                        cols = slice(h * P, (h + 1) * P)
                        last = dve.scalar_tensor_tensor(states[:, (n + 1) % 4, cols], before[:, cols],
                                                        e_cum[:, h, end:end + 1], bank[:, cols], ALU.mult, ALU.add)
                    last.then_inc(dve_done, dve_p.mark(f"grown {d} {n}", f"state {d} {n + 1}"))
                    dve.wait_ge(dve_done, dve_at(f"state {d} {n + 1}"))

            dve.wait_ge(act_done, act_at("o_sq 1"))
            dve.tensor_reduce(o_sum, o_sq.rearrange("p s (h v) -> p (s h) v", h=HEADS2), AX_X, ALU.add)\
               .then_inc(dve_done, dve_p.mark("o sums"))
            dve.wait_ge(act_done, act_at("o root"))
            then(dve.reciprocal(o_inv, o_root), "o inv")
            for half in range(TH):
                inv = o_inv[:, half * HEADS2:(half + 1) * HEADS2].unsqueeze(2).broadcast_to([P, HEADS2, P])
                dve.tensor_tensor(o_tok[:, half, :].rearrange("p (h v) -> p h v", h=HEADS2),
                                  banks[4 + half][:].rearrange("p (h v) -> p h v", h=HEADS2), inv, ALU.mult)\
                   .then_inc(dve_done, dve_p.mark(f"o_tok {half}"))
            for half in range(TH):
                bank = bank_v()[:].rearrange("p (h t) -> p h t", h=HEADS2)
                dve.wait_ge(pe_done, pe_at(f"y_a {half}"))
                dve.scalar_tensor_tensor(y_a[:, :, row_of(half)], bank, par2[:, R_HGN:R_HGN + 1],
                                         g_hg[:, :, row_of(half)], ALU.mult, ALU.mult)\
                   .then_inc(dve_done, dve_p.mark(f"y_a {half}"))

            for j in range(4):
                bank = two(bank_v())
                dve.wait_ge(act_done, act_at(f"gates2 {j}"))
                dve.wait_ge(pe_done, pe_at(f"pa {j}"))
                dve.tensor_tensor(merged2[:, 2 * j:2 * j + 2, :], bank, gates2[:, 2 * j:2 * j + 2, :], ALU.mult)\
                   .then_inc(dve_done, dve_p.mark(f"pa {j}"))
            for j in range(4):
                bank = two(bank_v())
                dve.wait_ge(act_done, act_at(f"gates2 {4 + j}"))
                dve.wait_ge(pe_done, pe_at(f"pb {j}"))
                then(dve.tensor_tensor(part2, bank, gates2[:, 8 + 2 * j:8 + 2 * j + 2, :], ALU.mult), f"pb {j} gated")
                then(dve.tensor_tensor(merged2[:, 2 * j:2 * j + 2, :], merged2[:, 2 * j:2 * j + 2, :], part2, ALU.add),
                     f"pb {j}")

            def add_gated(j, bank, gate):
                for c in range(2):
                    n = 2 * j + c
                    last = dve.scalar_tensor_tensor(h3[:, n, :], bank[:, c, :], ada[:, gate * DC + n, 0:1], h3[:, n, :],
                                                    ALU.mult, ALU.add)
                return last

            for j in range(4):
                bank = two(bank_v())
                dve.wait_ge(pe_done, pe_at(f"mix2 {j}"))
                add_gated(j, bank, 2).then_inc(dve_done, dve_p.mark(f"mix2 {j}"))
            scaled("m norm", "h2", h3, hn3, gain_2, lambda c: ada[:, 3 * DC + c, 0:1])

            bank = bank_v()[:, 0:TH * ROUTES].rearrange("p (h r) -> p h r", h=TH)
            dve.wait_ge(pe_done, pe_at("logits2"))
            bias = par2[:, R_RBIAS:R_RBIAS + ROUTES].unsqueeze(1).broadcast_to([P, TH, ROUTES])
            dve.memset(g_padded, MASKED)
            then(dve.tensor_tensor(logits2, bank, bias, ALU.add), "logits2")
            then(dve.tensor_copy(g_padded[:, :, 0:GROUPS], logits2[:, :, 0:GROUPS]), "g_padded")
            dve.tensor_reduce(g_max, logits2[:, :, 0:GROUPS], AX_X, ALU.max, negate=True)\
               .then_inc(dve_done, dve_p.mark("group max"))
            for half in range(TH):
                last = dve.max(g_top[:, half, :], g_padded[:, half, :])
            then(last, "group top")
            for half in range(TH):
                last = dve.max_index(g_at[:, half, :], g_top[:, half, :], g_padded[:, half, :])
            then(last, "group at")
            then(dve.tensor_copy(g_index, g_at[:, :, 0]), "group index")
            count = cst[:, C_IOTA:C_IOTA + TOP8]
            for half in range(TH):
                last = dve.tensor_scalar(in_group[:, half, :], count[:, 0:GROUPS], g_index[:, half:half + 1], None,
                                         ALU.is_equal)
            then(last, "in group")
            wide = [P, GROUPS, TOP8]
            for half in range(TH):
                last = dve.tensor_tensor(e_masked[:, half], logits2[:, half, GROUPS:].rearrange("p (g e) -> p g e", g=GROUPS),
                                         in_group[:, half, :].unsqueeze(2).broadcast_to(wide), ALU.mult)
            then(last, "e masked")
            for half in range(TH):
                last = dve.tensor_reduce(e_logits[:, half, :], e_masked[:, half].rearrange("p g e -> p e g"), AX_X, ALU.add)
            then(last, "e logits")
            for half in range(TH):
                last = dve.max(e_top[:, half, :], e_logits[:, half, :])
            then(last, "e top")
            for half in range(TH):
                last = dve.max_index(e_at[:, half, :], e_top[:, half, :], e_logits[:, half, :])
            dve.tensor_tensor(e_diff, e_top[:, :, 1], e_top[:, :, 0], ALU.subtract)\
               .then_inc(dve_done, dve_p.mark("second less first"))
            dve.wait_ge(dve_done, dve_at("second less first"))
            then(dve.tensor_copy(e_index, e_at[:, :, 0:2]), "e index")
            dve.wait_ge(act_done, act_at("second"))
            then(dve.tensor_scalar(e_weight[:, :, 0], e_second, 1.0, None, ALU.add), "weights 1")
            then(dve.tensor_tensor(e_weight[:, :, 0], e_weight[:, :, 0], g_sum, ALU.mult), "weights 2")
            then(dve.reciprocal(e_weight[:, :, 0], e_weight[:, :, 0]), "weights 3")
            then(dve.tensor_tensor(e_weight[:, :, 1], e_weight[:, :, 0], e_second, ALU.mult), "weights")
            for half in range(TH):
                for n in range(2):
                    is_it = e_index[:, half, n:n + 1]
                    dve.tensor_scalar(e_hot[:, n, half, :], count, is_it, None, ALU.is_equal)
                    last = dve.tensor_scalar(e_part[:, n, half, :], count, is_it, e_weight[:, half, n:n + 1],
                                             ALU.is_equal, ALU.mult)
            then(last, "e parts")
            dve.tensor_tensor(e_hot[:, 0], e_hot[:, 0], e_hot[:, 1], ALU.add)
            then(dve.tensor_tensor(e_part[:, 0], e_part[:, 0], e_part[:, 1], ALU.add), "e both")
            for half in range(TH):
                for dst, src in ((weights, e_part), (chosen, e_hot)):
                    last = dve.tensor_tensor(dst[:, half, :].rearrange("p (g e) -> p g e", g=GROUPS),
                                             in_group[:, half, :].unsqueeze(2).broadcast_to(wide),
                                             src[:, 0, half, :].unsqueeze(1).broadcast_to(wide), ALU.mult)
            then(last, "chosen")
            bank = bank_v()
            dve.wait_ge(pe_done, pe_at("rank"))
            then(dve.scalar_tensor_tensor(rank, bank[:, 0:TH * EXPERTS2].rearrange("p (h e) -> p h e", h=TH), 1.0, chosen,
                                          ALU.add, ALU.mult), "rank 1")
            then(dve.tensor_reduce(fullest, bank[:, TH * EXPERTS2:(TH + 1) * EXPERTS2], AX_X, ALU.max), "fullest")
            dve.tensor_scalar(rank, rank, -1.0, None, ALU.add).then_inc(dve_done, dve_p.mark("rank"))
            then(dve.tensor_scalar(lots, count, float(SLOTS), fullest, ALU.mult, ALU.is_lt), "lots")
            then(dve.tensor_reduce(lots_sum, lots, AX_X, ALU.add), "lots sum")
            then(dve.tensor_copy(n_passes[:], lots_sum), "passes")

            passes = dve.value_load(n_passes[0:1, 0:1], min_val=1, max_val=S // SLOTS)
            dve_p.enter("pass")
            with dve.Fori(0, passes) as p:
                loops["pass"] = p
                dve.wait_ge(pe_done, pe_at("tile2 back3", loops, **{"pass": 1}))
                wide = [P, EXPERTS2, SLOTS]
                for half in range(TH):
                    last = dve.tensor_tensor(pick2[:, half, :].rearrange("p (e s) -> p e s", e=EXPERTS2),
                                             rank[:, half, :].unsqueeze(2).broadcast_to(wide),
                                             cst[:, C_IOTA:C_IOTA + SLOTS].unsqueeze(1).broadcast_to(wide), ALU.is_equal)
                then(last, "picked2")
                for half in range(TH):
                    last = dve.tensor_tensor(weighed[:, half, :].rearrange("p (e s) -> p e s", e=EXPERTS2),
                                             pick2[:, half, :].rearrange("p (e s) -> p e s", e=EXPERTS2),
                                             weights[:, half, :].unsqueeze(2).broadcast_to(wide), ALU.mult)
                then(last, "weighed")
                then(dve.tensor_scalar(rank, rank, -float(SLOTS), None, ALU.add), "rank next")
                dve.sem_inc(waited, 1)
                ring_v[0] = 0
                dve_p.enter("tile2")
                with dve.Fori(0, TILES2) as t:
                    loops["tile2"] = t
                    expert_tile("tile2", FE2, lambda j, back: add_gated(j, back, 5))
                dve_p.leave(TILES2)
                del loops["tile2"]
            dve_p.leave_counted()
            loops["pass"] = passes
            one_back = {"pass": 1}
            dve.wait_ge(act_done, act_at("l norm root", loops, **one_back))
            dve.reciprocal(rms_inv, rms_root).then_inc(dve_done, dve_p.mark("l norm inv"))
            dve.wait_ge(dve_done, dve_at("l norm inv", loops, **one_back))
            for c in range(DC):
                last = dve.scalar_tensor_tensor(hn3[:, c, :], h3[:, c, :], par2[:, R_FINAL2 + c:R_FINAL2 + c + 1],
                                                rms_inv, ALU.mult, ALU.mult)
            last.then_inc(dve_done, dve_p.mark("out"))

        @block.sync
        def _(sp):
            loops = {}
            sp.dma_start(cst[:], io["consts"]).then_inc(consts_loaded, 16)
            sp.dma_start(h3, io["xT"].rearrange("(c p) t -> p c t", p=P)).then_inc(consts_loaded, 16)

            def load(i, dst, src):
                sp.dma_start(dst, src).then_inc(unit_loaded[i % RING], 16)

            def load_cols(i, src, c0, cols=512):
                dst = slot(i)[:, 0:src.shape[0] // P * cols].rearrange("p (k n) -> p k n", n=cols)
                load(i, dst, src[:, c0:c0 + cols].rearrange("(k p) n -> p k n", p=P))

            def load_expert_unit(i, u, gate, up, down, t, f_width):
                per_unit = 2 // (f_width // 512)
                n_in = DC // per_unit
                if u < 2 * n_in:
                    c = (u % n_in) * per_unit
                    src = gate if u < n_in else up
                    src = src[bass.ds(t * TILE_E, TILE_E), :, :]
                    if per_unit == 1:
                        src = src[:, c * P:(c + 1) * P, :].rearrange("e p f -> p e f")
                    else:
                        src = src.rearrange("e (p c) f -> p e (c f)", c=DC)[:, :, c * f_width:(c + per_unit) * f_width]
                    load(i, slot(i).rearrange("p (e x) -> p e x", e=TILE_E), src)
                else:
                    f = u - 2 * n_in
                    src = down[bass.ds(t * TILE_E, TILE_E), f * P:(f + 1) * P, :]
                    load(i, slot(i).rearrange("p (e d) -> p e d", e=TILE_E), src.rearrange("e p d -> p e d"))

            with sp.Fori(0, LAYERS) as layer:
                loops["layer"] = layer
                sp.wait_ge(dve_done, dve_at("spread", loops, layer=1))
                sp.wait_ge(pe_done, pe_at("router", loops, layer=1))
                sp.sem_inc(waited, 1)
                sp.dma_start(par[:], io["params"][layer]).then_inc(params_loaded, 16)
                w_in = io["w_in"][layer]
                q_w = 3 * DIL_QKV
                kv_w = q_w + WIN_HEADS * HD
                gate_w = kv_w + 2 * WIN_KV * HD
                starts = [0, 512, 1024, 2 * DIL_QKV, 2 * DIL_QKV + 512, q_w, q_w + 512, kv_w] + \
                    [gate_w + 512 * n for n in range(4)]
                for i in range(UNITS1_HEAD):
                    if i < RING:
                        last = UNITS1_TILE - RING + i
                        sp.wait_ge(pe_done, pe_at(f"tile unit {last}", loops, layer=1))
                    else:
                        sp.wait_ge(pe_done, pe_at(f"unit {i - RING}", loops))
                    sp.sem_inc(waited, 1)
                    if i < 12:
                        load_cols(i, w_in, starts[i], 256 if i == 4 else 512)
                    elif i < 14:
                        load_cols(i, io["w_branch_a"][layer][(i - 12) * P:(i - 11) * P, :], 0, D)
                    elif i < 16:
                        load_cols(i, io["w_branch_b"][layer], 512 * (i - 14))
                    else:
                        load_cols(i, io["w_out"][layer], 512 * (i - 16))
                experts = [io[n][layer] for n in ("w_expert_gate", "w_expert_up", "w_expert_down")]
                for u in range(RING):
                    sp.wait_ge(pe_done, pe_at(f"unit {UNITS1_HEAD - RING + u}", loops))
                    sp.sem_inc(waited, 1)
                    load_expert_unit(u, u, *experts, 0, FE)

                def rest_of_tile(t):
                    for u in range(RING, UNITS1_TILE):
                        sp.wait_ge(pe_done, pe_at(f"tile unit {u - RING}", loops | {"tile": t}))
                        sp.sem_inc(waited, 1)
                        load_expert_unit(u, u, *experts, t, FE)

                with sp.Fori(0, TILES1 - 1) as t:
                    rest_of_tile(t)
                    for u in range(RING):
                        sp.wait_ge(pe_done, pe_at(f"tile unit {UNITS1_TILE - RING + u}", loops | {"tile": t}))
                        sp.sem_inc(waited, 1)
                        load_expert_unit(u, u, *experts, t + 1, FE)
                rest_of_tile(TILES1 - 1)
            del loops["layer"]
            sp.wait_ge(dve_done, dve_at("spread"))
            sp.wait_ge(pe_done, pe_at("slot cols"))
            sp.dma_start(cst2, io["consts_2"]).then_inc(consts2_loaded, 16)
            sp.dma_start(par2, io["params_2"]).then_inc(consts2_loaded, 16)
            sp.dma_start(hcT, io["ctxT"].rearrange("(c p) t -> p c t", p=P)).then_inc(consts2_loaded, 16)
            for i in range(RING):
                sp.wait_ge(pe_done, pe_at(f"tile unit {UNITS1_TILE - RING + i}"))
                load_cols(i, io["ada_w_2"], 512 * i)
            sp.wait_ge(dve_done, dve_at("tile add3"))
            sp.dma_start(lb_raw, io["hgrn_lb_2"].partition_broadcast(P)).then_inc(inputs2_loaded, 16)
            sp.dma_start(posT, io["posT"].rearrange("(c p) t -> p c t", p=P)).then_inc(inputs2_loaded, 16)
            w_in = io["w_in_2"]
            hy0 = 3 * KD + 2 * KD
            starts = [hy0 + 512 * n for n in range(3)] + [KD, 2 * KD, 3 * KD, 0, 3 * KD + KD] + \
                [hy0 + 3 * HY + 512 * n for n in range(4)]
            for i in range(RING, UNITS2_HEAD):
                sp.wait_ge(pe_done, pe_at(f"unit2 {i - RING}"))
                if i < 12:
                    load_cols(i, io["ada_w_2"], 512 * i)
                elif i < 24:
                    load_cols(i, w_in, starts[i - 12])
                elif i < 28:
                    src = io["w_proj_a_2"] if i < 26 else io["w_proj_b_2"]
                    load_cols(i, src[(i % 2) * 2 * P:(i % 2 + 1) * 2 * P, :], 0, D)
                else:
                    load_cols(i, io["w_out_2"], 512 * (i - 28))
            experts = [io[n] for n in ("moe_w_gate_2", "moe_w_up_2", "moe_w_down_2")]
            for u in range(RING):
                sp.wait_ge(pe_done, pe_at(f"unit2 {UNITS2_HEAD - RING + u}"))
                load_expert_unit(u, u, *experts, 0, FE2)

            def rest_of_tile2(t):
                for u in range(RING, UNITS2_TILE):
                    sp.wait_ge(pe_done, pe_at(f"tile2 unit {u - RING}", loops | {"tile2": t}))
                    sp.sem_inc(waited, 1)
                    load_expert_unit(u, u, *experts, t, FE2)

            def tiles2():
                with sp.Fori(0, TILES2 - 1) as t:
                    rest_of_tile2(t)
                    for u in range(RING):
                        sp.wait_ge(pe_done, pe_at(f"tile2 unit {UNITS2_TILE - RING + u}", loops | {"tile2": t}))
                        sp.sem_inc(waited, 1)
                        load_expert_unit(u, u, *experts, t + 1, FE2)
                rest_of_tile2(TILES2 - 1)

            loops["pass"] = 0
            tiles2()
            sp.wait_ge(dve_done, dve_at("passes"))
            passes = sp.value_load(n_passes[0:1, 0:1], min_val=1, max_val=S // SLOTS)
            with sp.If(passes > 1):
                with sp.Fori(1, passes) as p:
                    loops["pass"] = p
                    for u in range(RING):
                        sp.wait_ge(pe_done, pe_at(f"tile2 unit {UNITS2_TILE - RING + u}", loops, **{"pass": 1}))
                        sp.sem_inc(waited, 1)
                        load_expert_unit(u, u, *experts, 0, FE2)
                    tiles2()
            sp.wait_ge(dve_done, dve_at("out", {"pass": passes}, **{"pass": 1}))
            sp.dma_start(io["outT"].rearrange("(c p) t -> p c t", p=P), hn3).then_inc(stored, 16)
            sp.wait_ge(stored, 16)
    return {"pe": pe_p.new, "act": act_p.new, "dve": dve_p.new}


def kernel(**inputs):
    import concourse.bacc as bacc
    from concourse.bass_utils import run_bass_kernel_spmd

    a = {name: np.asarray(value) for name, value in inputs.items()}

    def columns(v):
        return np.ascontiguousarray(v.reshape(-1, P).T)

    def on_all(v):
        return np.broadcast_to(v.reshape(1, -1), (P, v.size))

    def rows(v):
        out = np.zeros((P, v.shape[1]), np.float32)
        out[:v.shape[0]] = v
        return out

    params = np.stack([np.concatenate([
        columns(a["norm_mix"][l]), columns(a["norm_ffn"][l]), columns(a["b_gate"][l]), on_all(a["sink_logit"][l]),
        a["w_router"][l].reshape(DC, P, EXPERTS).transpose(1, 0, 2).reshape(P, DC * EXPERTS)], axis=1)
        for l in range(LAYERS)])
    router_2 = np.concatenate([a["moe_router_g_w_2"][0],
                               a["moe_router_e_w_2"][0].transpose(1, 0, 2).reshape(D, EXPERTS2)], axis=1)
    params_2 = np.concatenate([
        columns(a["norm_final"]), columns(a["final_norm_g_2"]), columns(a["norm1_g_2"]), columns(a["norm2_g_2"]),
        columns(a["ada_b_2"]), columns(a["c_2"]), columns(a["c_ctx_2"]), columns(a["hgrn_norm_g_2"]),
        columns(a["hy_conv_w_2"]), columns(a["hy_conv_b_2"]), columns(a["hy_d_2"]),
        router_2.reshape(DC, P, ROUTES).transpose(1, 0, 2).reshape(P, DC * ROUTES),
        on_all(np.concatenate([a["moe_router_g_b_2"][0], a["moe_router_e_b_2"][0].reshape(-1)])),
        rows(a["hy_filt_w1_2"][0]), rows(a["hy_filt_w2_2"][0]), rows(a["hy_filt_w3_2"][0]),
        rows(a["hy_filt_b1_2"].T), rows(a["hy_filt_freq1_2"].T), rows(a["hy_filt_b2_2"].T),
        rows(a["hy_filt_freq2_2"].T)], axis=1)
    arrays = {
        "consts": constants(), "consts_2": constants_2(), "posT": positions(),
        "xT": a["x"][0].T, "ctxT": a["ctx_2"][0].T, "params": params, "params_2": params_2,
        "hgrn_lb_2": a["hgrn_lb_2"],
    }
    for name in ("w_in", "w_branch_a", "w_branch_b", "w_out", "w_expert_gate", "w_expert_up", "w_expert_down"):
        arrays[name] = a[name]
    for name in ("ada_w_2", "w_in_2", "w_proj_a_2", "w_proj_b_2", "w_out_2"):
        arrays[name] = a[name][0]
    for name in ("moe_w_gate_2", "moe_w_up_2", "moe_w_down_2"):
        arrays[name] = a[name].reshape(EXPERTS2, *a[name].shape[3:])
    arrays = {name: np.ascontiguousarray(value) for name, value in arrays.items()}

    def program(tables):
        nc = bacc.Bacc("TRN2", target_bir_lowering=False, num_devices=1, dynamic_dma_scratch_size=1024)
        io = {name: nc.dram_tensor(name, list(value.shape), F32, kind="ExternalInput").ap()
              for name, value in arrays.items()}
        io["outT"] = nc.dram_tensor("outT", [D, S], F32, kind="ExternalOutput").ap()
        return nc, build(nc, io, tables)

    _, counts = program({})
    nc, _ = program(counts)
    result = run_bass_kernel_spmd(nc, [arrays], core_ids=[0])
    return np.ascontiguousarray(result.results[0]["outT"].T).reshape(1, S, D)
```

```python
from contextlib import ExitStack

import concourse.bass as bass
import numpy as np
from concourse import mybir

F32 = mybir.dt.float32
F32R = mybir.dt.float32r
U32 = mybir.dt.uint32
I32 = mybir.dt.int32
ALU = mybir.AluOpType
ACT = mybir.ActivationFunctionType
AX_X = mybir.AxisListType.X

P = 128
D = 1024
DC = D // P
S = 256
TH = S // P
LAYERS = 2
HD = 64
DIL_SLOTS = 4
DIL_GROUPS = 3
DIL_QKV = DIL_SLOTS * DIL_GROUPS * HD
DIL_STEP = (1, 4, 16)
DIL_REACH = (64, 256, 1024)
WIN_HEADS = 16
WIN_KV = 4
WIN_REACH = 128
IN1 = 3 * DIL_QKV + WIN_HEADS * HD + 2 * WIN_KV * HD + 2 * D
EXPERTS = 16
CAP = 2 * S // EXPERTS
FE = 1024
EPS = 1e-6
MASKED = -1e30

TILE_E = 4
SLOTS = P // TILE_E
TILES1 = EXPERTS // TILE_E

RING = 6
UNIT = 4096
ADA_UNITS = 6
UNITS1_HEAD = 18 + ADA_UNITS
UNITS1_TILE = 24
UNITS1 = UNITS1_HEAD + TILES1 * UNITS1_TILE

HY = 512
HY_EMB, HY_HID = 33, 64
KD = 512
HEADS2 = KD // P
CHUNK = 32
CHUNKS = S // CHUNK
GRID = 64
GROUPS, TOP8 = 4, 8
EXPERTS2 = GROUPS * TOP8
ROUTES = GROUPS + EXPERTS2
FE2 = 512
TILES2 = EXPERTS2 // TILE_E
UNITS_L = LAYERS * UNITS1
UNITS2_HEAD = 18
HEAD_SLOTS = 3
UNITS2_TILE = 12
TURN = 2 * np.pi
TURN_PIECES = (6.28125, 0.0019350051879882812, 3.019916050561733e-07)
ROUNDER = 1.5 * 2.0 ** 23
HALF_TURN = 3.1415925
ARENA = 24848
ROOM = 13355
JOB = 256
IN_JOBS = [(n // 2, n % 2 * JOB, f"qk_dil {n}", "width", "act" if n < 3 else "dve") for n in range(6)] + \
    [(3 + n // 2, n % 2 * JOB, f"v_dil {n}", "token", "act") for n in range(3)] + \
    [(5 + n // 2, n % 2 * JOB, f"q_win {n}", "width", "act") for n in range(4)] + \
    [(7, 0, "k_win", "width", "dve"), (7, JOB, "v_win", "token", "act")]
GATE_BUFS = 3
GATE_JOBS = [(8 + n // 4, n % 4 * P, f"gate {n}") for n in range(2 * DC)]
OUT_JOBS = [(14 + n // 2, n % 2 * JOB, f"yb {n}", "width", "dve") for n in range(4)] + \
    [(16 + n // 2, n % 2 * JOB, f"mix {n}", "width", "dve") for n in range(4)]
JOBS = IN_JOBS + OUT_JOBS
JOBS2 = [(n // 2, n % 2 * JOB, f"hy {n}", DC) for n in range(6)] + \
    [(3 + n // 2, n % 2 * JOB, f"gates2 {n}", DC) for n in range(8)] + \
    [(7 + n // 2, n % 2 * JOB, f"z {n // 2} {n % 2}", DC) for n in range(6)] + \
    [(10 + n // 2, n % 2 * JOB, f"qg {n}", DC) for n in range(4)] + \
    [(12 + n // 2, n % 2 * JOB, f"pb {n}", KD // P) for n in range(4)] + \
    [(14 + n // 2, n % 2 * JOB, f"pa {n}", KD // P) for n in range(4)] + \
    [(16 + n // 2, n % 2 * JOB, f"mix2 {n}", DC) for n in range(4)]
HY0, GATE0, Z0, QG0, PB0, PA0, MIX0 = 0, 6, 14, 20, 24, 28, 32


def slopes(n):
    return [2.0 ** (-8.0 * (i + 1) / n) for i in range(n)]


class Progress:

    def __init__(self, table):
        self.table, self.new = table, {}
        self.n, self.open = 0, []

    def mark(self, *steps):
        self.n += 1
        for step in steps:
            self.new[step] = (self.n, tuple(s for s, _ in self.open))
        return 1

    def enter(self, scope):
        self.open.append((scope, self.n))

    def leave(self, rounds):
        scope, start = self.open.pop()
        self.new[("per", scope)] = (self.n - start, rounds)
        self.n = start + (self.n - start) * rounds

    def leave_counted(self):
        scope, start = self.open[-1]
        self.new[("per", scope)] = (self.n - start, 1)

    @property
    def credit(self):
        return self.table.get(("per", "layer"), (1, 1))[0]

    def at(self, step, loops=None, **back):
        loops = loops or {}
        n, scopes = self.table.get(step, (1, ()))
        value = n + self.credit
        moving = []
        for scope in scopes:
            per, rounds = self.table.get(("per", scope), (1, 1))
            value -= back.get(scope, 0) * per
            round_ = loops.get(scope, rounds - 1)
            if isinstance(round_, int):
                value += round_ * per
            else:
                moving.append(round_ * per)
        for term in moving:
            value = term + value
        return value


C_IDENT, C_ONES = 0, P
C_IOTA = 2 * P
C_TOK = C_IOTA + S
C_EPS = C_TOK + TH
C_DIST = C_EPS + 1
C_COLS = C_DIST + 4 * TH * S
WIN_TABLE = 3


def constants():
    c = np.zeros((P, C_COLS), np.float32)
    c[:, C_IDENT:C_IDENT + P] = np.eye(P)
    c[:, C_ONES:C_ONES + P] = 1.0
    i = np.arange(S)
    dist = np.abs(i[:, None] - i[None, :])
    reach = [(r, m) for r, m in zip(DIL_STEP, DIL_REACH)] + [(1, WIN_REACH)]
    for n, (step, far) in enumerate(reach):
        table = np.where((dist <= far) & (dist % step == 0), -dist.astype(np.float32), np.float32(MASKED))
        c[:, C_DIST + n * TH * S:C_DIST + (n + 1) * TH * S] = (
            table.reshape(TH, P, S).transpose(1, 0, 2).reshape(P, TH * S))
    c[:, C_IOTA:C_IOTA + S] = i
    c[:, C_TOK:C_TOK + TH] = i.reshape(TH, P).T
    c[:, C_EPS] = EPS
    return c


Q_NORM1, Q_NORM2 = 0, DC
Q_BGATE = 2 * DC
Q_SINK = Q_BGATE + 2 * DC
Q_ROUTER = Q_SINK + WIN_HEADS
Q_C = Q_ROUTER + DC * EXPERTS
Q_COLS = Q_C + 2 * DC


B_CTX = 0
B_SCAN = B_CTX + 2 * P
B_DFT = B_SCAN + 2 * 4 * P
B_IDFT = B_DFT + TH * 2 * S
B_DECAY = B_IDFT + 4 * S
B_POS = B_DECAY + TH * HY
B_COLS = B_POS + S


def constants_2():
    f4 = np.float32
    c = np.zeros((P, B_COLS), np.float32)
    i = np.arange(P)
    of, to = i[:, None], i[None, :]
    c[:, B_CTX:B_CTX + P] = of > to
    c[:, B_CTX + P:B_CTX + 2 * P] = of < to
    together = of // CHUNK == to // CHUNK
    start = to // CHUNK * CHUNK
    for d in range(2):
        before = of <= to if d == 0 else of >= to
        middle = start + CHUNK // 2 - d
        reach = of <= middle if d == 0 else of >= middle
        left = of > to if d == 0 else of < to
        tables = (together & before, together * (before.astype(f4) - reach.astype(f4)), together & left,
                  together & before)
        for n, table in enumerate(tables):
            at = B_SCAN + (d * 4 + n) * P
            c[:, at:at + P] = table
    t, f = np.arange(S, dtype=np.float64), np.arange(S, dtype=np.float64)
    angle = 2 * np.pi * np.outer(t, f) / (2 * S)
    cos, sin = np.cos(angle), np.sin(angle)
    sin[:, 0] = (-1.0) ** t
    for half in range(TH):
        at = B_DFT + half * 2 * S
        rows = slice(half * P, (half + 1) * P)
        c[:, at:at + S], c[:, at + S:at + 2 * S] = cos[rows], sin[rows]
    scale = np.where(f == 0, 1.0, 2.0)[:, None] / (2 * S)
    for n, wave in enumerate((cos.T, sin.T)):
        for chunk in range(2):
            at = B_IDFT + (n * 2 + chunk) * S
            c[:, at:at + S] = (wave * scale)[chunk * P:(chunk + 1) * P]
    along = np.linspace(0, 1, S, dtype=f4)[:, None]
    deltas = np.abs(np.linspace(np.log(1e-2) / 1.5, np.log(1e-2) / 0.3, HY, dtype=f4))
    decay = np.exp(-along * deltas)
    for half in range(TH):
        c[:, B_DECAY + half * HY:B_DECAY + (half + 1) * HY] = decay[half * P:(half + 1) * P]
    bands = (HY_EMB - 1) // 2
    turns = (f4(2 * np.pi) * np.arange(S, dtype=f4) / f4(S))[:, None] * np.linspace(1e-4, bands - 1, bands, dtype=f4)
    c[0:HY_EMB, B_POS:B_POS + S] = np.concatenate([along, np.cos(turns), -np.sin(turns)], axis=1).T
    return c


def positions():
    quarter = D // 4
    omega = (1.0 / 10000.0 ** (np.arange(quarter, dtype=np.float32) / np.float32(quarter))).astype(np.float32)
    token = np.arange(S)
    parts = []
    for pos in (token // GRID, token % GRID):
        a = pos.astype(np.float32)[:, None] * omega
        parts += [np.sin(a), np.cos(a)]
    return np.ascontiguousarray(np.concatenate(parts, axis=1).T.astype(np.float32))


R_FINAL1, R_FINAL2, R_NORM1, R_NORM2 = 0, DC, 2 * DC, 3 * DC
R_ADA = 4 * DC
R_HGN = R_ADA + 6 * DC
R_CONV = R_HGN + 1
R_CONVB = R_CONV + 3 * 3 * HY // P
R_SKIP = R_CONVB + 3 * HY // P
R_ROUTER = R_SKIP + HY // P
R_RBIAS = R_ROUTER + DC * ROUTES
R_W1 = R_RBIAS + ROUTES
R_W2 = R_W1 + HY_HID
R_W3 = R_W2 + HY_HID
R_B1 = R_W3 + 2 * HY
R_FR1, R_B2, R_FR2 = R_B1 + 1, R_B1 + 2, R_B1 + 3
R_COLS = R_B1 + 4


def build(nc, io, tables):
    pe_p, act_p, dve_p = (Progress(tables.get(n, {})) for n in ("pe", "act", "dve"))
    pe_at, act_at, dve_at = pe_p.at, act_p.at, dve_p.at
    with ExitStack() as ctx:
        def sb(name, cols, dt=F32, rows=P):
            return ctx.enter_context(nc.sbuf_tensor(name, [rows, cols], dt))

        def sem(name):
            return ctx.enter_context(nc.semaphore(name))

        with ExitStack() as first_view:
            ring = [first_view.enter_context(nc.sbuf_tensor(f"ring{i}", [P, UNIT], F32)) for i in range(RING)]
            arena = first_view.enter_context(nc.sbuf_tensor("arena", [P, ARENA], F32))
            hnT = first_view.enter_context(nc.sbuf_tensor("hnT", [P, DC * S], F32))
        ring_parts = [sb(f"ring_parts{i}", UNIT, F32R) for i in range(RING)]
        arena_parts = sb("arena_parts", ARENA, F32R)
        hnT_parts = sb("hnT_parts", DC * S, F32R)
        hT = sb("hT", DC * S)
        cst = sb("cst", C_COLS)
        par = sb("par", Q_COLS)
        rms = sb("rms", 2 * S)
        small = sb("small", 208)
        picks = sb("picks", CAP, U32, rows=EXPERTS)
        n_passes = sb("n_passes", 1, I32)
        banks = [ctx.enter_context(nc.psum_tensor(f"bank{i}", [P, 512], F32)) for i in range(8)]

        h3 = hT[:].rearrange("p (c t) -> p c t", c=DC)
        hn3 = hnT[:].rearrange("p (c t) -> p c t", c=DC)
        hn_low = hnT_parts[:].rearrange("p (c t) -> p c t", c=DC)
        ident = cst[:, C_IDENT:C_IDENT + P]
        ones = cst[:, C_ONES:C_ONES + P]
        eps = cst[:, C_EPS:C_EPS + 1]
        rms_root, rms_inv = rms[:, 0:S], rms[:, S:2 * S]

        def dist(table, half):
            at = C_DIST + (table * TH + half) * S
            return cst[:, at:at + S]

        used = [0]

        def piece(cols, start=None):
            if start is not None:
                used[0] = start
            at = used[0]
            used[0] += cols
            assert used[0] <= ARENA
            return arena[:, at:at + cols]

        def parts(at, cols):
            return arena_parts[:, at:at + cols].rearrange("p (c t) -> p c t", t=S)

        q_dil = piece(6 * S, 0).rearrange("p (c t) -> p c t", c=6)
        k_dil = piece(12 * S).rearrange("p (c t) -> p c t", c=12)
        v_dil = piece(TH * DIL_QKV).rearrange("p (h c) -> p h c", h=TH)
        q_win_at = used[0]
        q_win = piece(8 * S).rearrange("p (c t) -> p c t", c=8)
        k_win = piece(8 * S).rearrange("p (c t) -> p c t", c=8)
        v_win = piece(TH * WIN_KV * HD).rearrange("p (h c) -> p h c", h=TH)
        gates = piece(16 * S).rearrange("p (c t) -> p c t", c=16)
        WCOLS = S + 1
        WBUFS = 3
        prob_at = used[0]
        prob = piece(WBUFS * 4 * WCOLS)
        prob_t = piece(2 * DIL_GROUPS * 512)
        prob_dil = prob[:, 0:2 * TH * DIL_GROUPS * S].rearrange("p (q h k) -> p q h k", q=TH, h=2)
        prob_win = prob[:, 0:WBUFS * 4 * WCOLS].rearrange("p (b q h k) -> p b q h k", b=WBUFS, q=TH, h=2)
        probT_dil = prob_t.rearrange("p (h g x) -> p h g x", h=2, g=DIL_GROUPS)
        probT_win = prob_t.rearrange("p (b h x) -> p b h x", b=WBUFS, h=2)
        w_high = [arena_parts[:, prob_at + 2048 + b * DC * JOB:prob_at + 2048 + (b + 1) * DC * JOB]
                  .rearrange("p (k n) -> p k n", k=DC) for b in range(2)]
        w_high_out = ring_parts[13 % RING][:, UNIT - DC * JOB:UNIT].rearrange("p (k n) -> p k n", k=DC)

        def high_room(i):
            return w_high_out if i == len(IN_JOBS) else w_high[i % 2]

        squares = prob[:, 0:2048].rearrange("p (c t) -> p c t", c=DC)
        o_dil = q_dil
        o_high, o_low = (parts(2 * S + n * DC * S, DC * S) for n in range(2))
        assert 2 * S + 2 * DC * S <= q_win_at
        merged = q_win
        merged_low = parts(q_win_at, DC * S)
        part = prob[:, 0:512]
        c_silu = piece(DC * 32).rearrange("p (k m) -> p k m", k=DC)
        hn_high = parts(used[0], DC * S)
        merged_high = hn_high
        piece(DC * S)
        gate_high = [ring_parts[12 % RING][:, UNIT - (b + 1) * DC * P:UNIT - b * DC * P]
                     .rearrange("p (k n) -> p k n", k=DC) for b in range(GATE_BUFS)]
        assert used[0] <= ARENA - 12 * P and D + GATE_BUFS * DC * P <= UNIT
        ada_rows = piece(12 * P, ARENA - 12 * P)
        hn_tok = piece(TH * D, 0).rearrange("p (h c) -> p h c", h=TH)
        pick = piece(TH * EXPERTS * SLOTS).rearrange("p (h s) -> p h s", h=TH)
        spread1 = piece(TILES1 * S).rearrange("p (g t) -> p g t", g=TILES1)
        x_slots = piece(DC * P).rearrange("p (c s) -> p c s", c=DC)
        silu_sb = piece(FE)
        hid = piece(FE)
        hidT = piece(FE).rearrange("p (f s) -> p f s", f=FE // P)
        y_sb = piece(D)
        idx_diag = piece(EXPERTS * CAP)
        gate_diag = piece(EXPERTS * CAP)
        aff_rows = piece(2 * S)
        topv = piece(CAP)
        idxf = piece(CAP)

        neg_max = small[:, 0:40]
        row_sum = small[:, 40:80]
        row_inv = small[:, 80:120]
        r_max = small[:, 120:122]
        r_sum = small[:, 122:124]
        r_inv = small[:, 124:126]
        r_exp = small[:, 128:160].rearrange("p (h e) -> p h e", h=TH)
        aff = small[:, 160:192].rearrange("p (h e) -> p h e", h=TH)
        slot_cols = small[:, 192:200]

        cst2 = piece(B_COLS, ROOM)
        par2 = piece(R_COLS)
        ada_flat = piece(48 * 2)
        ada = ada_flat.rearrange("p (n r) -> p n r", r=2)
        gain_x, gain_c, gain_2 = (piece(DC) for _ in range(3))
        hc_at = used[0]
        hc_flat = piece(DC * S)
        hcT = hc_flat.rearrange("p (c t) -> p c t", c=DC)
        bounds = piece(4 * KD)
        lower = bounds[:, 0:2 * KD].rearrange("p (d c) -> p d c", d=2)
        upper = bounds[:, 2 * KD:4 * KD].rearrange("p (d c) -> p d c", d=2)
        y_b_at = used[0]
        y_b = piece(4 * S).rearrange("p (c t) -> p c t", c=4)
        assert used[0] <= ARENA
        lb_raw = bounds.rearrange("p (a d c) -> p a d c", a=2, d=2)
        lb_part = arena[:, y_b_at:y_b_at + 2 * KD].rearrange("p (d c) -> p d c", d=2)
        w_high2 = [ring_parts[3][:, b * DC * JOB:(b + 1) * DC * JOB].rearrange("p (k n) -> p k n", k=DC) for b in range(2)]
        hx_high, hc_high = (ring_parts[4][:, n * DC * S:(n + 1) * DC * S].rearrange("p (c t) -> p c t", c=DC)
                            for n in range(2))
        y_b_high, y_a_high = (ring_parts[4][:, DC * S + n * 4 * S:DC * S + (n + 1) * 4 * S]
                              .rearrange("p (c t) -> p c t", c=4) for n in range(2))
        merged2 = ring[4][:, 0:DC * S].rearrange("p (c t) -> p c t", c=DC)
        merged2_low = ring_parts[4][:, 0:DC * S].rearrange("p (c t) -> p c t", c=DC)
        merged2_high = parts(8 * S, DC * S)
        gates2 = ring[5][:].rearrange("p (c t) -> p c t", c=16)
        hc_low, y_b_low = parts(hc_at, DC * S), parts(y_b_at, 4 * S)
        k_cos = piece(2 * HY, 0).rearrange("p (f c) -> p f c", f=2)
        k_sin = piece(2 * HY).rearrange("p (f c) -> p f c", f=2)
        k_nyq = piece(HY)
        taps_f, taps_b, taps_sum = (piece(2 * HY).rearrange("p (h c) -> p h c", h=TH) for _ in range(3))
        conv = piece(12 * S).rearrange("p (c t) -> p c t", c=12)
        squares_at = used[0]
        squares2_flat = piece(DC * S)
        squares2 = squares2_flat.rearrange("p (c t) -> p c t", c=DC)
        assert used[0] <= ROOM - DC * S
        posT = piece(DC * S, ROOM - DC * S).rearrange("p (c t) -> p c t", c=DC)
        f_arg, f_turns, f_sin = (piece(S, ROOM - (n + 1) * S) for n in range(3))
        u_tok, u_cos, u_sin = (piece(2 * HY, squares_at - 12 * S - (3 - n) * 2 * HY).rearrange("p (f c) -> p f c", f=2)
                               for n in range(3))
        prod_cos, prod_sin, prod_part = (piece(2 * HY, squares_at + n * 2 * HY).rearrange("p (f c) -> p f c", f=2)
                                         for n in range(3))
        q_hg = piece(4 * S, 0).rearrange("p (h t) -> p h t", h=HEADS2)
        g_hg = piece(4 * S).rearrange("p (h t) -> p h t", h=HEADS2)
        logf_flat = piece(4 * KD)
        keys_flat = piece(4 * KD)
        vals_flat = piece(2 * KD)
        state0 = piece(2 * KD).rearrange("p (d x) -> p d x", d=2)
        hg_work = used[0]
        logf_c_flat = piece(4 * KD)
        keys_c_flat = piece(4 * KD)
        vals_c_flat = piece(2 * KD)
        assert used[0] <= ROOM
        logf, keys, logf_c, keys_c = (x.rearrange("p (d s c) -> p d s c", d=2, s=TH)
                                      for x in (logf_flat, keys_flat, logf_c_flat, keys_c_flat))
        vals, vals_c = (x.rearrange("p (s c) -> p s c", s=TH) for x in (vals_flat, vals_c_flat))
        keys_decayed = hc_flat.rearrange("p (d s c) -> p d s c", d=2, s=TH)
        e_cum = bounds[:, 0:4 * S].rearrange("p (h t) -> p h t", h=HEADS2)
        q_cum = bounds[:, 4 * S:8 * S].rearrange("p (h t) -> p h t", h=HEADS2)
        k_rest = hc_flat[:, 0:2 * KD].rearrange("p (s c) -> p s c", s=TH)
        inner_flat = hc_flat[:, 2 * KD:4 * KD]
        inner = inner_flat.rearrange("p (s h t) -> p s h t", s=TH, h=HEADS2)
        q_mid = piece(4 * S, hg_work).rearrange("p (h t) -> p h t", h=HEADS2)
        k_mid = piece(4 * S).rearrange("p (h t) -> p h t", h=HEADS2)
        states = piece(4 * KD).rearrange("p (n x) -> p n x", n=4)
        o_tok = piece(2 * KD, hg_work).rearrange("p (s c) -> p s c", s=TH)
        y_a_low = parts(used[0], 4 * S)
        y_a = piece(4 * S).rearrange("p (h t) -> p h t", h=HEADS2)
        o_sq = piece(2 * KD).rearrange("p (s c) -> p s c", s=TH)
        part2 = piece(512).rearrange("p (c t) -> p c t", c=2)
        pick2 = piece(TH * TILES2 * P, 9216).rearrange("p (h s) -> p h s", h=TH)
        weighed = piece(TH * TILES2 * P).rearrange("p (h s) -> p h s", h=TH)
        spread2 = piece(TILES2 * S).rearrange("p (g t) -> p g t", g=TILES2)
        sq_moe = arena[:, 9216:9216 + DC * S].rearrange("p (c t) -> p c t", c=DC)
        routes = piece(1024)
        assert used[0] <= ROOM + B_COLS

        def direction(d):
            at = B_SCAN + d * 4 * P
            return cst2[:, at:at + 2 * P], cst2[:, at + 2 * P:at + 3 * P], cst2[:, at + 3 * P:at + 4 * P]
        routed = [0]

        def field(cols, pattern=None, **sizes):
            at = routed[0]
            routed[0] += cols
            assert routed[0] <= 1024
            out = routes[:, at:at + cols]
            return out.rearrange(pattern, **sizes) if pattern else out

        chosen, weights, rank = (field(TH * EXPERTS2, "p (h e) -> p h e", h=TH) for _ in range(3))
        logits2 = field(TH * ROUTES, "p (h r) -> p h r", h=TH)
        g_padded = field(TH * TOP8, "p (h e) -> p h e", h=TH)
        g_top = field(TH * TOP8, "p (h e) -> p h e", h=TH)
        g_at = field(TH * TOP8).bitcast(U32).rearrange("p (h e) -> p h e", h=TH)
        g_max, g_sum, g_index = (field(TH) for _ in range(3))
        g_exp = field(TH * GROUPS, "p (h g) -> p h g", h=TH)
        in_group = field(TH * GROUPS, "p (h g) -> p h g", h=TH)
        e_masked = field(TH * EXPERTS2, "p (h g e) -> p h g e", h=TH, g=GROUPS)
        e_logits = field(TH * TOP8, "p (h e) -> p h e", h=TH)
        e_top = field(TH * TOP8, "p (h e) -> p h e", h=TH)
        e_at = field(TH * TOP8).bitcast(U32).rearrange("p (h e) -> p h e", h=TH)
        e_index, e_weight = (field(TH * 2, "p (h n) -> p h n", h=TH) for _ in range(2))
        e_diff, e_second = (field(TH) for _ in range(2))
        e_hot, e_part = (field(2 * TH * TOP8, "p (n h e) -> p n h e", n=2, h=TH) for _ in range(2))
        fullest, lots_sum = field(1), field(1)
        lots = field(TOP8)
        o_sum, o_root, o_inv = small[:, 0:8], small[:, 8:16], small[:, 16:24]

        pe_done = sem("tensor_steps_done")
        act_done = sem("scalar_steps_done")
        dve_done = sem("vector_steps_done")
        unit_loaded = [sem(f"unit_loaded_{i}") for i in range(RING)]
        consts_loaded = sem("consts_loaded")
        dist_loaded = sem("distances_loaded")
        params_loaded = sem("params_loaded")
        consts2_loaded = sem("second_consts_loaded")
        inputs2_loaded = sem("second_inputs_loaded")
        stored = sem("output_stored")
        waited = sem("waited")

        block = ctx.enter_context(nc.Block())

        def slot(i):
            return ring[i % RING][:]

        def job_weights(job, of=ring):
            unit, c0 = job[0:2]
            cols = JOB if unit == 4 else 2 * JOB
            return of[unit % RING][:, 0:DC * cols].rearrange("p (k n) -> p k n", k=DC)[:, :, c0:c0 + JOB]

        def gate_weights(n, of=ring):
            unit, c0 = GATE_JOBS[n][0:2]
            return of[unit % RING][:].rearrange("p (k n) -> p k n", k=DC)[:, :, c0:c0 + P]

        def job2_weights(i, of=ring):
            unit, c0, _, chunks_ = JOBS2[i]
            cols = chunks_ * 2 * JOB
            return of[unit % HEAD_SLOTS][:, 0:cols].rearrange("p (k n) -> p k n", k=chunks_)[:, :, c0:c0 + JOB]

        @block.tensor
        def _(pe):
            loops = {}
            taken = {}

            def take(bank, engine, reader):
                if bank in taken:
                    done, at, step = taken[bank]
                    pe.wait_ge(done, at(step, loops))
                taken[bank] = (act_done, act_at, reader) if engine == "act" else (dve_done, dve_at, reader)
                return banks[bank]

            ring_a, ring_v = [0], [0]

            def to_act(reader):
                ring_a[0] += 1
                return take(ring_a[0] % 2, "act", reader)

            def to_dve(reader):
                ring_v[0] += 1
                return take(2 + ring_v[0] % 2, "dve", reader)

            def unit_ready(base, i, rounds=0):
                pe.wait_ge(unit_loaded[i % RING], (rounds + (base + i) // RING + 1) * 16)

            def chunks(out, w, src, n0, n1, cols=P):
                for n in range(n0, n1):
                    for k in range(DC):
                        last = pe.matmul(out[:, (n - n0) * S:(n - n0 + 1) * S], w[:, k, n * P:(n + 1) * P],
                                         src[:, k, :], start=k == 0, stop=k == DC - 1)
                return last

            def by_token(out, w, src, half, c0, cols):
                for k in range(DC):
                    last = pe.matmul(out, src[:, k, half * P:(half + 1) * P], w[:, k, c0:c0 + cols],
                                     start=k == 0, stop=k == DC - 1)
                return last

            def split_product(out, high, low, src_high, src_low, way="width", chunks_=DC, blocks=2):
                passes_ = ((high, src_high), (high, src_low), (low, src_high))
                for n in range(blocks):
                    for k in range(chunks_):
                        for m, (w, x) in enumerate(passes_):
                            first, final = k == 0 and m == 0, k == chunks_ - 1 and m == 2
                            if way == "width":
                                last = pe.matmul(out[:, n * S:(n + 1) * S], w[:, k, n * P:(n + 1) * P], x[:, k, :],
                                                 start=first, stop=final)
                            else:
                                last = pe.matmul(out[:, n * JOB:(n + 1) * JOB], x[:, k, n * P:(n + 1) * P], w[:, k, :],
                                                 start=first, stop=final)
                return last

            def sum_squares(step, sq, cols=S):
                out = to_act(step + " root")
                for k in range(DC):
                    last = pe.matmul(out[:, 0:cols], ones, sq[:, k, :], start=k == 0, stop=k == DC - 1)
                last.then_inc(pe_done, pe_p.mark(step + " sum"))

            def expert_tile(name, before, rounds, hn, pick_of, spread_of, f_width):
                fc = f_width // P
                halves = f_width // 512
                per_unit = 2 // halves
                n_in = DC // per_unit
                for j in range(2):
                    out = to_act(f"{name} x{j}")
                    for c in range(4 * j, 4 * j + 4):
                        for half in range(TH):
                            last = pe.matmul(out[:, (c % 4) * P:(c % 4 + 1) * P], hn[:, half, c * P:(c + 1) * P],
                                             pick_of(half), start=half == 0, stop=half == TH - 1)
                    last.then_inc(pe_done, pe_p.mark(f"{name} x{j}"))
                pe.wait_ge(act_done, act_at(f"{name} x1", loops))
                pe.wait_ge(act_done, act_at(f"{name} y1", loops, **{name: 1}))
                pe.wait_ge(dve_done, dve_at(f"{name} hid", loops, **{name: 1}))
                for which, bank0 in (("gate", 4), ("up", 6)):
                    for n in range(n_in):
                        u = n + (n_in if which == "up" else 0)
                        pe.wait_ge(unit_loaded[u % RING], (rounds + before(u % RING) + u // RING + 1) * 16)
                        w = slot(u).rearrange("p (e k f) -> p k e f", k=per_unit, e=TILE_E)
                        for k in range(per_unit):
                            c = n * per_unit + k
                            for f in range(halves):
                                for e in range(TILE_E):
                                    last = pe.matmul(banks[bank0 + f][32 * e:32 * e + 32, :],
                                                     x_slots[:, c, 32 * e:32 * e + 32],
                                                     w[:, k, e, f * 512:(f + 1) * 512],
                                                     start=c == 0, stop=c == DC - 1)
                        steps = [f"{name} unit {u}"] + ([f"{name} {which}"] if n == n_in - 1 else [])
                        last.then_inc(pe_done, pe_p.mark(*steps))
                pe.wait_ge(dve_done, dve_at(f"{name} hid", loops))
                for j in range(fc // 4):
                    out = to_act(f"{name} hidT{j}")
                    for f in range(4):
                        last = pe.transpose(out[:, f * P:(f + 1) * P], hid[:, (4 * j + f) * P:(4 * j + f + 1) * P],
                                            ident)
                    last.then_inc(pe_done, pe_p.mark(f"{name} hidT{j}"))
                pe.wait_ge(act_done, act_at(f"{name} hidT{fc // 4 - 1}", loops))
                for f in range(fc):
                    u = 2 * n_in + f
                    pe.wait_ge(unit_loaded[u % RING], (rounds + before(u % RING) + u // RING + 1) * 16)
                    w = slot(u).rearrange("p (e d) -> p e d", e=TILE_E)
                    for d in range(2):
                        for e in range(TILE_E):
                            last = pe.matmul(banks[4 + d][32 * e:32 * e + 32, :], hidT[:, f, 32 * e:32 * e + 32],
                                             w[:, e, d * 512:(d + 1) * 512], start=f == 0, stop=f == fc - 1)
                    steps = [f"{name} unit {u}"] + ([f"{name} down"] if f == fc - 1 else [])
                    last.then_inc(pe_done, pe_p.mark(*steps))
                pe.wait_ge(act_done, act_at(f"{name} y1", loops))
                for j in range(4):
                    out = to_dve(f"{name} add{j}")
                    for c in range(2):
                        last = pe.matmul(out[:, c * S:(c + 1) * S], y_sb[:, (2 * j + c) * P:(2 * j + c + 1) * P],
                                         spread_of(), start=True, stop=True)
                    last.then_inc(pe_done, pe_p.mark(f"{name} back{j}"))

            pe.sem_inc(pe_done, pe_p.credit)
            pe.wait_ge(consts_loaded, 32)
            pe_p.enter("layer")
            with pe.Fori(0, LAYERS) as layer:
                loops["layer"] = layer
                ring_rounds = layer * (UNITS1 // RING)

                def unit_done(i):
                    return f"unit {i}"

                pe.wait_ge(act_done, act_at("squares", loops))
                sum_squares("norm1", squares)
                def job(i, src_high, src_low):
                    unit, _, step, way, reader = JOBS[i]
                    out = to_act(step) if reader == "act" else to_dve(step)
                    pe.wait_ge(dve_done, dve_at(f"low {i}", loops))
                    low = job_weights(JOBS[i], ring_parts)
                    steps = [step] + ([unit_done(unit)] if i + 1 == len(JOBS) or JOBS[i + 1][0] != unit else [])
                    if i == len(IN_JOBS):
                        steps.append(unit_done(13))
                    split_product(out, high_room(i), low, src_high, src_low, way).then_inc(pe_done, pe_p.mark(*steps))

                def gate(n):
                    unit, _, step = GATE_JOBS[n]
                    out = take(2 + n % 2, "act", step)
                    pe.wait_ge(dve_done, dve_at(f"gate low {n}", loops))
                    steps = [step] + ([unit_done(unit)] if n % 4 == 3 else [])
                    split_product(out, gate_high[n % GATE_BUFS], gate_weights(n, ring_parts), hn_high, hn_low, blocks=1)\
                        .then_inc(pe_done, pe_p.mark(*steps))

                flip = {"s": 0, "p": 0}

                def scores(step, q, k):
                    flip["s"] ^= 1
                    out = take(4 + flip["s"], "dve", step)
                    pe.matmul(out[:], q, k, start=True, stop=True).then_inc(pe_done, pe_p.mark(step))

                def turned(step, of):
                    flip["p"] ^= 1
                    out = take(6 + flip["p"], "act", step)
                    for n in range(4):
                        last = pe.transpose(out[:, n * P:(n + 1) * P], of(n // 2, n % 2), ident)
                    last.then_inc(pe_done, pe_p.mark(step))

                def dil_scores(sp, qh):
                    for g in range(DIL_GROUPS):
                        c = 2 * g + sp
                        scores(f"s dil {sp} {qh} {g}", q_dil[:, c, qh * P:(qh + 1) * P], k_dil[:, 2 * c:2 * c + 2, :])

                def dil_turn(sp, qh):
                    pe.wait_ge(dve_done, dve_at(f"p dil {sp} {qh}", loops))
                    for g in range(DIL_GROUPS):
                        turned(f"t dil {sp} {qh} {g}",
                               lambda h, kh: prob_dil[:, qh, h, g * S + kh * P:g * S + (kh + 1) * P])

                def dil_out(sp):
                    pe.wait_ge(act_done, act_at(f"t dil {sp} {TH - 1} {DIL_GROUPS - 1}", loops))
                    out = to_act(f"o dil {sp}")
                    for g in range(DIL_GROUPS):
                        for kh in range(TH):
                            for h in range(2):
                                head = g * DIL_SLOTS + 2 * sp + h
                                last = pe.matmul(out[h * HD:(h + 1) * HD, 0:S],
                                                 v_dil[:, kh, head * HD:(head + 1) * HD],
                                                 probT_dil[:, h, g, kh * S:(kh + 1) * S],
                                                 start=g == 0 and kh == 0,
                                                 stop=g == DIL_GROUPS - 1 and kh == TH - 1)
                    last.then_inc(pe_done, pe_p.mark(f"o dil {sp}"))

                def win_scores(w):
                    kv = w // 2
                    for qh in range(TH):
                        scores(f"s win {w} {qh}", q_win[:, w, qh * P:(qh + 1) * P], k_win[:, 2 * kv:2 * kv + 2, :])

                def win_turn(w):
                    pe.wait_ge(dve_done, dve_at(f"p win {w} {TH - 1}", loops))
                    for h in range(2):
                        turned(f"t win {w} {h}",
                               lambda kh, qh: prob_win[:, w % WBUFS, qh, h, kh * P:(kh + 1) * P])

                def win_out(w):
                    pe.wait_ge(act_done, act_at(f"t win {w} 1", loops))
                    if w >= 2:
                        pe.wait_ge(dve_done, dve_at(f"o win {w - 2}", loops))
                    out = to_act(f"o win {w}")
                    kv = w // 2
                    for kh in range(TH):
                        for h in range(2):
                            last = pe.matmul(out[h * HD:(h + 1) * HD, 0:S], v_win[:, kh, kv * HD:(kv + 1) * HD],
                                             probT_win[:, w % WBUFS, h, kh * S:(kh + 1) * S],
                                             start=kh == 0, stop=kh == TH - 1)
                    last.then_inc(pe_done, pe_p.mark(f"o win {w}"))

                pairs = WIN_HEADS // 2
                pe.wait_ge(dve_done, dve_at("hn1 low", loops))
                for i in range(len(IN_JOBS)):
                    job(i, hn_high, hn_low)
                pe.wait_ge(dve_done, dve_at("k_win", loops))
                pe.wait_ge(act_done, act_at("v_win", loops))
                dil_scores(0, 0)
                gate(0)
                gate(1)
                dil_scores(0, 1)
                gate(2)
                gate(3)
                dil_turn(0, 0)
                dil_scores(1, 0)
                gate(4)
                dil_turn(0, 1)
                dil_scores(1, 1)
                gate(5)
                dil_out(0)
                dil_turn(1, 0)
                gate(6)
                win_scores(0)
                dil_turn(1, 1)
                gate(7)
                win_scores(1)
                dil_out(1)
                win_scores(2)
                for w in range(pairs):
                    gate(DC + w)
                    win_turn(w)
                    if w:
                        win_out(w - 1)
                    if w + 3 < pairs:
                        win_scores(w + 3)
                pe.wait_ge(act_done, act_at("o dil 1", loops))
                unit_ready(0, 12, ring_rounds)
                unit_ready(0, 13, ring_rounds)
                for j in range(4):
                    if j == 2:
                        win_out(pairs - 1)
                    out = to_dve(f"ya {j}")
                    for n in range(2):
                        for c in range(2):
                            last = pe.matmul(out[:, n * S:(n + 1) * S],
                                             slot(12 + c)[:, (2 * j + n) * P:(2 * j + n + 1) * P], o_dil[:, c, :],
                                             start=c == 0, stop=c == 1)
                    last.then_inc(pe_done, pe_p.mark(f"ya {j}", unit_done(12)))
                pe.wait_ge(dve_done, dve_at(f"o win {pairs - 1}", loops))
                for n in range(4):
                    job(len(IN_JOBS) + n, o_high, o_low)
                def ada_unit(n):
                    u = 18 + n
                    if n == 0:
                        pe.wait_ge(act_done, act_at("c_silu", loops))
                    unit_ready(0, u, ring_rounds)
                    w = slot(u).rearrange("p (k n) -> p k n", k=DC)
                    for k in range(DC):
                        for b in range(4):
                            last = pe.matmul(ada_bank[32 * b:32 * b + 32, (n % 4) * P:(n % 4 + 1) * P], c_silu[:, k, :],
                                             w[:, k, b * P:(b + 1) * P], start=k == 0, stop=k == DC - 1)
                    last.then_inc(pe_done, pe_p.mark(f"ada {n}", unit_done(u)))

                ada_bank = take(7, "act", "ada 3")
                ada_unit(0)
                ada_unit(1)
                pe.wait_ge(dve_done, dve_at("merged low 3", loops))
                for n in range(4, 8):
                    job(len(IN_JOBS) + n, merged_high, merged_low)

                ada_unit(2)
                pe.wait_ge(act_done, act_at("squares2", loops))
                sum_squares("norm2", squares)
                ada_unit(3)
                out = take(0, "act", "router exp")
                for k in range(DC):
                    pe.wait_ge(dve_done, dve_at(f"hn2 {k}", loops))
                    last = pe.matmul(out[0:EXPERTS, 0:S], par[:, Q_ROUTER + k * EXPERTS:Q_ROUTER + (k + 1) * EXPERTS],
                                     hn3[:, k, :], start=k == 0, stop=k == DC - 1)
                last.then_inc(pe_done, pe_p.mark("router rows"))
                for j in range(4):
                    half, c0 = j // 2, 4 * (j % 2)
                    out = take((1, 4, 5, 6)[j], "act", f"hn_tok {j}")
                    if j == 1:
                        pe.wait_ge(dve_done, dve_at("router rows", loops))
                    for c in range(4):
                        if j == 1 and c == 1:
                            for h in range(TH):
                                last = pe.transpose(banks[0][:, S + h * EXPERTS:S + (h + 1) * EXPERTS],
                                                    aff_rows[0:EXPERTS, h * P:(h + 1) * P], ident[0:EXPERTS, 0:EXPERTS])
                            last.then_inc(pe_done, pe_p.mark("router"))
                        last = pe.transpose(out[:, c * P:(c + 1) * P], hn3[:, c0 + c, half * P:(half + 1) * P], ident)
                    last.then_inc(pe_done, pe_p.mark(f"hn_tok {j}"))
                ada_bank = take(7, "act", "ada 5")
                ada_unit(4)
                pe.wait_ge(dve_done, dve_at("aff", loops))
                out = take(2, "dve", "aff rows")
                for half in range(TH):
                    last = pe.transpose(out[0:EXPERTS, half * P:(half + 1) * P], aff[:, half, :], ident)
                last.then_inc(pe_done, pe_p.mark("aff rows"))
                ada_unit(5)
                pe.wait_ge(dve_done, dve_at("diag", loops))
                out = take(3, "dve", "picked")
                pe.matmul(out[:], ones[0:EXPERTS, :], idx_diag[0:EXPERTS, :], start=True, stop=True)\
                  .then_inc(pe_done, pe_p.mark("slot tokens"))
                out = take(2, "dve", "slot cols")
                for g in range(TILES1):
                    for n, diag in enumerate((idx_diag, gate_diag)):
                        last = pe.matmul(out[:, n * TILES1 + g:n * TILES1 + g + 1],
                                         diag[0:EXPERTS, g * P:(g + 1) * P], ones[0:EXPERTS, 0:1],
                                         start=True, stop=True)
                last.then_inc(pe_done, pe_p.mark("slot cols"))

                pe.wait_ge(dve_done, dve_at("spread", loops))
                pe.wait_ge(act_done, act_at("hn_tok 3", loops))
                pe.wait_ge(act_done, act_at("ada 5", loops))
                pe.sem_inc(waited, 1)
                taken.clear()
                ring_a[0] = ring_v[0] = 0
                taken[1] = (act_done, lambda step, l: act_at(step, l, tile=1), f"tile hidT0")
                taken[0] = (act_done, lambda step, l: act_at(step, l, tile=1), f"tile hidT1")
                taken[3] = (dve_done, lambda step, l: dve_at(step, l, tile=1), f"tile add2")
                taken[2] = (dve_done, lambda step, l: dve_at(step, l, tile=1), f"tile add3")
                pe_p.enter("tile")
                with pe.Fori(0, TILES1) as t:
                    loops["tile"] = t
                    expert_tile("tile", lambda slot_: UNITS1_HEAD // RING, ring_rounds + t * (UNITS1_TILE // RING), hn_tok,
                                lambda half: pick[:, half, bass.ds(t * P, P)],
                                lambda: spread1[:, t, :], FE)
                pe_p.leave(TILES1)
                del loops["tile"]
                taken.clear()
                ring_a[0] = ring_v[0] = 0
            pe_p.leave(LAYERS)
            del loops["layer"]
            def row_of(half):
                return slice(half * P, (half + 1) * P)

            pe.wait_ge(consts2_loaded, 64)
            pe.wait_ge(act_done, act_at("f squares"))
            sum_squares("f norm", squares2)
            pe.wait_ge(dve_done, dve_at("tile add3"))
            for r in range(3):
                out = to_dve(f"ada cols {r}")
                for b in range(4):
                    n = 4 * r + b
                    last = pe.transpose(out[:, b * P:(b + 1) * P], ada_rows[:, n * P:(n + 1) * P], ident)
                last.then_inc(pe_done, pe_p.mark(f"ada cols {r}"))
            pe.wait_ge(act_done, act_at("x squares"))
            sum_squares("x norm", squares2)
            out = to_act("f_sin 1")
            pe.matmul(out[0:HY_HID, 0:S], par2[0:HY_EMB, R_W1:R_W1 + HY_HID], cst2[0:HY_EMB, B_POS:B_POS + S], start=True,
                      stop=True).then_inc(pe_done, pe_p.mark("filter 1"))

            def job2(i, out, src_high, src_low, way="width", steps=(), step=None):
                unit, _, name, chunks_ = JOBS2[i]
                pe.wait_ge(dve_done, dve_at(f"low2 {i}"))
                last = split_product(out, w_high2[i % 2], job2_weights(i, ring_parts), src_high, src_low, way, chunks_)
                last.then_inc(pe_done, pe_p.mark(step or name, *steps, f"unit2 {unit}"))

            def spectrum(step, taps, sine, f):
                out = to_dve(step)
                for half in range(TH):
                    at = B_DFT + half * 2 * S + sine * S + f * P
                    last = pe.matmul(out[:], cst2[:, at:at + P], taps[:, half, :], start=half == 0, stop=half == TH - 1)
                last.then_inc(pe_done, pe_p.mark(step))

            def hy_job(n):
                job2(HY0 + n, to_dve(f"hy {n}"), hx_high, hn_low)

            def gate_job(n):
                job2(GATE0 + n, to_act(f"gates2 {n}"), hx_high, hn_low)

            pe.wait_ge(dve_done, dve_at("hx low"))
            hy_job(0)
            hy_job(1)
            pe.wait_ge(act_done, act_at("f_sin 1"))
            out = to_act("f_sin 2")
            pe.matmul(out[0:HY_HID, 0:S], par2[0:HY_HID, R_W2:R_W2 + HY_HID], f_sin[0:HY_HID, :], start=True,
                      stop=True).then_inc(pe_done, pe_p.mark("filter 2"))
            hy_job(2)
            hy_job(3)
            pe.wait_ge(act_done, act_at("f_sin 2"))
            for n in range(2):
                for half in range(TH):
                    out = to_dve(f"taps {n} {half}")
                    pe.matmul(out[:], f_sin[0:HY_HID, row_of(half)], par2[0:HY_HID, R_W3 + n * HY:R_W3 + (n + 1) * HY],
                              start=True, stop=True).then_inc(pe_done, pe_p.mark(f"taps {n} {half}"))
            hy_job(4)
            hy_job(5)

            gate_job(0)
            pe.wait_ge(dve_done, dve_at("taps"))
            for f in range(2):
                spectrum(f"k_cos {f}", taps_sum, 0, f)
            for f in range(2):
                spectrum(f"k_sin {f}", taps_f, 1, f)
            out = to_dve("k_nyq")
            for half in range(TH):
                at = B_DFT + half * 2 * S + S
                last = pe.matmul(out[0:1, :], cst2[:, at:at + 1], taps_sum[:, half, :], start=half == 0, stop=half == 1)
            last.then_inc(pe_done, pe_p.mark("k_nyq"))
            pe.wait_ge(act_done, act_at("c squares"))
            sum_squares("c norm", squares2)
            gate_job(1)
            pe.wait_ge(dve_done, dve_at("hy u"))
            for half in range(TH):
                out = to_act(f"u_tok {half}")
                for c in range(4):
                    last = pe.transpose(out[:, c * P:(c + 1) * P], conv[:, c, row_of(half)], ident)
                last.then_inc(pe_done, pe_p.mark(f"u_tok {half}"))
            gate_job(2)
            pe.wait_ge(act_done, act_at("u_tok 1"))
            for f in range(2):
                for sine in range(2):
                    step = f"u {'sin' if sine else 'cos'} {f}"
                    out = to_act(step)
                    for half in range(TH):
                        at = B_DFT + half * 2 * S + sine * S + f * P
                        last = pe.matmul(out[:], cst2[:, at:at + P], u_tok[:, half, :], start=half == 0,
                                         stop=half == TH - 1)
                    last.then_inc(pe_done, pe_p.mark(step))
            gate_job(3)
            gate_job(4)
            gate_job(5)
            pe.wait_ge(dve_done, dve_at("products"))
            for j in range(2):
                out = to_dve(f"hy y {j}")
                for c in range(2):
                    ch = slice((2 * j + c) * P, (2 * j + c + 1) * P)
                    for n, prod in enumerate((prod_cos, prod_sin)):
                        for f in range(2):
                            at = B_IDFT + (n * 2 + f) * S
                            last = pe.matmul(out[:, c * S:(c + 1) * S], prod[:, f, ch], cst2[:, at:at + S],
                                             start=n == 0 and f == 0, stop=n == 1 and f == 1)
                last.then_inc(pe_done, pe_p.mark(f"hy y {j}"))
            gate_job(6)
            gate_job(7)

            pe.wait_ge(dve_done, dve_at("hc low"))
            for i in range(Z0, QG0):
                name = JOBS2[i][2]
                job2(i, to_act(f"{name} c"), hc_high, hc_low, "token", step=f"{name} c")
                job2(i, to_act(f"{name} x"), hx_high, hn_low, "token", (f"{name} x",))

            pe.wait_ge(act_done, act_at("log c"))
            for d in range(2):
                near = cst2[:, B_CTX + d * P:B_CTX + (d + 1) * P]
                for half in range(TH):
                    out = to_act(f"decay {d} {half}")
                    whole = half == d
                    last = pe.matmul(out[:], near, logf_c[:, d, half, :], start=True, stop=not whole)
                    if whole:
                        last = pe.matmul(out[:], ones, logf_c[:, d, 1 - half, :], start=False, stop=True)
                    last.then_inc(pe_done, pe_p.mark(f"decay {d} {half}"))
            def qg_job(n):
                job2(QG0 + n, to_act(f"qg {n}"), hx_high, hn_low)

            qg_job(0)
            qg_job(1)
            for d in range(2):
                pe.wait_ge(dve_done, dve_at(f"decayed {d}"))
                out = to_dve(f"state0 {d}")
                for h in range(HEADS2):
                    for half in range(TH):
                        last = pe.matmul(out[:, h * P:(h + 1) * P], keys_decayed[:, d, half, h * P:(h + 1) * P],
                                         vals_c[:, half, h * P:(h + 1) * P], start=half == 0, stop=half == TH - 1)
                last.then_inc(pe_done, pe_p.mark(f"state0 {d}"))

            o_banks = (4, 5)

            def scan_sums(d):
                sums, rest, _ = direction(d)
                pe.wait_ge(act_done, act_at("log x"))
                for half in range(TH):
                    for pair in range(2):
                        out = to_act(f"cum {d} {half} {pair}")
                        for h in range(2):
                            last = pe.matmul(out[:, h * S:(h + 1) * S],
                                             logf[:, d, half, (2 * pair + h) * P:(2 * pair + h + 1) * P], sums,
                                             start=True, stop=True)
                        last.then_inc(pe_done, pe_p.mark(f"cum {d} {half} {pair}"))
                    out = to_act(f"rest {d} {half}")
                    pe.matmul(out[:], rest, logf[:, d, half, :], start=True, stop=True)\
                      .then_inc(pe_done, pe_p.mark(f"rest {d} {half}"))
                    out = to_dve(f"keyT {d} {half}")
                    for h in range(HEADS2):
                        last = pe.transpose(out[:, h * P:(h + 1) * P], keys[:, d, half, h * P:(h + 1) * P], ident)
                    last.then_inc(pe_done, pe_p.mark(f"keyT {d} {half}"))

            def scan(d):
                for half in range(TH):
                    pe.wait_ge(dve_done, dve_at(f"qk {d} {half}"))
                    out = to_dve(f"inner {d} {half}")
                    for h in range(HEADS2):
                        last = pe.matmul(out[:, h * P:(h + 1) * P], k_mid[:, h, row_of(half)], q_mid[:, h, row_of(half)],
                                         start=True, stop=True)
                    last.then_inc(pe_done, pe_p.mark(f"inner {d} {half}"))
                for half in range(TH):
                    pe.wait_ge(dve_done, dve_at(f"inner {d} {half}"))
                    for h in range(HEADS2):
                        last = pe.matmul(banks[o_banks[half]][:, h * P:(h + 1) * P], inner[:, half, h, :],
                                         vals[:, half, h * P:(h + 1) * P], start=d == 0 and h == 0, stop=False,
                                         skip_group_check=True)
                    last.then_inc(pe_done, pe_p.mark(f"o inner {d} {half}"))
                pe.wait_ge(dve_done, dve_at(f"k_rest {d}"))
                for n in range(CHUNKS):
                    c = n if d == 0 else CHUNKS - 1 - n
                    half, at = c // 4, 32 * (c % 4)
                    rows = slice(at, at + CHUNK)
                    if n < CHUNKS - 1:
                        out = to_dve(f"grown {d} {n}")
                        for h in range(HEADS2):
                            last = pe.matmul(out[:, h * P:(h + 1) * P], k_rest[rows, half, h * P:(h + 1) * P],
                                             vals[rows, half, h * P:(h + 1) * P], start=True, stop=True)
                        last.then_inc(pe_done, pe_p.mark(f"grown {d} {n}"))
                    pe.wait_ge(dve_done, dve_at(f"state {d} {n}"))
                    state = state0[:, d, :] if n == 0 else states[:, n % 4, :]
                    for h in range(HEADS2):
                        last = pe.matmul(banks[o_banks[half]][rows, h * P:(h + 1) * P],
                                         q_cum[:, h, half * P + at:half * P + at + CHUNK],
                                         state[:, h * P:(h + 1) * P], start=False,
                                         stop=d == 1, skip_group_check=True)
                    last.then_inc(pe_done, pe_p.mark(f"o {d} {n}"))

            scan_sums(0)
            qg_job(2)
            qg_job(3)
            pe.wait_ge(dve_done, dve_at("y_b low"))
            for n in range(4):
                job2(PB0 + n, to_dve(f"pb {n}"), y_b_high, y_b_low)
            scan(0)
            scan_sums(1)
            scan(1)
            taken[4] = taken[5] = (act_done, act_at, "o_sq 1")
            for half in range(TH):
                pe.wait_ge(dve_done, dve_at(f"o_tok {half}"))
                out = to_dve(f"y_a {half}")
                for h in range(HEADS2):
                    last = pe.transpose(out[:, h * P:(h + 1) * P], o_tok[:, half, h * P:(h + 1) * P], ident)
                last.then_inc(pe_done, pe_p.mark(f"y_a {half}"))

            pe.wait_ge(dve_done, dve_at("y_a low"))
            for n in range(4):
                job2(PA0 + n, to_dve(f"pa {n}"), y_a_high, y_a_low)
            pe.wait_ge(dve_done, dve_at("merged2 low 3"))
            for n in range(4):
                job2(MIX0 + n, to_dve(f"mix2 {n}"), merged2_high, merged2_low)

            pe.wait_ge(act_done, act_at("m squares"))
            sum_squares("m norm", sq_moe)
            pe.wait_ge(dve_done, dve_at("h2"))
            out = to_dve("logits2")
            for half in range(TH):
                for k in range(DC):
                    at = R_ROUTER + k * ROUTES
                    last = pe.matmul(out[:, half * ROUTES:(half + 1) * ROUTES], hn3[:, k, row_of(half)],
                                     par2[:, at:at + ROUTES], start=k == 0, stop=k == DC - 1)
            last.then_inc(pe_done, pe_p.mark("logits2"))
            for j in range(4):
                half, c0 = j // 2, 4 * (j % 2)
                out = to_act(f"hn_tok2 {j}")
                for c in range(4):
                    last = pe.transpose(out[:, c * P:(c + 1) * P], hn3[:, c0 + c, row_of(half)], ident)
                last.then_inc(pe_done, pe_p.mark(f"hn_tok2 {j}"))
            pe.wait_ge(dve_done, dve_at("chosen"))
            out = to_dve("rank")
            before = cst2[:, B_CTX + P:B_CTX + 2 * P]
            for half in range(TH):
                cols = slice(half * EXPERTS2, (half + 1) * EXPERTS2)
                last = pe.matmul(out[:, cols], before, chosen[:, half, :], start=True, stop=half == 0)
                if half:
                    last = pe.matmul(out[:, cols], ones, chosen[:, 0, :], start=False, stop=True)
            for half in range(TH):
                last = pe.matmul(out[:, TH * EXPERTS2:(TH + 1) * EXPERTS2], ones, chosen[:, half, :],
                                 start=half == 0, stop=half == TH - 1)
            last.then_inc(pe_done, pe_p.mark("rank"))

            pe.wait_ge(dve_done, dve_at("passes"))
            passes = pe.value_load(n_passes[0:1, 0:1], min_val=1, max_val=S // SLOTS)
            pe_p.enter("pass")
            with pe.Fori(0, passes) as p:
                loops["pass"] = p
                taken.clear()
                ring_a[0] = ring_v[0] = 0
                pe.wait_ge(dve_done, dve_at("weighed", loops))
                pe.wait_ge(act_done, act_at("hn_tok2 3", loops))
                for j in range(TILES2 // 2):
                    out = to_act(f"spread2 {j}")
                    for n in range(2):
                        for half in range(TH):
                            g = 2 * j + n
                            last = pe.transpose(out[:, n * S + half * P:n * S + (half + 1) * P],
                                                weighed[:, half, g * P:(g + 1) * P], ident)
                    last.then_inc(pe_done, pe_p.mark(f"spread2 {j}"))
                pe.wait_ge(act_done, act_at(f"spread2 {TILES2 // 2 - 1}", loops))
                pe.sem_inc(waited, 1)
                taken.clear()
                ring_a[0] = ring_v[0] = 0
                taken[1] = (act_done, lambda step, l: act_at(step, l, tile2=1), "tile2 hidT0")
                taken[0] = (act_done, lambda step, l: act_at(step, l, tile2=1), "tile2 x1")
                taken[3] = (dve_done, lambda step, l: dve_at(step, l, tile2=1), "tile2 add2")
                taken[2] = (dve_done, lambda step, l: dve_at(step, l, tile2=1), "tile2 add3")
                pe_p.enter("tile2")
                with pe.Fori(0, TILES2) as t:
                    loops["tile2"] = t
                    expert_tile("tile2", lambda slot_: UNITS_L // RING + (UNITS2_HEAD // HEAD_SLOTS if slot_ < HEAD_SLOTS else 0),
                                p * (TILES2 * UNITS2_TILE // RING) + t * (UNITS2_TILE // RING), hn_tok,
                                lambda half: pick2[:, half, bass.ds(t * P, P)], lambda: spread2[:, t, :], FE2)
                pe_p.leave(TILES2)
                del loops["tile2"]
            pe_p.leave_counted()
            loops["pass"] = passes
            pe.wait_ge(act_done, act_at("l squares", loops, **{"pass": 1}))
            for k in range(DC):
                last = pe.matmul(banks[0][:, 0:S], ones, sq_moe[:, k, :], start=k == 0, stop=k == DC - 1)
            last.then_inc(pe_done, pe_p.mark("l norm sum"))

        @block.scalar
        def _(act):
            loops = {}

            def copy(step, out, in_, scale=1.0):
                act.wait_ge(pe_done, pe_at(step, loops))
                act.activation(out, in_, ACT.Copy, scale=scale).then_inc(act_done, act_p.mark(step))

            def two(bank, n=2):
                return bank[:].rearrange("p (c t) -> p c t", c=n)

            ring_a = [0]

            def bank_a():
                ring_a[0] += 1
                return banks[ring_a[0] % 2]

            def root(step, cols=S, out=None):
                bank = bank_a()
                act.wait_ge(pe_done, pe_at(step + " sum", loops))
                act.activation(rms_root if out is None else out, bank[:, 0:cols], ACT.Sqrt, bias=eps,
                               scale=1.0 / D).then_inc(act_done, act_p.mark(step + " root"))

            def expert_tile(name, f_width):
                fc = f_width // P
                for j in range(2):
                    copy(f"{name} x{j}", x_slots[:, 4 * j:4 * j + 4, :], two(bank_a(), 4))
                act.wait_ge(dve_done, dve_at(f"{name} hid", loops, **{name: 1}))
                act.wait_ge(pe_done, pe_at(f"{name} gate", loops))
                for f in range(f_width // 512):
                    act.activation(silu_sb[:, f * 512:(f + 1) * 512], banks[4 + f][:], ACT.Silu)\
                       .then_inc(act_done, act_p.mark(f"{name} silu {f}"))
                for j in range(fc // 4):
                    copy(f"{name} hidT{j}", hidT[:, 4 * j:4 * j + 4, :], two(bank_a(), 4))
                act.wait_ge(pe_done, pe_at(f"{name} back3", loops, **{name: 1}))
                act.wait_ge(pe_done, pe_at(f"{name} down", loops))
                for d in range(2):
                    act.activation(y_sb[:, d * 512:(d + 1) * 512], banks[4 + d][:], ACT.Copy)\
                       .then_inc(act_done, act_p.mark(f"{name} y{d}"))

            act.sem_inc(act_done, act_p.credit)
            act.wait_ge(consts_loaded, 32)
            act.dma_start(cst[:, C_DIST:C_COLS], io["consts"][:, C_DIST:C_COLS]).then_inc(dist_loaded, 16)
            act_p.enter("layer")
            with act.Fori(0, LAYERS) as layer:
                loops["layer"] = layer
                ring_rounds = layer * (UNITS1 // RING)
                def high(i, after=None):
                    unit = JOBS[i][0]
                    act.wait_ge(unit_loaded[unit % RING], (ring_rounds + unit // RING + 1) * 16)
                    if after or i >= 2:
                        act.wait_ge(pe_done, pe_at(after or JOBS[i - 2][2], loops))
                    act.activation(high_room(i), job_weights(JOBS[i]), ACT.Copy)\
                       .then_inc(act_done, act_p.mark(f"high {i}"))

                def gate_high_part(n):
                    unit = GATE_JOBS[n][0]
                    act.wait_ge(unit_loaded[unit % RING], (ring_rounds + unit // RING + 1) * 16)
                    act.wait_ge(pe_done, pe_at(GATE_JOBS[n - GATE_BUFS][2] if n >= GATE_BUFS else "unit 6", loops))
                    act.activation(gate_high[n % GATE_BUFS], gate_weights(n), ACT.Copy)\
                       .then_inc(act_done, act_p.mark(f"gate high {n}"))

                def gate(n):
                    if n + GATE_BUFS < len(GATE_JOBS):
                        gate_high_part(n + GATE_BUFS)
                    at = Q_BGATE + n
                    act.wait_ge(pe_done, pe_at(GATE_JOBS[n][2], loops))
                    act.activation(gates[:, n, :], banks[2 + n % 2][:, 0:S], ACT.Identity, bias=par[:, at:at + 1])\
                       .then_inc(act_done, act_p.mark(GATE_JOBS[n][2]))

                def gates_open(branch):
                    chunks_ = gates[:, branch * DC:(branch + 1) * DC, :]
                    act.wait_ge(act_done, act_at(f"gate {branch * DC + DC - 1}", loops))
                    act.activation(chunks_, chunks_, ACT.Sigmoid).then_inc(act_done, act_p.mark(f"gates {branch}"))

                act.wait_ge(dve_done, dve_at("tile add3", loops, layer=1))
                act.activation(squares, h3, ACT.Square).then_inc(act_done, act_p.mark("squares"))
                high(0)
                root("norm1")
                high(1)
                for half in range(2):
                    act.wait_ge(dve_done, dve_at(f"hn1 {half}", loops))
                    act.activation(hn_high[:, 4 * half:4 * half + 4, :], hn3[:, 4 * half:4 * half + 4, :], ACT.Copy)\
                       .then_inc(act_done, act_p.mark(f"hn1 high {half}"))
                act.wait_ge(params_loaded, layer * 16 + 16)
                act.wait_ge(dve_done, dve_at("c_pad"))
                for r in range(2):
                    act.activation(c_silu[:, :, r], par[:, Q_C + r * DC:Q_C + (r + 1) * DC], ACT.Silu)\
                       .then_inc(act_done, act_p.mark("c_silu"))
                for i, (_, c0, step, _, reader) in enumerate(IN_JOBS):
                    if i + 2 < len(IN_JOBS):
                        high(i + 2)
                    else:
                        gate_high_part(i + 2 - len(IN_JOBS))
                    if reader == "act":
                        kind, n = step.split(" ") if " " in step else (step, 0)
                        n = int(n)
                        if kind in ("qk_dil", "q_win"):
                            q = (q_dil if kind == "qk_dil" else q_win)[:, 2 * n:2 * n + 2, :]
                            copy(step, q, two(bank_a()), HD ** -0.5)
                        else:
                            copy(step, v_dil[:, :, JOB * n:JOB * n + JOB] if kind == "v_dil" else v_win, two(bank_a()))
                flip = [0]

                def bank_p():
                    flip[0] ^= 1
                    return banks[6 + flip[0]]

                def exps(step, col, row):
                    act.wait_ge(dve_done, dve_at("m" + step, loops))
                    for h in range(2):
                        act.activation(row(h), row(h), ACT.Exp, bias=neg_max[:, col + h:col + h + 1],
                                       accum_out=row_sum[:, col + h:col + h + 1])\
                           .then_inc(act_done, act_p.mark(f"e{step} {h}"))

                def dil_exps(sp, qh):
                    exps(f" dil {sp} {qh}", 4 * sp + 2 * qh, lambda h: prob_dil[:, qh, h, :])

                def dil_turn(sp, qh):
                    if sp:
                        act.wait_ge(pe_done, pe_at(f"o dil {sp - 1}", loops))
                    for g in range(DIL_GROUPS):
                        out = probT_dil[:, :, g, :].rearrange("p h (k q x) -> p h k q x", k=TH, q=TH)[:, :, :, qh, :]
                        copy(f"t dil {sp} {qh} {g}", out, bank_p()[:].rearrange("p (h k x) -> p h k x", h=2, k=TH))

                def dil_out(sp):
                    copy(f"o dil {sp}", o_dil[:, sp, :], bank_a()[:, 0:S])

                pairs = WIN_HEADS // 2
                first = len(IN_JOBS)

                def win_exps(w):
                    for qh in range(TH):
                        exps(f" win {w} {qh}", 8 + 4 * w + 2 * qh, lambda h: prob_win[:, w % WBUFS, qh, h, :])

                def win_turn(w):
                    act.wait_ge(pe_done, pe_at(f"o win {w - WBUFS}" if w >= WBUFS else "o dil 1", loops))
                    for h in range(2):
                        copy(f"t win {w} {h}", probT_win[:, w % WBUFS, h, :], bank_p()[:])

                def win_out(w):
                    copy(f"o win {w}", o_high[:, w, :], bank_a()[:, 0:S])

                gate_high_part(2)
                gate(0)
                dil_exps(0, 0)
                gate(1)
                dil_exps(0, 1)
                gate(2)
                gate(3)
                dil_turn(0, 0)
                dil_exps(1, 0)
                gate(4)
                dil_turn(0, 1)
                dil_exps(1, 1)
                gate(5)
                dil_out(0)
                dil_turn(1, 0)
                gate(6)
                dil_turn(1, 1)
                win_exps(0)
                gate(7)
                dil_out(1)
                win_exps(1)
                for w in range(pairs):
                    gate(DC + w)
                    win_turn(w)
                    if w:
                        win_out(w - 1)
                    if w + 2 < pairs:
                        win_exps(w + 2)
                    if w == pairs - 2:
                        gates_open(0)
                        high(first, after="unit 7")
                high(first + 1, after=f"o win {pairs - 2}")
                win_out(pairs - 1)
                gates_open(1)
                for n in range(8):
                    if n + 2 < 8:
                        high(first + n + 2)
                    if n < 4:
                        act.wait_ge(dve_done, dve_at(f"merged {n}", loops))
                        act.activation(merged_high[:, 2 * n:2 * n + 2, :], merged[:, 2 * n:2 * n + 2, :], ACT.Copy)\
                           .then_inc(act_done, act_p.mark(f"merged high {n}"))
                act.wait_ge(dve_done, dve_at("mix 3", loops))
                act.activation(squares, h3, ACT.Square).then_inc(act_done, act_p.mark("squares2"))
                root("norm2")

                def ada_copy(n0, n1):
                    act.wait_ge(pe_done, pe_at(f"ada {n1 - 1}", loops))
                    act.activation(ada_rows[:, bass.ds(layer * (ADA_UNITS * P) + n0 * P, (n1 - n0) * P)],
                                   banks[7][:, 0:(n1 - n0) * P], ACT.Copy).then_inc(act_done, act_p.mark(f"ada {n1 - 1}"))

                ada_copy(0, 4)
                act.wait_ge(dve_done, dve_at("router max", loops))
                for half in range(TH):
                    act.activation(r_exp[:, half, :], banks[0][:, S + half * EXPERTS:S + (half + 1) * EXPERTS], ACT.Exp,
                                   bias=r_max[:, half:half + 1], accum_out=r_sum[:, half:half + 1])\
                       .then_inc(act_done, act_p.mark("router exp"))
                for j in range(4):
                    half, c0 = j // 2, 4 * (j % 2)
                    copy(f"hn_tok {j}", hn_tok[:, half, c0 * P:(c0 + 4) * P], banks[(1, 4, 5, 6)[j]][:])
                ada_copy(4, ADA_UNITS)
                ring_a[0] = 0
                act_p.enter("tile")
                with act.Fori(0, TILES1) as t:
                    loops["tile"] = t
                    expert_tile("tile", FE)
                act_p.leave(TILES1)
                del loops["tile"]
                ring_a[0] = 0
            act_p.leave(LAYERS)
            del loops["layer"]
            def row_of(half):
                return slice(half * P, (half + 1) * P)

            def high2(i):
                unit = JOBS2[i][0]
                act.wait_ge(unit_loaded[unit % HEAD_SLOTS], (UNITS_L // RING + unit // HEAD_SLOTS + 1) * 16)
                if i >= 2:
                    act.wait_ge(pe_done, pe_at(JOBS2[i - 2][2]))
                act.activation(w_high2[i % 2][:, 0:JOBS2[i][3], :], job2_weights(i), ACT.Copy)\
                   .then_inc(act_done, act_p.mark(f"high2 {i}"))

            act.wait_ge(dve_done, dve_at("tile add3"))
            act.activation(squares2, h3, ACT.Square).then_inc(act_done, act_p.mark("f squares"))
            high2(0)
            root("f norm")
            act.wait_ge(dve_done, dve_at("x"))
            act.activation(squares2, h3, ACT.Square).then_inc(act_done, act_p.mark("x squares"))
            high2(1)
            root("x norm")

            def sine(n):
                bank_a()
                if n == 2:
                    act.wait_ge(pe_done, pe_at("filter 2"))
                act.wait_ge(dve_done, dve_at(f"f_arg {n}"))
                act.activation(f_sin[0:HY_HID, :], f_arg[0:HY_HID, :], ACT.Sin)\
                   .then_inc(act_done, act_p.mark(f"f_sin {n}"))

            def gate_job(n):
                high2(GATE0 + n + 2)
                act.wait_ge(pe_done, pe_at(f"gates2 {n}"))
                act.activation(gates2[:, 2 * n:2 * n + 2, :], two(bank_a()), ACT.Sigmoid)\
                   .then_inc(act_done, act_p.mark(f"gates2 {n}"))

            for half in range(2):
                act.wait_ge(dve_done, dve_at(f"hx {half}"))
                act.activation(hx_high[:, 4 * half:4 * half + 4, :], hn3[:, 4 * half:4 * half + 4, :], ACT.Copy)\
                   .then_inc(act_done, act_p.mark(f"hx high {half}"))
            sine(1)
            high2(2)
            high2(3)
            sine(2)
            high2(4)
            high2(5)
            act.wait_ge(consts2_loaded, 64)
            act.wait_ge(pe_done, pe_at("x norm sum"))
            act.activation(squares2, hcT, ACT.Square).then_inc(act_done, act_p.mark("c squares"))
            high2(6)
            high2(7)
            gate_job(0)
            act.wait_ge(dve_done, dve_at("x norm inv"))
            root("c norm")
            gate_job(1)
            for half in range(TH):
                copy(f"u_tok {half}", u_tok[:, half, :], bank_a()[:])
            gate_job(2)
            for f in range(2):
                copy(f"u cos {f}", u_cos[:, f, :], bank_a()[:])
                copy(f"u sin {f}", u_sin[:, f, :], bank_a()[:])
            gate_job(3)
            act.wait_ge(dve_done, dve_at("hc"))
            act.activation(hc_high, hcT, ACT.Copy).then_inc(act_done, act_p.mark("hc high"))
            gate_job(4)
            act.wait_ge(dve_done, dve_at("lb shifted"))
            act.activation(lb_raw, lb_raw, ACT.Exp).then_inc(act_done, act_p.mark("lb exp"))
            gate_job(5)
            gate_job(6)
            gate_job(7)
            act.wait_ge(dve_done, dve_at("y_b"))
            for i in range(Z0, QG0):
                name = JOBS2[i][2]
                d, cols = (i - Z0) // 2, slice((i - Z0) % 2 * JOB, (i - Z0) % 2 * JOB + JOB)
                if i == QG0 - 1:
                    for which, flat in (("c", logf_c_flat), ("x", logf_flat)):
                        act.wait_ge(dve_done, dve_at(f"keys {which}"))
                        act.activation(flat, flat, ACT.Ln).then_inc(act_done, act_p.mark(f"log {which}"))
                for which, lf, ks, vs in (("c", logf_c, keys_c, vals_c), ("x", logf, keys, vals)):
                    if which == "x":
                        high2(i + 2)
                    bank = two(bank_a())
                    act.wait_ge(pe_done, pe_at(f"{name} {which}"))
                    if d < 2:
                        act.activation(lf[:, d, :, cols], bank, ACT.Sigmoid)
                        last = act.activation(ks[:, d, :, cols], bank, ACT.Sigmoid, scale=-1.0)
                    else:
                        last = act.activation(vs[:, :, cols], bank, ACT.Copy)
                    last.then_inc(act_done, act_p.mark(f"{name} {which}"))
            act.activation(y_b_high, y_b, ACT.Copy).then_inc(act_done, act_p.mark("y_b high"))
            for d in range(2):
                for half in range(TH):
                    act.wait_ge(pe_done, pe_at(f"decay {d} {half}"))
                    act.activation(keys_decayed[:, d, half, :], bank_a()[:], ACT.Exp)\
                       .then_inc(act_done, act_p.mark(f"decay {d} {half}"))

            def qg_job(n):
                high2(QG0 + n + 2)
                out = (q_hg if n < 2 else g_hg)[:, n % 2 * 2:n % 2 * 2 + 2, :]
                act.wait_ge(pe_done, pe_at(f"qg {n}"))
                act.activation(out, two(bank_a()), ACT.Copy if n < 2 else ACT.Silu)\
                   .then_inc(act_done, act_p.mark(f"qg {n}"))

            def scan_exps(d):
                if d:
                    act.wait_ge(pe_done, pe_at(f"o 0 {CHUNKS - 1}"))
                    act.wait_ge(dve_done, dve_at(f"state 0 {CHUNKS - 1}"))
                else:
                    act.wait_ge(dve_done, dve_at("decayed 1"))
                for half in range(TH):
                    for pair in range(2):
                        bank = bank_a()[:].rearrange("p (h x t) -> p h x t", h=2, x=2)
                        heads = slice(2 * pair, 2 * pair + 2)
                        act.wait_ge(pe_done, pe_at(f"cum {d} {half} {pair}"))
                        act.activation(e_cum[:, heads, row_of(half)], bank[:, :, 0, :], ACT.Exp)
                        act.activation(q_mid[:, heads, row_of(half)], bank[:, :, 1, :], ACT.Exp)
                        act.activation(k_mid[:, heads, row_of(half)], bank[:, :, 1, :], ACT.Exp, scale=-1.0)\
                           .then_inc(act_done, act_p.mark(f"cum {d} {half} {pair}"))
                    act.wait_ge(pe_done, pe_at(f"rest {d} {half}"))
                    act.activation(k_rest[:, half, :], bank_a()[:], ACT.Exp)\
                       .then_inc(act_done, act_p.mark(f"rest {d} {half}"))

            qg_job(0)
            qg_job(1)
            scan_exps(0)
            qg_job(2)
            qg_job(3)
            for n in range(4):
                high2(PB0 + n + 2)
            scan_exps(1)
            act.wait_ge(pe_done, pe_at(f"o 1 {CHUNKS - 1}"))
            for half in range(TH):
                act.activation(o_sq[:, half, :], banks[4 + half][:], ACT.Square)\
                   .then_inc(act_done, act_p.mark(f"o_sq {half}"))
            act.wait_ge(dve_done, dve_at("o sums"))
            act.activation(o_root, o_sum, ACT.Sqrt, bias=eps, scale=1.0 / P).then_inc(act_done, act_p.mark("o root"))
            act.wait_ge(dve_done, dve_at("y_a 1"))
            act.activation(y_a_high, y_a, ACT.Copy).then_inc(act_done, act_p.mark("y_a high"))
            for n in range(4):
                high2(PA0 + n + 2)
                act.wait_ge(dve_done, dve_at(f"merged2 {n}"))
                act.activation(merged2_high[:, 2 * n:2 * n + 2, :], merged2[:, 2 * n:2 * n + 2, :], ACT.Copy)\
                   .then_inc(act_done, act_p.mark(f"merged2 high {n}"))
            high2(MIX0 + 2)
            high2(MIX0 + 3)
            act.wait_ge(dve_done, dve_at("mix2 3"))
            act.activation(sq_moe, h3, ACT.Square).then_inc(act_done, act_p.mark("m squares"))
            root("m norm")
            for j in range(4):
                half, c0 = j // 2, 4 * (j % 2)
                place = hn_tok[:, half, :].rearrange("t (k c q) -> t c q k", k=DC, c=DC)[:, c0:c0 + 4]
                copy(f"hn_tok2 {j}", place, bank_a()[:].rearrange("t (c q k) -> t c q k", c=4, k=DC))
            act.wait_ge(dve_done, dve_at("group max"))
            for half in range(TH):
                act.activation(g_exp[:, half, :], logits2[:, half, 0:GROUPS], ACT.Exp,
                               bias=g_max[:, half:half + 1], accum_out=g_sum[:, half:half + 1])\
                   .then_inc(act_done, act_p.mark("group exp"))
            act.wait_ge(dve_done, dve_at("second less first"))
            act.activation(e_second, e_diff, ACT.Exp).then_inc(act_done, act_p.mark("second"))

            act.wait_ge(dve_done, dve_at("passes"))
            passes = act.value_load(n_passes[0:1, 0:1], min_val=1, max_val=S // SLOTS)
            act_p.enter("pass")
            with act.Fori(0, passes) as p:
                loops["pass"] = p
                ring_a[0] = 0
                for j in range(TILES2 // 2):
                    copy(f"spread2 {j}", spread2[:, 2 * j:2 * j + 2, :], two(bank_a()))
                ring_a[0] = 0
                act_p.enter("tile2")
                with act.Fori(0, TILES2) as t:
                    loops["tile2"] = t
                    expert_tile("tile2", FE2)
                act_p.leave(TILES2)
                del loops["tile2"]
            act_p.leave_counted()
            loops["pass"] = passes
            one_back = {"pass": 1}
            act.wait_ge(dve_done, dve_at("tile2 add3", loops, **one_back))
            act.activation(sq_moe, h3, ACT.Square).then_inc(act_done, act_p.mark("l squares"))
            act.wait_ge(pe_done, pe_at("l norm sum", loops, **one_back))
            act.activation(rms_root, banks[0][:, 0:S], ACT.Sqrt, bias=eps, scale=1.0 / D)\
               .then_inc(act_done, act_p.mark("l norm root"))

        @block.vector
        def _(dve):
            loops = {}
            ring_v = [0]

            def bank_v():
                ring_v[0] += 1
                return banks[2 + ring_v[0] % 2]

            def then(ins, step):
                ins.then_inc(dve_done, dve_p.mark(step))
                dve.wait_ge(dve_done, dve_at(step, loops))

            def two(bank, n=2):
                return bank[:].rearrange("p (c t) -> p c t", c=n)

            def normed(step, name, gain, src, out, parts=0):
                dve.wait_ge(act_done, act_at(step + " root", loops))
                then(dve.reciprocal(rms_inv, rms_root), step + " inv")
                for c in range(DC):
                    last = dve.scalar_tensor_tensor(out[:, c, :], src[:, c, :], gain[:, c:c + 1], rms_inv,
                                                    ALU.mult, ALU.mult)
                    if parts and (c + 1) % (DC // parts) == 0:
                        last.then_inc(dve_done, dve_p.mark(f"{name} {c // (DC // parts)}"))
                if not parts:
                    last.then_inc(dve_done, dve_p.mark(name))

            def expert_tile(name, f_width, add):
                dve.wait_ge(pe_done, pe_at(f"{name} hidT{f_width // 512 - 1}", loops, **{name: 1}))
                dve.wait_ge(pe_done, pe_at(f"{name} up", loops))
                for f in range(f_width // 512):
                    dve.wait_ge(act_done, act_at(f"{name} silu {f}", loops))
                    last = dve.tensor_tensor(hid[:, f * 512:(f + 1) * 512], silu_sb[:, f * 512:(f + 1) * 512],
                                             banks[6 + f][:], ALU.mult)
                last.then_inc(dve_done, dve_p.mark(f"{name} hid"))
                for j in range(4):
                    bank = bank_v()
                    dve.wait_ge(pe_done, pe_at(f"{name} back{j}", loops))
                    add(j, two(bank)).then_inc(dve_done, dve_p.mark(f"{name} add{j}"))

            dve.sem_inc(dve_done, dve_p.credit)
            dve.memset(c_silu, 0.0).then_inc(dve_done, dve_p.mark("c_pad"))
            dve.wait_ge(consts_loaded, 32)
            dve_p.enter("layer")
            with dve.Fori(0, LAYERS) as layer:
                loops["layer"] = layer
                def low(i):
                    dve.wait_ge(act_done, act_at(f"high {i}", loops))
                    w = job_weights(JOBS[i])
                    dve.tensor_tensor(job_weights(JOBS[i], ring_parts), w, high_room(i).bitcast(F32), ALU.subtract)\
                       .then_inc(dve_done, dve_p.mark(f"low {i}"))

                low(0)
                dve.wait_ge(params_loaded, layer * 16 + 16)
                normed("norm1", "hn1", par[:, Q_NORM1:Q_NORM1 + DC], h3, hn3, parts=2)

                for half in range(2):
                    dve.wait_ge(act_done, act_at(f"hn1 high {half}", loops))
                    c = slice(4 * half, 4 * half + 4)
                    last = dve.tensor_tensor(hn_low[:, c, :], hn3[:, c, :], hn_high[:, c, :].bitcast(F32), ALU.subtract)
                last.then_inc(dve_done, dve_p.mark("hn1 low"))
                low(1)
                dve.memset(k_dil, 0.0).then_inc(dve_done, dve_p.mark("k_dil zero"))
                dve.memset(k_win, 0.0).then_inc(dve_done, dve_p.mark("k_win zero"))
                dve.wait_ge(dve_done, dve_at("k_win zero", loops))

                def gate_low(n):
                    dve.wait_ge(act_done, act_at(f"gate high {n}", loops))
                    dve.tensor_tensor(gate_weights(n, ring_parts), gate_weights(n), gate_high[n % GATE_BUFS].bitcast(F32),
                                      ALU.subtract).then_inc(dve_done, dve_p.mark(f"gate low {n}"))

                flip = [0]

                def bank_s():
                    flip[0] ^= 1
                    return banks[4 + flip[0]]

                def biased(step, name, table, qh, slope, row):
                    bank = bank_s()
                    dve.wait_ge(pe_done, pe_at(step, loops))
                    for h in range(2):
                        last = dve.scalar_tensor_tensor(row(h), dist(table, qh), slope(h),
                                                        bank[:, h * S:(h + 1) * S], ALU.mult, ALU.add)
                    last.then_inc(dve_done, dve_p.mark(step, name))

                def maxima(step, name, col, rows):
                    dve.wait_ge(dve_done, dve_at(name, loops))
                    dve.tensor_reduce(neg_max[:, col:col + 2], rows, AX_X, ALU.max, negate=True)\
                       .then_inc(dve_done, dve_p.mark(step))

                def probs(step, col, row):
                    dve.wait_ge(act_done, act_at(f"e{step} 1", loops))
                    then(dve.reciprocal(row_inv[:, col:col + 2], row_sum[:, col:col + 2]), "inv" + step)
                    for h in range(2):
                        last = dve.tensor_scalar(row(h), row(h), row_inv[:, col + h:col + h + 1], None, ALU.mult)
                    last.then_inc(dve_done, dve_p.mark("p" + step))

                dil_slope = slopes(DIL_SLOTS * DIL_GROUPS)
                def dil_scores(sp, qh):
                    if sp:
                        dve.wait_ge(pe_done, pe_at(f"t dil {sp - 1} {qh} {DIL_GROUPS - 1}", loops))
                    for g in range(DIL_GROUPS):
                        biased(f"s dil {sp} {qh} {g}", f"b dil {sp} {qh} {g}", g, qh,
                               lambda h: dil_slope[g * DIL_SLOTS + 2 * sp + h],
                               lambda h: prob_dil[:, qh, h, g * S:(g + 1) * S])
                    maxima(f"m dil {sp} {qh}", f"b dil {sp} {qh} {DIL_GROUPS - 1}", 4 * sp + 2 * qh,
                           prob_dil[:, qh, :, :])

                def dil_probs(sp, qh):
                    probs(f" dil {sp} {qh}", 4 * sp + 2 * qh, lambda h: prob_dil[:, qh, h, :])

                win_slope = slopes(WIN_HEADS)

                def win_scores(w):
                    before = f"t win {w - WBUFS} 1" if w >= WBUFS else f"t dil 1 {min(w, 1)} {DIL_GROUPS - 1}"
                    dve.wait_ge(pe_done, pe_at(before, loops))
                    for qh in range(TH):
                        dve.tensor_copy(prob_win[:, w % WBUFS, qh, :, S:S + 1],
                                        par[:, Q_SINK + 2 * w:Q_SINK + 2 * w + 2].unsqueeze(2))\
                           .then_inc(dve_done, dve_p.mark(f"sink {w} {qh}"))
                        biased(f"s win {w} {qh}", f"b win {w} {qh}", WIN_TABLE, qh,
                               lambda h: win_slope[2 * w + h], lambda h: prob_win[:, w % WBUFS, qh, h, 0:S])
                        maxima(f"m win {w} {qh}", f"b win {w} {qh}", 8 + 4 * w + 2 * qh, prob_win[:, w % WBUFS, qh, :, :])

                def win_probs(w):
                    for qh in range(TH):
                        probs(f" win {w} {qh}", 8 + 4 * w + 2 * qh, lambda h: prob_win[:, w % WBUFS, qh, h, 0:S])

                out_bank = 1 + 1 + len([job for job in IN_JOBS if job[4] == "act"]) + DIL_SLOTS // 2

                def win_low(w):
                    bank = banks[(out_bank + w) % 2]
                    dve.wait_ge(act_done, act_at(f"o win {w}", loops))
                    dve.tensor_tensor(o_low[:, w, :], bank[:, 0:S], o_high[:, w, :].bitcast(F32), ALU.subtract)\
                       .then_inc(dve_done, dve_p.mark(f"o win {w}"))

                for i, (_, _, step, _, reader) in enumerate(IN_JOBS):
                    if reader == "dve":
                        bank = two(bank_v())
                        dve.wait_ge(pe_done, pe_at(step, loops))
                        if step == "k_win":
                            for kv in range(2):
                                for r in range(2):
                                    last = dve.tensor_copy(k_win[r * HD:(r + 1) * HD, 2 * kv + r:2 * kv + r + 5:4, :],
                                                           bank[kv * HD:(kv + 1) * HD, :, :])
                        else:
                            c = 2 * (i - 3)
                            for r in range(2):
                                rows = slice(r * HD, (r + 1) * HD)
                                last = dve.tensor_copy(k_dil[rows, 2 * c + r:2 * c + r + 3:2, :], bank[rows, :, :])
                        last.then_inc(dve_done, dve_p.mark(step))
                    if i + 2 < len(IN_JOBS):
                        low(i + 2)
                    else:
                        gate_low(i + 2 - len(IN_JOBS))

                pairs = WIN_HEADS // 2
                dve.wait_ge(dist_loaded, 16)
                gate_low(2)
                dil_scores(0, 0)
                gate_low(3)
                dil_scores(0, 1)
                dil_probs(0, 0)
                gate_low(4)
                dil_scores(1, 0)
                dil_probs(0, 1)
                gate_low(5)
                dil_scores(1, 1)
                dil_probs(1, 0)
                gate_low(6)
                gate_low(7)
                dil_probs(1, 1)
                win_scores(0)
                gate_low(8)
                gate_low(9)
                win_scores(1)
                gate_low(10)
                for w in range(pairs):
                    win_probs(w)
                    if w + 2 < pairs:
                        win_scores(w + 2)
                    if DC + w + GATE_BUFS < len(GATE_JOBS):
                        gate_low(DC + w + GATE_BUFS)
                    if w >= 2:
                        win_low(w - 2)
                first = len(IN_JOBS)
                low(first)
                win_low(pairs - 2)
                low(first + 1)

                dve.wait_ge(act_done, act_at("gates 0", loops))
                for j in range(4):
                    if j == 2:
                        win_low(pairs - 1)
                    bank = bank_v()
                    dve.wait_ge(pe_done, pe_at(f"ya {j}", loops))
                    dve.tensor_tensor(merged[:, 2 * j:2 * j + 2, :], two(bank), gates[:, 2 * j:2 * j + 2, :],
                                      ALU.mult).then_inc(dve_done, dve_p.mark(f"ya {j}"))
                for j in range(4):
                    bank = bank_v()
                    dve.wait_ge(act_done, act_at("gates 1", loops))
                    dve.wait_ge(pe_done, pe_at(f"yb {j}", loops))
                    then(dve.tensor_tensor(part.rearrange("p (c t) -> p c t", c=2), two(bank),
                                           gates[:, 8 + 2 * j:8 + 2 * j + 2, :], ALU.mult), f"yb {j}")
                    rows = merged[:, 2 * j:2 * j + 2, :]
                    dve.tensor_tensor(rows, rows, part.rearrange("p (c t) -> p c t", c=2), ALU.add)\
                       .then_inc(dve_done, dve_p.mark(f"merged {j}"))
                    low(first + j + 2)
                    dve.wait_ge(act_done, act_at(f"merged high {j}", loops))
                    dve.tensor_tensor(merged_low[:, 2 * j:2 * j + 2, :], rows, merged_high[:, 2 * j:2 * j + 2, :].bitcast(F32),
                                      ALU.subtract)\
                       .then_inc(dve_done, dve_p.mark(f"merged low {j}"))
                for j in range(4):
                    if j < 2:
                        low(first + 6 + j)
                    bank = bank_v()
                    dve.wait_ge(pe_done, pe_at(f"mix {j}", loops))
                    dve.tensor_tensor(h3[:, 2 * j:2 * j + 2, :], h3[:, 2 * j:2 * j + 2, :], two(bank), ALU.add)\
                       .then_inc(dve_done, dve_p.mark(f"mix {j}"))

                normed("norm2", "hn2", par[:, Q_NORM2:Q_NORM2 + DC], h3, hn3, parts=DC)
                dve.wait_ge(pe_done, pe_at("router rows", loops))
                dve.tensor_copy(aff_rows[0:EXPERTS, 0:S], banks[0][0:EXPERTS, 0:S])\
                   .then_inc(dve_done, dve_p.mark("router rows"))
                dve.wait_ge(pe_done, pe_at("router", loops))
                logits = banks[0][:, S:S + TH * EXPERTS].rearrange("p (h e) -> p h e", h=TH)
                dve.tensor_reduce(r_max, logits, AX_X, ALU.max, negate=True)\
                   .then_inc(dve_done, dve_p.mark("router max"))
                dve.wait_ge(act_done, act_at("router exp", loops))
                then(dve.reciprocal(r_inv, r_sum), "router inv")
                dve.tensor_tensor(aff, r_exp, r_inv.unsqueeze(2).broadcast_to([P, TH, EXPERTS]), ALU.mult)\
                   .then_inc(dve_done, dve_p.mark("aff"))
                dve.wait_ge(pe_done, pe_at("aff rows", loops))
                left = [aff_rows[0:EXPERTS, 0:S], aff_rows[0:EXPERTS, S:2 * S]]
                then(dve.tensor_copy(left[0], banks[2][0:EXPERTS, 0:S]), "aff rows")
                dve.sem_inc(waited, 1)
                for r in range(CAP // 8):
                    best = topv[0:EXPERTS, 8 * r:8 * r + 8]
                    then(dve.max(best, left[r % 2]), f"top {r}")
                    dve.sem_inc(waited, 1)
                    if r + 1 < CAP // 8:
                        dve.match_replace(left[1 - r % 2], best, left[r % 2], -1.0)\
                           .then_inc(dve_done, dve_p.mark(f"left {r}"))
                    dve.max_index(picks[:, 8 * r:8 * r + 8], best, left[r % 2])\
                       .then_inc(dve_done, dve_p.mark(f"index {r}"))
                    if r + 1 < CAP // 8:
                        dve.wait_ge(dve_done, dve_at(f"left {r}", loops))
                        dve.sem_inc(waited, 1)
                dve.wait_ge(dve_done, dve_at(f"index {CAP // 8 - 1}", loops))
                then(dve.tensor_copy(idxf[0:EXPERTS, :], picks[:, :]), "index")
                eye = ident[0:EXPERTS, 0:EXPERTS].unsqueeze(2).broadcast_to([EXPERTS, EXPERTS, CAP])
                for diag, rows in ((idx_diag, idxf), (gate_diag, topv)):
                    last = dve.tensor_tensor(diag[0:EXPERTS, :].rearrange("p (e s) -> p e s", e=EXPERTS), eye,
                                             rows[0:EXPERTS, :].unsqueeze(1).broadcast_to([EXPERTS, EXPERTS, CAP]),
                                             ALU.mult)
                last.then_inc(dve_done, dve_p.mark("diag"))
                dve.wait_ge(pe_done, pe_at("slot tokens", loops))
                for half in range(TH):
                    last = dve.tensor_scalar(pick[:, half, :], banks[3][:], cst[:, C_TOK + half:C_TOK + half + 1],
                                             None, ALU.is_equal)
                last.then_inc(dve_done, dve_p.mark("picked"))
                dve.wait_ge(pe_done, pe_at("slot cols", loops))
                then(dve.tensor_copy(slot_cols, banks[2][:, 0:8]), "slot cols")
                for g in range(TILES1):
                    last = dve.tensor_scalar(spread1[:, g, :], cst[:, C_IOTA:C_IOTA + S], slot_cols[:, g:g + 1],
                                             slot_cols[:, TILES1 + g:TILES1 + g + 1], ALU.is_equal, ALU.mult)
                last.then_inc(dve_done, dve_p.mark("spread"))
                ring_v[0] = 0
                dve_p.enter("tile")
                with dve.Fori(0, TILES1) as t:
                    loops["tile"] = t
                    expert_tile("tile", FE, lambda j, back: dve.tensor_tensor(
                        h3[:, 2 * j:2 * j + 2, :], h3[:, 2 * j:2 * j + 2, :], back, ALU.add))
                dve_p.leave(TILES1)
                del loops["tile"]
                ring_v[0] = 0
            dve_p.leave(LAYERS)
            del loops["layer"]
            def row_of(half):
                return slice(half * P, (half + 1) * P)

            def scaled(step, name, src, out, gain, shift, parts=False):
                dve.wait_ge(act_done, act_at(step + " root", loops))
                then(dve.reciprocal(rms_inv, rms_root), step + " inv")
                then(dve.tensor_tensor(out, src, rms_inv.unsqueeze(1).broadcast_to([P, DC, S]), ALU.mult),
                     step + " normed")
                for c in range(DC):
                    last = dve.tensor_scalar(out[:, c, :], out[:, c, :], gain[:, c:c + 1], shift(c), ALU.mult, ALU.add)
                    if parts and c % (DC // 2) == DC // 2 - 1:
                        last.then_inc(dve_done, dve_p.mark(f"{name} {c // (DC // 2)}"))
                if not parts:
                    last.then_inc(dve_done, dve_p.mark(name))

            def low2(i):
                dve.wait_ge(act_done, act_at(f"high2 {i}"))
                dve.tensor_tensor(job2_weights(i, ring_parts), job2_weights(i), w_high2[i % 2][:, 0:JOBS2[i][3], :].bitcast(F32),
                                  ALU.subtract).then_inc(dve_done, dve_p.mark(f"low2 {i}"))

            def low_of(name, out, whole, leading):
                dve.wait_ge(act_done, act_at(f"{name} high"))
                dve.tensor_tensor(out, whole, leading.bitcast(F32), ALU.subtract)\
                   .then_inc(dve_done, dve_p.mark(f"{name} low"))

            dve.wait_ge(consts2_loaded, 64)
            low2(0)
            normed("f norm", "first block", par2[:, R_FINAL1:R_FINAL1 + DC], h3, h3)
            dve.wait_ge(dve_done, dve_at("first block"))
            then(dve.tensor_tensor(h3, h3, posT, ALU.add), "x")
            for r in range(3):
                bank = bank_v()[:].rearrange("p (j b x) -> p j b x", j=4, b=4)
                dve.wait_ge(pe_done, pe_at(f"ada cols {r}"))
                cols = slice(16 * r, 16 * r + 16)
                bias = par2[:, R_ADA + 16 * r:R_ADA + 16 * r + 16].rearrange("p (j b) -> p j b", j=4)
                then(dve.tensor_tensor(ada[:, cols, :].rearrange("p (j b) r -> p j b r", j=4), bank[:, :, :, 0:2],
                                       bias.unsqueeze(3).broadcast_to([P, 4, 4, 2]), ALU.add), f"ada cols {r}")
            for gain, scale, row, norm in ((gain_x, 1, 0, R_NORM1), (gain_c, 1, 1, R_NORM1), (gain_2, 4, 0, R_NORM2)):
                last = dve.scalar_tensor_tensor(gain, ada[:, scale * DC:(scale + 1) * DC, row], 1.0,
                                                par2[:, norm:norm + DC], ALU.add, ALU.mult)
            then(last, "gains")
            low2(1)
            scaled("x norm", "hx", h3, hn3, gain_x, lambda c: ada[:, c, 0:1], parts=True)
            for half in range(2):
                c = slice(4 * half, 4 * half + 4)
                dve.wait_ge(act_done, act_at(f"hx high {half}"))
                last = dve.tensor_tensor(hn_low[:, c, :], hn3[:, c, :], hx_high[:, c, :].bitcast(F32), ALU.subtract)
            last.then_inc(dve_done, dve_p.mark("hx low"))

            def sine_arg(n, bank, bias, freq):
                a, m = f_arg[0:HY_HID, :], f_turns[0:HY_HID, :]
                dve.wait_ge(pe_done, pe_at(f"filter {n}"))
                then(dve.tensor_scalar(a, bank[0:HY_HID, 0:S], par2[0:HY_HID, bias:bias + 1], par2[0:HY_HID, freq:freq + 1],
                                       ALU.add, ALU.mult), f"arg {n}")
                then(dve.tensor_scalar(m, a, 1.0 / TURN, ROUNDER, ALU.mult, ALU.add), f"turns {n} rounded")
                then(dve.tensor_scalar(m, m, -ROUNDER, None, ALU.add), f"turns {n}")
                for i, piece_ in enumerate(TURN_PIECES):
                    then(dve.scalar_tensor_tensor(a, m, -piece_, a, ALU.mult, ALU.add), f"turn {n} {i}")
                then(dve.tensor_scalar(a, a, HALF_TURN, -HALF_TURN, ALU.min, ALU.max), f"f_arg {n}")

            sine_arg(1, banks[1], R_B1, R_FR1)

            def short_conv(j):
                bank = two(bank_v())
                dve.wait_ge(pe_done, pe_at(f"hy {j}"))

                def tap(c, w):
                    at = R_CONV + w * 12 + 2 * j + c
                    return par2[:, at:at + 1]

                for c in range(2):
                    at = R_CONVB + 2 * j + c
                    last = dve.tensor_scalar(conv[:, 2 * j + c, :], bank[:, c, :], tap(c, 1), par2[:, at:at + 1],
                                             ALU.mult, ALU.add)
                then(last, f"conv {j} 1")
                for c in range(2):
                    now = conv[:, 2 * j + c, 1:S]
                    last = dve.scalar_tensor_tensor(now, bank[:, c, 0:S - 1], tap(c, 0), now, ALU.mult, ALU.add)
                then(last, f"conv {j} 0")
                for c in range(2):
                    now = conv[:, 2 * j + c, 0:S - 1]
                    last = dve.scalar_tensor_tensor(now, bank[:, c, 1:S], tap(c, 2), now, ALU.mult, ALU.add)
                then(last, f"hy {j}")
            short_conv(0)
            low2(2)
            short_conv(1)
            low2(3)
            sine_arg(2, banks[0], R_B2, R_FR2)
            short_conv(2)
            low2(4)
            short_conv(3)
            low2(5)
            for n, taps in enumerate((taps_f, taps_b)):
                for half in range(TH):
                    bank = bank_v()
                    dve.wait_ge(pe_done, pe_at(f"taps {n} {half}"))
                    at = B_DECAY + half * HY
                    dve.tensor_tensor(taps[:, half, :], bank[:], cst2[:, at:at + HY], ALU.mult)\
                       .then_inc(dve_done, dve_p.mark(f"taps {n} {half}"))
            short_conv(4)
            low2(6)
            short_conv(5)
            low2(7)
            then(dve.tensor_tensor(conv[:, 0:4, :], conv[:, 0:4, :], conv[:, 4:8, :], ALU.mult), "hy u")
            dve.wait_ge(dve_done, dve_at("taps 1 1"))
            then(dve.memset(taps_b[0:1, 0, :], 0.0), "taps_b zero")
            then(dve.tensor_tensor(taps_sum, taps_f, taps_b, ALU.add), "taps sum")
            then(dve.tensor_tensor(taps_f, taps_f, taps_b, ALU.subtract), "taps")
            low2(8)
            for name, dst in (("k_cos", k_cos), ("k_sin", k_sin)):
                for f in range(2):
                    bank = bank_v()
                    dve.wait_ge(pe_done, pe_at(f"{name} {f}"))
                    dve.tensor_copy(dst[:, f, :], bank[:]).then_inc(dve_done, dve_p.mark(f"{name} {f}"))
            dve.wait_ge(dve_done, dve_at("k_sin 1"))
            dve.memset(k_sin[0:1, 0, :], 0.0)
            then(dve.tensor_copy(k_nyq, k_cos[:, 0, :]), "k_nyq rest")
            bank = bank_v()
            dve.wait_ge(pe_done, pe_at("k_nyq"))
            dve.tensor_copy(k_nyq[0:1, :], bank[0:1, :]).then_inc(dve_done, dve_p.mark("k_nyq"))

            low2(9)
            scaled("c norm", "hc", hcT, hcT, gain_c, lambda c: ada[:, c, 1:2])
            low2(10)
            dve.wait_ge(inputs2_loaded, 16)
            then(dve.tensor_tensor(lb_part, lb_raw[:, 0], lb_raw[:, 1], ALU.max), "lb max")
            for a in range(2):
                last = dve.tensor_tensor(lb_raw[:, a], lb_raw[:, a], lb_part, ALU.subtract)
            last.then_inc(dve_done, dve_p.mark("lb shifted"))
            low2(11)
            dve.wait_ge(act_done, act_at("u sin 1"))
            dve.tensor_tensor(prod_cos, u_cos, k_cos, ALU.mult)
            then(dve.tensor_tensor(prod_part, u_sin, k_sin, ALU.mult), "products 1")
            then(dve.tensor_tensor(prod_cos, prod_cos, prod_part, ALU.subtract), "products 2")
            dve.tensor_tensor(prod_sin, u_cos, k_sin, ALU.mult)
            dve.tensor_tensor(prod_part[:, 0, :], u_sin[:, 0, :], k_nyq, ALU.mult)
            then(dve.tensor_tensor(prod_part[:, 1, :], u_sin[:, 1, :], k_cos[:, 1, :], ALU.mult), "products 3")
            then(dve.tensor_tensor(prod_sin, prod_sin, prod_part, ALU.add), "products")
            low2(12)
            low_of("hc", hc_low, hcT, hc_high)
            low2(13)
            dve.wait_ge(act_done, act_at("lb exp"))
            then(dve.tensor_tensor(lb_part, lb_raw[:, 0], lb_raw[:, 1], ALU.add), "lb sum")
            then(dve.reciprocal(lb_part, lb_part), "lb inv")
            then(dve.tensor_tensor(lower, lower, lb_part, ALU.mult), "lower")
            then(dve.tensor_scalar(upper, lower, -1.0, 1.0, ALU.mult, ALU.add), "bounds")
            for j in range(2):
                bank = two(bank_v())
                dve.wait_ge(pe_done, pe_at(f"hy y {j}"))
                for c in range(2):
                    at = R_SKIP + 2 * j + c
                    last = dve.scalar_tensor_tensor(y_b[:, 2 * j + c, :], conv[:, 2 * j + c, :], par2[:, at:at + 1],
                                                    bank[:, c, :], ALU.mult, ALU.add)
                then(last, f"hy y {j}")
            then(dve.tensor_tensor(y_b, y_b, conv[:, 8:12, :], ALU.mult), "y_b")
            low2(14)
            low2(15)

            low2(16)
            low2(17)
            for d in range(2):
                for which, lf, ks in (("c", logf_c, keys_c), ("x", logf, keys)):
                    wide = [P, TH, KD]
                    up, low_ = (x[:, d, :].unsqueeze(1).broadcast_to(wide) for x in (upper, lower))
                    dve.wait_ge(act_done, act_at(f"z {d} 1 {which}"))
                    dve.tensor_tensor(ks[:, d], ks[:, d], up, ALU.mult)
                    then(dve.tensor_tensor(lf[:, d], lf[:, d], up, ALU.mult), f"gate {d} {which}")
                    then(dve.tensor_tensor(lf[:, d], lf[:, d], low_, ALU.add), f"keys {which}" if d else f"keys 0 {which}")
                if d == 0:
                    low2(18)
                    low2(19)
            low2(20)
            low2(21)
            low_of("y_b", y_b_low, y_b, y_b_high)
            for d in range(2):
                dve.wait_ge(act_done, act_at(f"decay {d} 1"))
                dve.tensor_tensor(keys_decayed[:, d], keys_decayed[:, d], keys_c[:, d], ALU.mult)\
                   .then_inc(dve_done, dve_p.mark(f"decayed {d}"))
            low2(22)
            for d in range(2):
                bank = bank_v()
                dve.wait_ge(pe_done, pe_at(f"state0 {d}"))
                then(dve.tensor_copy(state0[:, d, :], bank[:]), f"state0 {d}")
            low2(23)

            def scan_keys(d):
                for half in range(TH):
                    bank = bank_v()[:].rearrange("p (h t) -> p h t", h=HEADS2)
                    rows = row_of(half)
                    dve.wait_ge(act_done, act_at(f"cum {d} {half} 1"))
                    dve.tensor_tensor(q_mid[:, :, rows], q_mid[:, :, rows], q_hg[:, :, rows], ALU.mult)
                    dve.tensor_tensor(q_cum[:, :, rows], e_cum[:, :, rows], q_hg[:, :, rows], ALU.mult)
                    dve.wait_ge(pe_done, pe_at(f"keyT {d} {half}"))
                    dve.tensor_tensor(k_mid[:, :, rows], k_mid[:, :, rows], bank, ALU.mult)\
                       .then_inc(dve_done, dve_p.mark(f"keyT {d} {half}", f"qk {d} {half}"))
                dve.wait_ge(act_done, act_at(f"rest {d} 1"))
                dve.tensor_tensor(k_rest, k_rest, keys[:, d], ALU.mult)\
                   .then_inc(dve_done, dve_p.mark(f"k_rest {d}", f"state {d} 0"))

            def scan(d):
                mask = direction(d)[2].bitcast(U32)
                dve.wait_ge(pe_done, pe_at("o inner 0 1" if d else "state0 1"))
                then(dve.memset(inner_flat, 0.0), f"inner {d} zero")
                for half in range(TH):
                    bank = bank_v()[:].rearrange("p (h t) -> p h t", h=HEADS2)
                    dve.wait_ge(pe_done, pe_at(f"inner {d} {half}"))
                    dve.copy_predicated(inner[:, half], mask.unsqueeze(1).broadcast_to([P, HEADS2, P]), bank)\
                       .then_inc(dve_done, dve_p.mark(f"inner {d} {half}"))
                for n in range(CHUNKS - 1):
                    c = n if d == 0 else CHUNKS - 1 - n
                    end = c * CHUNK + (CHUNK - 1 if d == 0 else 0)
                    bank = bank_v()
                    before = state0[:, d, :] if n == 0 else states[:, n % 4, :]
                    if n >= 3:
                        dve.wait_ge(pe_done, pe_at(f"o {d} {n - 3}"))
                    elif d and n == 0:
                        dve.wait_ge(pe_done, pe_at(f"o 0 {CHUNKS - 1}"))
                    dve.wait_ge(pe_done, pe_at(f"grown {d} {n}"))
                    for h in range(HEADS2):
                        cols = slice(h * P, (h + 1) * P)
                        last = dve.scalar_tensor_tensor(states[:, (n + 1) % 4, cols], before[:, cols],
                                                        e_cum[:, h, end:end + 1], bank[:, cols], ALU.mult, ALU.add)
                    last.then_inc(dve_done, dve_p.mark(f"grown {d} {n}", f"state {d} {n + 1}"))
                    dve.wait_ge(dve_done, dve_at(f"state {d} {n + 1}"))

            scan_keys(0)
            low2(24)
            low2(25)
            for j in range(4):
                bank = two(bank_v())
                dve.wait_ge(pe_done, pe_at(f"pb {j}"))
                dve.tensor_tensor(merged2[:, 2 * j:2 * j + 2, :], bank, gates2[:, 8 + 2 * j:8 + 2 * j + 2, :], ALU.mult)\
                   .then_inc(dve_done, dve_p.mark(f"pb {j}"))
                low2(PB0 + j + 2)
            scan(0)
            scan_keys(1)
            scan(1)

            dve.wait_ge(act_done, act_at("o_sq 1"))
            dve.tensor_reduce(o_sum, o_sq.rearrange("p s (h v) -> p (s h) v", h=HEADS2), AX_X, ALU.add)\
               .then_inc(dve_done, dve_p.mark("o sums"))
            dve.wait_ge(act_done, act_at("o root"))
            then(dve.reciprocal(o_inv, o_root), "o inv")
            for half in range(TH):
                inv = o_inv[:, half * HEADS2:(half + 1) * HEADS2].unsqueeze(2).broadcast_to([P, HEADS2, P])
                dve.tensor_tensor(o_tok[:, half, :].rearrange("p (h v) -> p h v", h=HEADS2),
                                  banks[4 + half][:].rearrange("p (h v) -> p h v", h=HEADS2), inv, ALU.mult)\
                   .then_inc(dve_done, dve_p.mark(f"o_tok {half}"))
            for half in range(TH):
                bank = bank_v()[:].rearrange("p (h t) -> p h t", h=HEADS2)
                dve.wait_ge(pe_done, pe_at(f"y_a {half}"))
                dve.scalar_tensor_tensor(y_a[:, :, row_of(half)], bank, par2[:, R_HGN:R_HGN + 1],
                                         g_hg[:, :, row_of(half)], ALU.mult, ALU.mult)\
                   .then_inc(dve_done, dve_p.mark(f"y_a {half}"))

            low_of("y_a", y_a_low, y_a, y_a_high)
            for j in range(4):
                bank = two(bank_v())
                rows = merged2[:, 2 * j:2 * j + 2, :]
                dve.wait_ge(pe_done, pe_at(f"pa {j}"))
                then(dve.tensor_tensor(part2, bank, gates2[:, 2 * j:2 * j + 2, :], ALU.mult), f"pa {j}")
                dve.tensor_tensor(rows, rows, part2, ALU.add).then_inc(dve_done, dve_p.mark(f"merged2 {j}"))
                low2(PA0 + j + 2)
                dve.wait_ge(act_done, act_at(f"merged2 high {j}"))
                dve.tensor_tensor(merged2_low[:, 2 * j:2 * j + 2, :], rows, merged2_high[:, 2 * j:2 * j + 2, :].bitcast(F32),
                                  ALU.subtract).then_inc(dve_done, dve_p.mark(f"merged2 low {j}"))

            def add_gated(j, bank, gate):
                for c in range(2):
                    n = 2 * j + c
                    last = dve.scalar_tensor_tensor(h3[:, n, :], bank[:, c, :], ada[:, gate * DC + n, 0:1], h3[:, n, :],
                                                    ALU.mult, ALU.add)
                return last

            for j in range(4):
                if j < 2:
                    low2(MIX0 + j + 2)
                bank = two(bank_v())
                dve.wait_ge(pe_done, pe_at(f"mix2 {j}"))
                add_gated(j, bank, 2).then_inc(dve_done, dve_p.mark(f"mix2 {j}"))
            scaled("m norm", "h2", h3, hn3, gain_2, lambda c: ada[:, 3 * DC + c, 0:1])

            bank = bank_v()[:, 0:TH * ROUTES].rearrange("p (h r) -> p h r", h=TH)
            dve.wait_ge(pe_done, pe_at("logits2"))
            bias = par2[:, R_RBIAS:R_RBIAS + ROUTES].unsqueeze(1).broadcast_to([P, TH, ROUTES])
            dve.memset(g_padded, MASKED)
            then(dve.tensor_tensor(logits2, bank, bias, ALU.add), "logits2")
            then(dve.tensor_copy(g_padded[:, :, 0:GROUPS], logits2[:, :, 0:GROUPS]), "g_padded")
            dve.tensor_reduce(g_max, logits2[:, :, 0:GROUPS], AX_X, ALU.max, negate=True)\
               .then_inc(dve_done, dve_p.mark("group max"))
            for half in range(TH):
                last = dve.max(g_top[:, half, :], g_padded[:, half, :])
            then(last, "group top")
            for half in range(TH):
                last = dve.max_index(g_at[:, half, :], g_top[:, half, :], g_padded[:, half, :])
            then(last, "group at")
            then(dve.tensor_copy(g_index, g_at[:, :, 0]), "group index")
            count = cst[:, C_IOTA:C_IOTA + TOP8]
            for half in range(TH):
                last = dve.tensor_scalar(in_group[:, half, :], count[:, 0:GROUPS], g_index[:, half:half + 1], None,
                                         ALU.is_equal)
            then(last, "in group")
            wide = [P, GROUPS, TOP8]
            for half in range(TH):
                last = dve.tensor_tensor(e_masked[:, half], logits2[:, half, GROUPS:].rearrange("p (g e) -> p g e", g=GROUPS),
                                         in_group[:, half, :].unsqueeze(2).broadcast_to(wide), ALU.mult)
            then(last, "e masked")
            for half in range(TH):
                last = dve.tensor_reduce(e_logits[:, half, :], e_masked[:, half].rearrange("p g e -> p e g"), AX_X, ALU.add)
            then(last, "e logits")
            for half in range(TH):
                last = dve.max(e_top[:, half, :], e_logits[:, half, :])
            then(last, "e top")
            for half in range(TH):
                last = dve.max_index(e_at[:, half, :], e_top[:, half, :], e_logits[:, half, :])
            dve.tensor_tensor(e_diff, e_top[:, :, 1], e_top[:, :, 0], ALU.subtract)\
               .then_inc(dve_done, dve_p.mark("second less first"))
            dve.wait_ge(dve_done, dve_at("second less first"))
            then(dve.tensor_copy(e_index, e_at[:, :, 0:2]), "e index")
            dve.wait_ge(act_done, act_at("second"))
            then(dve.tensor_scalar(e_weight[:, :, 0], e_second, 1.0, None, ALU.add), "weights 1")
            then(dve.tensor_tensor(e_weight[:, :, 0], e_weight[:, :, 0], g_sum, ALU.mult), "weights 2")
            then(dve.reciprocal(e_weight[:, :, 0], e_weight[:, :, 0]), "weights 3")
            then(dve.tensor_tensor(e_weight[:, :, 1], e_weight[:, :, 0], e_second, ALU.mult), "weights")
            for half in range(TH):
                for n in range(2):
                    is_it = e_index[:, half, n:n + 1]
                    dve.tensor_scalar(e_hot[:, n, half, :], count, is_it, None, ALU.is_equal)
                    last = dve.tensor_scalar(e_part[:, n, half, :], count, is_it, e_weight[:, half, n:n + 1],
                                             ALU.is_equal, ALU.mult)
            then(last, "e parts")
            dve.tensor_tensor(e_hot[:, 0], e_hot[:, 0], e_hot[:, 1], ALU.add)
            then(dve.tensor_tensor(e_part[:, 0], e_part[:, 0], e_part[:, 1], ALU.add), "e both")
            for half in range(TH):
                for dst, src in ((weights, e_part), (chosen, e_hot)):
                    last = dve.tensor_tensor(dst[:, half, :].rearrange("p (g e) -> p g e", g=GROUPS),
                                             in_group[:, half, :].unsqueeze(2).broadcast_to(wide),
                                             src[:, 0, half, :].unsqueeze(1).broadcast_to(wide), ALU.mult)
            then(last, "chosen")
            bank = bank_v()
            dve.wait_ge(pe_done, pe_at("rank"))
            then(dve.scalar_tensor_tensor(rank, bank[:, 0:TH * EXPERTS2].rearrange("p (h e) -> p h e", h=TH), 1.0, chosen,
                                          ALU.add, ALU.mult), "rank 1")
            then(dve.tensor_reduce(fullest, bank[:, TH * EXPERTS2:(TH + 1) * EXPERTS2], AX_X, ALU.max), "fullest")
            dve.tensor_scalar(rank, rank, -1.0, None, ALU.add).then_inc(dve_done, dve_p.mark("rank"))
            then(dve.tensor_scalar(lots, count, float(SLOTS), fullest, ALU.mult, ALU.is_lt), "lots")
            then(dve.tensor_reduce(lots_sum, lots, AX_X, ALU.add), "lots sum")
            then(dve.tensor_copy(n_passes[:], lots_sum), "passes")

            passes = dve.value_load(n_passes[0:1, 0:1], min_val=1, max_val=S // SLOTS)
            dve_p.enter("pass")
            with dve.Fori(0, passes) as p:
                loops["pass"] = p
                dve.wait_ge(pe_done, pe_at("tile2 back3", loops, **{"pass": 1}))
                wide = [P, EXPERTS2, SLOTS]
                for half in range(TH):
                    last = dve.tensor_tensor(pick2[:, half, :].rearrange("p (e s) -> p e s", e=EXPERTS2),
                                             rank[:, half, :].unsqueeze(2).broadcast_to(wide),
                                             cst[:, C_IOTA:C_IOTA + SLOTS].unsqueeze(1).broadcast_to(wide), ALU.is_equal)
                then(last, "picked2")
                for half in range(TH):
                    last = dve.tensor_tensor(weighed[:, half, :].rearrange("p (e s) -> p e s", e=EXPERTS2),
                                             pick2[:, half, :].rearrange("p (e s) -> p e s", e=EXPERTS2),
                                             weights[:, half, :].unsqueeze(2).broadcast_to(wide), ALU.mult)
                then(last, "weighed")
                then(dve.tensor_scalar(rank, rank, -float(SLOTS), None, ALU.add), "rank next")
                dve.sem_inc(waited, 1)
                ring_v[0] = 0
                dve_p.enter("tile2")
                with dve.Fori(0, TILES2) as t:
                    loops["tile2"] = t
                    expert_tile("tile2", FE2, lambda j, back: add_gated(j, back, 5))
                dve_p.leave(TILES2)
                del loops["tile2"]
            dve_p.leave_counted()
            loops["pass"] = passes
            one_back = {"pass": 1}
            dve.wait_ge(act_done, act_at("l norm root", loops, **one_back))
            dve.reciprocal(rms_inv, rms_root).then_inc(dve_done, dve_p.mark("l norm inv"))
            dve.wait_ge(dve_done, dve_at("l norm inv", loops, **one_back))
            for c in range(DC):
                last = dve.scalar_tensor_tensor(hn3[:, c, :], h3[:, c, :], par2[:, R_FINAL2 + c:R_FINAL2 + c + 1],
                                                rms_inv, ALU.mult, ALU.mult)
            last.then_inc(dve_done, dve_p.mark("out"))

        @block.sync
        def _(sp):
            loops = {}
            sp.dma_start(h3, io["xT"].rearrange("(c p) t -> p c t", p=P)).then_inc(consts_loaded, 16)
            sp.dma_start(cst[:, 0:C_DIST], io["consts"][:, 0:C_DIST]).then_inc(consts_loaded, 16)

            def load(i, dst, src):
                sp.dma_start(dst, src).then_inc(unit_loaded[i % RING], 16)

            def load_cols(i, src, c0, cols=512):
                dst = slot(i)[:, 0:src.shape[0] // P * cols].rearrange("p (k n) -> p k n", n=cols)
                load(i, dst, src[:, bass.ds(c0, cols)].rearrange("(k p) n -> p k n", p=P))

            def load_expert_unit(i, u, gate, up, down, t, f_width):
                per_unit = 2 // (f_width // 512)
                n_in = DC // per_unit
                if u < 2 * n_in:
                    c = (u % n_in) * per_unit
                    src = gate if u < n_in else up
                    src = src[bass.ds(t * TILE_E, TILE_E), :, :]
                    if per_unit == 1:
                        src = src[:, c * P:(c + 1) * P, :].rearrange("e p f -> p e f")
                    else:
                        src = src.rearrange("e (p c) f -> p e (c f)", c=DC)[:, :, c * f_width:(c + per_unit) * f_width]
                    load(i, slot(i).rearrange("p (e x) -> p e x", e=TILE_E), src)
                else:
                    f = u - 2 * n_in
                    src = down[bass.ds(t * TILE_E, TILE_E), f * P:(f + 1) * P, :]
                    load(i, slot(i).rearrange("p (e d) -> p e d", e=TILE_E), src.rearrange("e p d -> p e d"))

            with sp.Fori(0, LAYERS) as layer:
                loops["layer"] = layer
                sp.wait_ge(dve_done, dve_at("spread", loops, layer=1))
                sp.wait_ge(pe_done, pe_at("router", loops, layer=1))
                sp.sem_inc(waited, 1)
                sp.dma_start(par[:], io["params"][layer]).then_inc(params_loaded, 16)
                w_in = io["w_in"][layer]
                q_w = 3 * DIL_QKV
                kv_w = q_w + WIN_HEADS * HD
                gate_w = kv_w + 2 * WIN_KV * HD
                starts = [0, 512, 1024, 2 * DIL_QKV, 2 * DIL_QKV + 512, q_w, q_w + 512, kv_w] + \
                    [gate_w + 512 * n for n in range(4)]
                experts = [io[n][layer] for n in ("w_expert_gate", "w_expert_up", "w_expert_down")]

                def load_first(u):
                    sp.wait_ge(pe_done, pe_at(f"unit {UNITS1_HEAD - RING + u}", loops))
                    sp.sem_inc(waited, 1)
                    load_expert_unit(u, u, *experts, 0, FE)

                for i in range(UNITS1_HEAD):
                    if i == UNITS1_HEAD - 2:
                        load_first(0)
                        load_first(1)
                    if i < RING:
                        last = UNITS1_TILE - RING + i
                        sp.wait_ge(pe_done, pe_at(f"tile unit {last}", loops, layer=1))
                    else:
                        sp.wait_ge(pe_done, pe_at(f"unit {i - RING}", loops))
                    sp.sem_inc(waited, 1)
                    if i < 12:
                        load_cols(i, w_in, starts[i], 256 if i == 4 else 512)
                    elif i < 14:
                        load_cols(i, io["w_branch_a"][layer][(i - 12) * P:(i - 11) * P, :], 0, D)
                    elif i < 16:
                        load_cols(i, io["w_branch_b"][layer], 512 * (i - 14))
                    elif i < 18:
                        load_cols(i, io["w_out"][layer], 512 * (i - 16))
                    else:
                        load_cols(i, io["ada_w_2"], layer * (512 * ADA_UNITS) + 512 * (i - 18))
                for u in range(2, RING):
                    load_first(u)

                def rest_of_tile(t):
                    for u in range(RING, UNITS1_TILE):
                        sp.wait_ge(pe_done, pe_at(f"tile unit {u - RING}", loops | {"tile": t}))
                        sp.sem_inc(waited, 1)
                        load_expert_unit(u, u, *experts, t, FE)

                with sp.Fori(0, TILES1 - 1) as t:
                    rest_of_tile(t)
                    for u in range(RING):
                        sp.wait_ge(pe_done, pe_at(f"tile unit {UNITS1_TILE - RING + u}", loops | {"tile": t}))
                        sp.sem_inc(waited, 1)
                        load_expert_unit(u, u, *experts, t + 1, FE)
                rest_of_tile(TILES1 - 1)
            del loops["layer"]
            sp.wait_ge(dve_done, dve_at("spread"))
            sp.wait_ge(pe_done, pe_at("slot cols"))
            sp.dma_start(cst2, io["consts_2"]).then_inc(consts2_loaded, 16)
            sp.dma_start(par2, io["params_2"]).then_inc(consts2_loaded, 16)
            sp.dma_start(hcT, io["ctxT"].rearrange("(c p) t -> p c t", p=P)).then_inc(consts2_loaded, 16)
            sp.dma_start(posT, io["posT"].rearrange("(c p) t -> p c t", p=P)).then_inc(consts2_loaded, 16)
            w_in = io["w_in_2"]
            hy0 = 3 * KD + 2 * KD
            starts = [hy0 + 512 * n for n in range(3)] + [hy0 + 3 * HY + 512 * n for n in range(4)] + \
                [KD, 2 * KD, 3 * KD, 0, 3 * KD + KD]
            for i in range(UNITS2_HEAD):
                if i < HEAD_SLOTS:
                    sp.wait_ge(pe_done, pe_at(f"tile unit {UNITS1_TILE - RING + i}"))
                else:
                    sp.wait_ge(pe_done, pe_at(f"unit2 {i - HEAD_SLOTS}"))
                if i < 12:
                    load_cols(i % HEAD_SLOTS, w_in, starts[i])
                else:
                    src = (io["w_proj_b_2"], io["w_proj_a_2"], io["w_out_2"])[(i - 12) // 2]
                    load_cols(i % HEAD_SLOTS, src, 512 * (i % 2))
                if i == HEAD_SLOTS - 1:
                    sp.wait_ge(pe_done, pe_at("ada cols 2"))
                    sp.dma_start(lb_raw, io["hgrn_lb_2"].partition_broadcast(P)).then_inc(inputs2_loaded, 16)
            experts = [io[n] for n in ("moe_w_gate_2", "moe_w_up_2", "moe_w_down_2")]
            for u in range(RING):
                sp.wait_ge(pe_done, pe_at(f"unit2 {UNITS2_HEAD - HEAD_SLOTS + u}" if u < HEAD_SLOTS else "mix2 3"))
                load_expert_unit(u, u, *experts, 0, FE2)

            def rest_of_tile2(t):
                for u in range(RING, UNITS2_TILE):
                    sp.wait_ge(pe_done, pe_at(f"tile2 unit {u - RING}", loops | {"tile2": t}))
                    sp.sem_inc(waited, 1)
                    load_expert_unit(u, u, *experts, t, FE2)

            def tiles2():
                with sp.Fori(0, TILES2 - 1) as t:
                    rest_of_tile2(t)
                    for u in range(RING):
                        sp.wait_ge(pe_done, pe_at(f"tile2 unit {UNITS2_TILE - RING + u}", loops | {"tile2": t}))
                        sp.sem_inc(waited, 1)
                        load_expert_unit(u, u, *experts, t + 1, FE2)
                rest_of_tile2(TILES2 - 1)

            loops["pass"] = 0
            tiles2()
            sp.wait_ge(dve_done, dve_at("passes"))
            passes = sp.value_load(n_passes[0:1, 0:1], min_val=1, max_val=S // SLOTS)
            with sp.If(passes > 1):
                with sp.Fori(1, passes) as p:
                    loops["pass"] = p
                    for u in range(RING):
                        sp.wait_ge(pe_done, pe_at(f"tile2 unit {UNITS2_TILE - RING + u}", loops, **{"pass": 1}))
                        sp.sem_inc(waited, 1)
                        load_expert_unit(u, u, *experts, 0, FE2)
                    tiles2()
            sp.wait_ge(dve_done, dve_at("out", {"pass": passes}, **{"pass": 1}))
            sp.dma_start(io["outT"].rearrange("(c p) t -> p c t", p=P), hn3).then_inc(stored, 16)
            sp.wait_ge(stored, 16)
    return {"pe": pe_p.new, "act": act_p.new, "dve": dve_p.new}


def kernel(**inputs):
    import concourse.bacc as bacc
    from concourse.bass_utils import run_bass_kernel_spmd

    a = {name: np.asarray(value) for name, value in inputs.items()}

    def columns(v):
        return np.ascontiguousarray(v.reshape(-1, P).T)

    def on_all(v):
        return np.broadcast_to(v.reshape(1, -1), (P, v.size))

    def rows(v):
        out = np.zeros((P, v.shape[1]), np.float32)
        out[:v.shape[0]] = v
        return out

    params = np.stack([np.concatenate([
        columns(a["norm_mix"][l]), columns(a["norm_ffn"][l]), columns(a["b_gate"][l]), on_all(a["sink_logit"][l]),
        a["w_router"][l].reshape(DC, P, EXPERTS).transpose(1, 0, 2).reshape(P, DC * EXPERTS),
        columns(a["c_2"]), columns(a["c_ctx_2"])], axis=1)
        for l in range(LAYERS)])
    router_2 = np.concatenate([a["moe_router_g_w_2"][0],
                               a["moe_router_e_w_2"][0].transpose(1, 0, 2).reshape(D, EXPERTS2)], axis=1)
    params_2 = np.concatenate([
        columns(a["norm_final"]), columns(a["final_norm_g_2"]), columns(a["norm1_g_2"]), columns(a["norm2_g_2"]),
        columns(a["ada_b_2"]), columns(a["hgrn_norm_g_2"]),
        columns(a["hy_conv_w_2"]), columns(a["hy_conv_b_2"]), columns(a["hy_d_2"]),
        router_2.reshape(DC, P, ROUTES).transpose(1, 0, 2).reshape(P, DC * ROUTES),
        on_all(np.concatenate([a["moe_router_g_b_2"][0], a["moe_router_e_b_2"][0].reshape(-1)])),
        rows(a["hy_filt_w1_2"][0]), rows(a["hy_filt_w2_2"][0]), rows(a["hy_filt_w3_2"][0]),
        rows(a["hy_filt_b1_2"].T), rows(a["hy_filt_freq1_2"].T), rows(a["hy_filt_b2_2"].T),
        rows(a["hy_filt_freq2_2"].T)], axis=1)
    arrays = {
        "consts": constants(), "consts_2": constants_2(), "posT": positions(),
        "xT": a["x"][0].T, "ctxT": a["ctx_2"][0].T, "params": params, "params_2": params_2,
        "hgrn_lb_2": a["hgrn_lb_2"],
    }
    for name in ("w_in", "w_branch_a", "w_branch_b", "w_out", "w_expert_gate", "w_expert_up", "w_expert_down"):
        arrays[name] = a[name]
    for name in ("ada_w_2", "w_in_2", "w_proj_a_2", "w_proj_b_2", "w_out_2"):
        arrays[name] = a[name][0]
    for name in ("moe_w_gate_2", "moe_w_up_2", "moe_w_down_2"):
        arrays[name] = a[name].reshape(EXPERTS2, *a[name].shape[3:])
    arrays = {name: np.ascontiguousarray(value) for name, value in arrays.items()}

    def program(tables):
        nc = bacc.Bacc("TRN2", target_bir_lowering=False, num_devices=1, dynamic_dma_scratch_size=1024)
        io = {name: nc.dram_tensor(name, list(value.shape), F32, kind="ExternalInput").ap()
              for name, value in arrays.items()}
        io["outT"] = nc.dram_tensor("outT", [D, S], F32, kind="ExternalOutput").ap()
        return nc, build(nc, io, tables)

    _, counts = program({})
    nc, _ = program(counts)
    result = run_bass_kernel_spmd(nc, [arrays], core_ids=[0])
    return np.ascontiguousarray(result.results[0]["outT"].T).reshape(1, S, D)
```
